# Optimizing a Trainium2 kernel written in Bass

```python
import math
import jax, jax.numpy as jnp
from jax import lax
import numpy as np

D_MODEL = 2048
BATCH = 1
SEQ = 256
DEPTH = 1
DEC_BATCH = 8
DEC_SEQ = 8
PAST_LEN = 1024
PAGE_SIZE = 128

HEAD_DIM = 64
A_HEADS = 16
A_PATTERNS = ((128, 1), (512, 4), (2048, 16))
A_WIN = max(w for w, _ in A_PATTERNS)
B_HEADS = 16
B_KV_HEADS = 2
B_GROUP = B_HEADS // B_KV_HEADS
B_WIN = 128
A_WIDTH = A_HEADS * HEAD_DIM
B_WIDTH = B_HEADS * HEAD_DIM
B_KV_WIDTH = B_KV_HEADS * HEAD_DIM
MIX_WIDTH = A_WIDTH + B_WIDTH
IN_WIDTH = 3 * A_WIDTH + B_WIDTH + 2 * B_KV_WIDTH
ATTN_SCALE = HEAD_DIM ** -0.5
N_BUCKETS = 32
MAX_EXACT = N_BUCKETS // 2
MAX_DISTANCE = A_WIN
MEM_LEN = 256
MEM_HEADS = 4
MEM_HEAD_DIM = 128
MEM_WIDTH = MEM_HEADS * MEM_HEAD_DIM
PEER_HEADS = 8
PEER_NKEYS = 128
PEER_EXPERTS = PEER_NKEYS * PEER_NKEYS
PEER_DKEY = 256
PEER_TOPK = 16
TOKEN_BLOCK = 128
BLK = 128
EPS = 1e-6

kernel_name = "hybrid_dilated_swa_peer_decoder_step"

def _rmsnorm(x, g):
    xf = x.astype(jnp.float32)
    y = xf * lax.rsqrt(jnp.mean(xf * xf, axis=-1, keepdims=True) + EPS)
    return (y * g.astype(jnp.float32)).astype(x.dtype)

def _rel_bucket(dist):
    dist = np.maximum(np.asarray(dist), 0)
    ratio = np.log(np.maximum(dist, 1) / MAX_EXACT) / math.log(MAX_DISTANCE / MAX_EXACT)
    large = np.minimum(MAX_EXACT + (ratio * (N_BUCKETS - MAX_EXACT)).astype(np.int32), N_BUCKETS - 1)
    return np.where(dist < MAX_EXACT, dist, large).astype(np.int32)

def _pos_bias(rel_bias, dist, head_lo, hk, g):
    b = rel_bias[_rel_bucket(dist)][..., head_lo:head_lo + hk * g]
    return b.reshape(*dist.shape, hk, g).astype(jnp.float32)

def _softmax_stats(s, sink):
    m = jnp.max(s, axis=-1)
    if sink is not None:
        m = jnp.maximum(m, sink)
    e = jnp.exp(s - m[..., None])
    den = jnp.sum(e, axis=-1)
    if sink is not None:
        den = den + jnp.exp(sink - m)
    return e / den[..., None], m + jnp.log(den)

def _banded_attention(q, k, v, n_back, stride, head_lo, rel_bias, sink):
    n, l, hk, g, dh = q.shape
    nb = -(-l // BLK)
    lp = nb * BLK
    kb = BLK + n_back
    qb = jnp.pad(q, ((0, 0), (0, lp - l), (0, 0), (0, 0), (0, 0))).reshape(n, nb, BLK, hk, g, dh)
    pad_kv = ((0, 0), (n_back, lp - l), (0, 0), (0, 0))
    kidx = np.arange(nb)[:, None] * BLK + np.arange(kb)[None, :]
    kblk = jnp.pad(k, pad_kv)[:, kidx]
    vblk = jnp.pad(v, pad_kv)[:, kidx]
    rel = np.arange(BLK)[:, None] - np.arange(kb)[None, :] + n_back
    qpos = np.arange(nb)[:, None, None] * BLK + np.arange(BLK)[None, :, None]
    kpos = qpos - rel[None]
    valid = (kpos >= 0) & (rel[None] >= 0) & (rel[None] <= n_back)
    bias = _pos_bias(rel_bias, rel * stride, head_lo, hk, g).transpose(2, 3, 0, 1)
    s = jnp.einsum('nbqhgd,nbkhd->nbhgqk', qb, kblk).astype(jnp.float32) * ATTN_SCALE + bias
    s = jnp.where(valid[None, :, None, None], s, -jnp.inf)
    p, lse = _softmax_stats(s, None if sink is None else sink[None, None, :, :, None])
    o = jnp.einsum('nbhgqk,nbkhd->nbqhgd', p.astype(v.dtype), vblk).reshape(n, lp, hk, g, dh)[:, :l]
    lse = lse.transpose(0, 1, 4, 2, 3).reshape(n, lp, hk, g)[:, :l]
    return o, lse

def _gathered_attention(q, kseq, vseq, n_back, stride, head_lo, rel_bias, sink):
    n, t, hk, g, dh = q.shape
    m = kseq.shape[1]
    offs = np.arange(n_back + 1)
    idx = (m - t) + np.arange(t)[:, None] - stride * offs[None, :]
    valid = idx >= 0
    idx = np.maximum(idx, 0)
    kg = kseq[:, idx]
    vg = vseq[:, idx]
    bias = _pos_bias(rel_bias, offs * stride, head_lo, hk, g).transpose(1, 2, 0)
    s = jnp.einsum('nthgd,ntjhd->nhgtj', q, kg).astype(jnp.float32) * ATTN_SCALE + bias[:, :, None, :]
    s = jnp.where(valid[None, None, None], s, -jnp.inf)
    p, lse = _softmax_stats(s, None if sink is None else sink[None, :, :, None])
    o = jnp.einsum('nhgtj,ntjhd->nthgd', p.astype(vseq.dtype), vg)
    return o, lse.transpose(0, 3, 1, 2)

def _combine_patterns(outs, lses):
    w = jax.nn.softmax(jnp.stack(lses), axis=0)
    return jnp.einsum('pnlh,pnlhd->nlhd', w.astype(outs[0].dtype), jnp.stack(outs))

def _dilated_prompt(q, k, v, rel_bias):
    b, s, h, dh = q.shape
    outs, lses = [], []
    for w, d in A_PATTERNS:
        def to_stream(x):
            return x.reshape(b, s // d, d, h, dh).swapaxes(1, 2).reshape(b * d, s // d, h, dh)
        o, lse = _banded_attention(to_stream(q)[:, :, :, None], to_stream(k), to_stream(v),
                                   w // d, d, 0, rel_bias, None)
        outs.append(o.reshape(b, d, s // d, h, dh).swapaxes(1, 2).reshape(b, s, h, dh))
        lses.append(lse.reshape(b, d, s // d, h).swapaxes(1, 2).reshape(b, s, h))
    return _combine_patterns(outs, lses)

def _dilated_sample(q, kseq, vseq, rel_bias):
    outs, lses = [], []
    for w, d in A_PATTERNS:
        o, lse = _gathered_attention(q[:, :, :, None], kseq, vseq, w // d, d, 0, rel_bias, None)
        outs.append(o[:, :, :, 0])
        lses.append(lse[..., 0])
    return _combine_patterns(outs, lses)

def _project(h, w_in):
    lead = h.shape[:-1]
    cuts = [A_WIDTH, 2 * A_WIDTH, 3 * A_WIDTH, 3 * A_WIDTH + B_WIDTH, 3 * A_WIDTH + B_WIDTH + B_KV_WIDTH]
    qa, ka, va, qb, kb, vb = jnp.split(h @ w_in, cuts, axis=-1)
    a = [t.reshape(*lead, A_HEADS, HEAD_DIM) for t in (qa, ka, va)]
    qb = qb.reshape(*lead, B_KV_HEADS, B_GROUP, HEAD_DIM)
    kb = kb.reshape(*lead, B_KV_HEADS, HEAD_DIM)
    vb = vb.reshape(*lead, B_KV_HEADS, HEAD_DIM)
    return a[0], a[1], a[2], qb, kb, vb

def _merge(oa, ob, ln_a, ln_b, w_out):
    lead = oa.shape[:-2]
    oa = _rmsnorm(oa.reshape(*lead, A_WIDTH), ln_a)
    ob = _rmsnorm(ob.reshape(*lead, B_WIDTH), ln_b)
    return jnp.concatenate([oa, ob], axis=-1) @ w_out

def _mem_kv(mem, ln_mem, w_ckv):
    b, m, _ = mem.shape
    kv = _rmsnorm(mem, ln_mem) @ w_ckv
    k, v = jnp.split(kv, 2, axis=-1)
    return k.reshape(b, m, MEM_HEADS, MEM_HEAD_DIM), v.reshape(b, m, MEM_HEADS, MEM_HEAD_DIM)

def _cross_attn(h, mk, mv, w_cq, w_co):
    b, s, _ = h.shape
    q = (h @ w_cq).reshape(b, s, MEM_HEADS, MEM_HEAD_DIM)
    sc = jnp.einsum('bshd,bmhd->bhsm', q, mk).astype(jnp.float32) * (MEM_HEAD_DIM ** -0.5)
    p = jax.nn.softmax(sc, axis=-1).astype(mv.dtype)
    o = jnp.einsum('bhsm,bmhd->bshd', p, mv).reshape(b, s, MEM_WIDTH)
    return o @ w_co

def _peer(h, w_pq, sub_k1, sub_k2, expert_u, expert_v):
    shape = h.shape
    flat = h.reshape(-1, D_MODEL)
    n = flat.shape[0]
    npad = -(-n // TOKEN_BLOCK) * TOKEN_BLOCK
    blocks = jnp.pad(flat, ((0, npad - n), (0, 0))).reshape(-1, TOKEN_BLOCK, D_MODEL)
    half = PEER_DKEY // 2

    def one_block(xb):
        q = (xb @ w_pq).reshape(TOKEN_BLOCK, PEER_HEADS, PEER_DKEY)
        s1 = jnp.einsum('thd,kd->thk', q[..., :half], sub_k1)
        s2 = jnp.einsum('thd,kd->thk', q[..., half:], sub_k2)
        v1, i1 = lax.top_k(s1, PEER_TOPK)
        v2, i2 = lax.top_k(s2, PEER_TOPK)
        cand = (v1[..., :, None] + v2[..., None, :]).reshape(TOKEN_BLOCK, PEER_HEADS, PEER_TOPK * PEER_TOPK)
        cidx = (i1[..., :, None] * PEER_NKEYS + i2[..., None, :]).reshape(TOKEN_BLOCK, PEER_HEADS, PEER_TOPK * PEER_TOPK)
        best, pos = lax.top_k(cand, PEER_TOPK)
        eidx = jnp.take_along_axis(cidx, pos, axis=-1)
        gate = jax.nn.softmax(best.astype(jnp.float32), axis=-1)
        u = expert_u[eidx]
        act = jax.nn.gelu(jnp.einsum('td,thkd->thk', xb, u).astype(jnp.float32), approximate=False)
        vv = expert_v[eidx]
        return jnp.einsum('thk,thkd->td', (gate * act).astype(xb.dtype), vv)

    out = lax.map(one_block, blocks).reshape(npad, D_MODEL)[:n]
    return out.reshape(shape)

def setup_inputs(seed: int = 0) -> dict:
    key = jax.random.key(seed)
    ks = jax.random.split(key, 32)
    f32 = jnp.float32

    def nrm(k, shape, scale):
        return scale * jax.random.normal(k, shape, f32)

    def gain(k, shape):
        return 1.0 + 0.02 * jax.random.normal(k, shape, f32)

    la = min(A_WIN, PAST_LEN)
    lb = min(B_WIN, PAST_LEN)
    return {
        "x_prompt": nrm(ks[0], (BATCH, SEQ, D_MODEL), 1.0),
        "x_sample": nrm(ks[1], (DEC_BATCH, DEC_SEQ, D_MODEL), 1.0),
        "cache_a_k": nrm(ks[2], (DEPTH, DEC_BATCH, la, A_HEADS, HEAD_DIM), 1.0),
        "cache_a_v": nrm(ks[3], (DEPTH, DEC_BATCH, la, A_HEADS, HEAD_DIM), 1.0),
        "cache_b_k": nrm(ks[4], (DEPTH, DEC_BATCH, lb, B_KV_HEADS, HEAD_DIM), 1.0),
        "cache_b_v": nrm(ks[5], (DEPTH, DEC_BATCH, lb, B_KV_HEADS, HEAD_DIM), 1.0),
        "cache_mem_k": nrm(ks[6], (DEPTH, DEC_BATCH, MEM_LEN, MEM_HEADS, MEM_HEAD_DIM), 1.0),
        "cache_mem_v": nrm(ks[7], (DEPTH, DEC_BATCH, MEM_LEN, MEM_HEADS, MEM_HEAD_DIM), 1.0),
        "mem_prompt": nrm(ks[8], (BATCH, MEM_LEN, D_MODEL), 1.0),
        "ln_mix": gain(ks[9], (DEPTH, D_MODEL)),
        "w_in": nrm(ks[10], (DEPTH, D_MODEL, IN_WIDTH), D_MODEL ** -0.5),
        "ln_a_out": gain(ks[11], (DEPTH, A_WIDTH)),
        "ln_b_out": gain(ks[12], (DEPTH, B_WIDTH)),
        "w_out": nrm(ks[13], (DEPTH, MIX_WIDTH, D_MODEL), MIX_WIDTH ** -0.5),
        "b_sinks": nrm(ks[14], (DEPTH, B_HEADS), 1.0),
        "rel_bias": nrm(ks[15], (N_BUCKETS, A_HEADS + B_HEADS), 0.5),
        "ln_cross": gain(ks[16], (DEPTH, D_MODEL)),
        "ln_mem": gain(ks[17], (DEPTH, D_MODEL)),
        "w_cq": nrm(ks[18], (DEPTH, D_MODEL, MEM_WIDTH), D_MODEL ** -0.5),
        "w_ckv": nrm(ks[19], (DEPTH, D_MODEL, 2 * MEM_WIDTH), D_MODEL ** -0.5),
        "w_co": nrm(ks[20], (DEPTH, MEM_WIDTH, D_MODEL), MEM_WIDTH ** -0.5),
        "ln_ffn": gain(ks[21], (DEPTH, D_MODEL)),
        "w_pq": nrm(ks[22], (DEPTH, D_MODEL, PEER_HEADS * PEER_DKEY), D_MODEL ** -0.5),
        "sub_keys_1": nrm(ks[23], (DEPTH, PEER_NKEYS, PEER_DKEY // 2), (PEER_DKEY // 2) ** -0.5),
        "sub_keys_2": nrm(ks[24], (DEPTH, PEER_NKEYS, PEER_DKEY // 2), (PEER_DKEY // 2) ** -0.5),
        "expert_u": nrm(ks[25], (DEPTH, PEER_EXPERTS, D_MODEL), D_MODEL ** -0.5),
        "expert_v": nrm(ks[26], (DEPTH, PEER_EXPERTS, D_MODEL), PEER_TOPK ** -0.5),
        "ln_final": gain(ks[27], (D_MODEL,)),
    }

def reference(x_prompt, x_sample, cache_a_k, cache_a_v, cache_b_k, cache_b_v, cache_mem_k, cache_mem_v,
              mem_prompt, ln_mix, w_in, ln_a_out, ln_b_out, w_out, b_sinks, rel_bias, ln_cross, ln_mem,
              w_cq, w_ckv, w_co, ln_ffn, w_pq, sub_keys_1, sub_keys_2, expert_u, expert_v, ln_final):
    yp = x_prompt
    ys = x_sample
    akp, avp, bkp, bvp, mkp, mvp = [], [], [], [], [], []
    aks, avs, bks, bvs = [], [], [], []
    for l in range(DEPTH):
        sinks = b_sinks[l].astype(jnp.float32).reshape(B_KV_HEADS, B_GROUP)
        h = _rmsnorm(yp, ln_mix[l])
        qa, ka, va, qb, kb, vb = _project(h, w_in[l])
        oa = _dilated_prompt(qa, ka, va, rel_bias)
        ob, _ = _banded_attention(qb, kb, vb, B_WIN, 1, A_HEADS, rel_bias, sinks)
        yp = yp + _merge(oa, ob, ln_a_out[l], ln_b_out[l], w_out[l])
        mk, mv = _mem_kv(mem_prompt, ln_mem[l], w_ckv[l])
        yp = yp + _cross_attn(_rmsnorm(yp, ln_cross[l]), mk, mv, w_cq[l], w_co[l])
        yp = yp + _peer(_rmsnorm(yp, ln_ffn[l]), w_pq[l], sub_keys_1[l], sub_keys_2[l], expert_u[l], expert_v[l])
        s_len = ka.shape[1]
        akp.append(ka[:, s_len - min(A_WIN, s_len):])
        avp.append(va[:, s_len - min(A_WIN, s_len):])
        bkp.append(kb[:, s_len - min(B_WIN, s_len):])
        bvp.append(vb[:, s_len - min(B_WIN, s_len):])
        mkp.append(mk)
        mvp.append(mv)
        h = _rmsnorm(ys, ln_mix[l])
        qa, ka, va, qb, kb, vb = _project(h, w_in[l])
        ka_seq = jnp.concatenate([cache_a_k[l], ka], axis=1)
        va_seq = jnp.concatenate([cache_a_v[l], va], axis=1)
        kb_seq = jnp.concatenate([cache_b_k[l], kb], axis=1)
        vb_seq = jnp.concatenate([cache_b_v[l], vb], axis=1)
        oa = _dilated_sample(qa, ka_seq, va_seq, rel_bias)
        ob, _ = _gathered_attention(qb, kb_seq, vb_seq, B_WIN, 1, A_HEADS, rel_bias, sinks)
        ys = ys + _merge(oa, ob, ln_a_out[l], ln_b_out[l], w_out[l])
        ys = ys + _cross_attn(_rmsnorm(ys, ln_cross[l]), cache_mem_k[l], cache_mem_v[l], w_cq[l], w_co[l])
        ys = ys + _peer(_rmsnorm(ys, ln_ffn[l]), w_pq[l], sub_keys_1[l], sub_keys_2[l], expert_u[l], expert_v[l])
        ma = ka_seq.shape[1]
        mb = kb_seq.shape[1]
        aks.append(ka_seq[:, ma - min(A_WIN, ma):])
        avs.append(va_seq[:, ma - min(A_WIN, ma):])
        bks.append(kb_seq[:, mb - min(B_WIN, mb):])
        bvs.append(vb_seq[:, mb - min(B_WIN, mb):])
    y_prompt = _rmsnorm(yp, ln_final)
    y_sample = _rmsnorm(ys, ln_final)
    return (y_prompt, y_sample,
            jnp.stack(akp), jnp.stack(avp), jnp.stack(bkp), jnp.stack(bvp), jnp.stack(mkp), jnp.stack(mvp),
            jnp.stack(aks), jnp.stack(avs), jnp.stack(bks), jnp.stack(bvs))


_drawn_inputs = setup_inputs


def setup_inputs(seed=0):
    import zlib

    import numpy as np

    out = dict(_drawn_inputs(seed))
    spreads = {}
    factors = {'ln_a_out': 3.939,
     'ln_b_out': 4.067,
     'ln_cross': 8.0,
     'ln_mem': 2.816,
     'ln_ffn': 15.131,
     'ln_final': 7.944}
    for name, (base, spread) in spreads.items():
        noise = np.random.default_rng([zlib.crc32(name.encode()), seed]).standard_normal(out[name].shape)
        drawn = base * np.exp(spread * noise) if base else spread * noise
        out[name] = __import__('jax').numpy.asarray(drawn.astype(out[name].dtype))
    for name, factor in factors.items():
        out[name] = (out[name] * factor).astype(out[name].dtype)
    return out
```

```python
import math
from contextlib import ExitStack

import numpy as np
import concourse.bass as bass
from concourse import mybir

F32 = mybir.dt.float32
U32 = mybir.dt.uint32
ALU = mybir.AluOpType
ACT = mybir.ActivationFunctionType
AX_X = mybir.AxisListType.X

P = 128
D = 2048
KT = D // P
NP_TOK, NS_TOK = 256, 64
NT = NP_TOK + NS_TOK
REQ, QPR = 8, 8
HEADS, DH = 16, 64
SCALE = DH ** -0.5
PAST = 1024
MEM, MEM_HEADS, MEM_DH = 256, 4, 128
MEM_SCALE = MEM_DH ** -0.5
EPS = 1e-6
NEG = -1e30
T_QA, T_KA, T_QB, T_KB, T_VA, T_VB, T_IN = 0, 8, 16, 24, 25, 33, 34
VW = 9 * P
USED = 768
FIRST = 256
NEWK = NS_TOK
SW = NEWK + USED
WIN = 15 * QPR
C_MEM, C_IN, C_OUT, C_CQ, C_CO, C_PQ, C_END = 0, 8, 42, 58, 62, 66, 82
WR_N = 4
PH, PK, NKEY = 8, 16, 128
SLOTS = PH * PK
W_IN, W_OUT, W_CQ, W_CO, W_PQ, W_END = 8, 42, 58, 62, 78, 94
RING = 4


def build(nc, d):
    with ExitStack() as ctx:
        def sem(name):
            return ctx.enter_context(nc.semaphore(name))

        def region(name, words):
            return ctx.enter_context(nc.sbuf_tensor(name, [P, words], F32))

        CST = region("CST", 776)
        XT = region("XT", KT * NT)
        WR = region("WR", WR_N * D)
        HT = region("HT", KT * NT)
        QK = region("QK", T_IN * NT)
        VO = region("VO", 3 * VW + KT * NT)
        KV = region("KV", 8 * SW + 6 * 1024)
        VB = region("VB", REQ * P)

        cst_at = [0]

        def const(n):
            cst_at[0] += n
            return CST[:, cst_at[0] - n:cst_at[0]]

        ident, ones = const(P), const(P)
        gains = const(5 * KT)
        G_MIX, G_MEM, G_CROSS, G_FFN, G_AB = (gains[:, i * KT:(i + 1) * KT] for i in range(5))
        sink_prompt, sink_sample = const(HEADS), const(1)
        iota16 = const(PK)
        pair_sel = const(64)
        sub_keys = const(2 * NKEY)
        n_host_const = cst_at[0]
        eps = const(1)
        stat = const(80)

        mem_x = QK[:, 0:KT * MEM]
        mem_kT = KV[:, 8 * SW:8 * SW + 1024]
        mem_v = KV[:, 8 * SW + 1024:8 * SW + 2048]
        VT = VO[:, 0:3 * VW].rearrange("p (t w) -> p t w", t=3)
        OT = VO[:, 3 * VW:3 * VW + KT * NT]
        sq = VO[:, 0:8 * NT]
        rs = VO[:, 8 * NT:9 * NT]
        rms = VO[:, 9 * NT:10 * NT]

        bias_p = WR[:, 0:32 * 256].rearrange("p (h c) -> p h c", h=32)
        tab = OT
        n_tab = 128 + 380 + 4 * 128 + 2 * (USED + WIN + P + WIN)
        rb_p, oh_p = tab[:, 0:128], tab[:, 128:508]
        rb_s = tab[:, 508:1020].rearrange("p (g t c) -> p g t c", g=2, t=2)
        oh_sa = tab[:, 1020:1020 + 2 * (USED + WIN)].rearrange("p (t u) -> p t u", t=2)
        oh_sb = tab[:, 1020 + 2 * (USED + WIN):n_tab].rearrange("p (t u) -> p t u", t=2)
        VTF = QK[:, T_VA * NT:T_IN * NT]
        probs_p = VTF[:, 0:768].rearrange("p (b c) -> p b c", b=2)
        probsT_p = VTF[:, 768:1536].rearrange("p (b c) -> p b c", b=2)
        bias_sa, bias_sb = HT[:, 0:USED + WIN], HT[:, 888:888 + P + WIN]
        head_mask = HT[:, 1136:1648]
        qpad_a = [HT[:, 1648 + i * 1088:2736 + i * 1088] for i in range(2)]
        qpad_b = [HT[:, 3824 + i * 128:3952 + i * 128] for i in range(2)]
        kbT = HT[:, 4080:5104].rearrange("p (n u) -> p n u", n=REQ)
        vb = VB[:, :].rearrange("p (n w) -> p n w", n=REQ)
        kr = [KV[:, j * SW:(j + 1) * SW] for j in range(8)]
        vr = [KV[:, 8 * SW + k * 1024:8 * SW + (k + 1) * 1024] for k in range(6)]
        s_a = VTF[:, 0:SW]
        pT_a = VTF[:, SW:SW + 896]
        s_b = VTF[:, 1728:1728 + 192]
        pT_b = VTF[:, 1920:1920 + 256]
        o_masked = VTF[:, 2176:2688]
        o_pair = VTF[:, 2688:2816]
        km = [KV[:, 0:4096], QK[:, 0:4096]]
        vm = [KV[:, 4096:8192], QK[:, 4096:8192]]
        km_p = KV[:, 8192:9216]
        vm_p = KV[:, 9216:10240]
        qc = QK[:, 8192:8192 + 4 * NT].rearrange("p (h t) -> p h t", h=4)
        oc = QK[:, 9472:9472 + 4 * NT].rearrange("p (h t) -> p h t", h=4)
        probs_c = VO[:, 0:512].rearrange("p (b c) -> p b c", b=2)
        probsT_c = VO[:, 512:1024].rearrange("p (b c) -> p b c", b=2)
        qpad_c = VO[:, 1024:1024 + 2176]
        qp = QK[:, 0:KT * 384].rearrange("p (f t) -> p f t", f=KT)
        sc = QK[:, 6144:8192]
        tk = QK[:, 8192:10880]
        top_v = tk[:, 0:256].rearrange("p (h z k) -> p h z k", h=PH, z=2)
        top_i = tk[:, 256:512].bitcast(U32).rearrange("p (h z k) -> p h z k", h=PH, z=2)
        top_f = tk[:, 512:768].rearrange("p (h z k) -> p h z k", h=PH, z=2)
        best = tk[:, 768:896].rearrange("p (h k) -> p h k", h=PH)
        pos = tk[:, 896:1024].bitcast(U32).rearrange("p (h k) -> p h k", h=PH)
        pos_i = tk[:, 1024:1280].bitcast(U32)
        pos_f = tk[:, 1280:1536]
        exp_f = tk[:, 1536:1792]
        eidx_f = tk[:, 1792:1920]
        gexp = [g.rearrange("p (h k) -> p h k", h=PH) for g in (tk[:, 1920:2048], VB[:, 768:896], VB[:, 896:1024])]
        eidx = tk[:, 2048:2432].bitcast(U32).rearrange("p (t s) -> p t s", t=3)
        gate = VB[:, 0:384].rearrange("p (t s) -> p t s", t=3)
        dots = VB[:, 384:768].rearrange("p (t s) -> p t s", t=3)
        pair_gate, pair_idx = tk[:, 2432:2496], tk[:, 2496:2560].bitcast(U32)
        h_tok = [VO[:, t * D:(t + 1) * D] for t in range(3)]
        g_row = VO[:, 3 * D:4 * D]
        u_ring = [KV[:, r * D:(r + 1) * D] for r in range(RING)]
        v_ring = [WR[:, r * D:(r + 1) * D] for r in range(RING)]
        diag = [HT[:, r * P:(r + 1) * P] for r in range(RING)]

        bank = [ctx.enter_context(nc.psum_tensor(f"bank{i}", [P, 512], F32))[:, :] for i in range(4)]
        big = ctx.enter_context(nc.psum_tensor("big", [P, 2048], F32))[:, :]
        bank += [big[:, i * 512:(i + 1) * 512] for i in range(4)]

        s_const, s_memx, s_x, s_tab = sem("consts_in"), sem("mem_in"), sem("x_in"), sem("tables_in")
        s_mask, s_kb, s_vb = sem("mask_in"), sem("kb_in"), sem("vb_in")
        s_w = [sem(f"chunk_in{i}") for i in range(WR_N)]
        s_used = sem("chunk_used")
        s_eps = sem("eps_set")
        s_sq, s_ss, s_rms, s_rs, s_h = sem("squares"), sem("square_sums"), sem("rms"), sem("inv_rms"), sem("normed")
        s_ev = sem("evacuated")
        s_memout, s_memev = sem("mem_out"), sem("mem_kept")
        s_bias, s_biasev = sem("bias_ready"), sem("bias_kept")
        s_vt, s_vtev = sem("values_turned"), sem("values_kept")
        s_S, s_max, s_exp, s_nrm = sem("p_scores"), sem("p_max"), sem("p_exp"), sem("p_normed")
        s_T, s_Tev, s_O, s_Oev = sem("p_turned"), sem("p_turned_kept"), sem("p_out"), sem("p_out_kept")
        s_kr = [sem(f"keys_in{j}") for j in range(8)]
        s_vr = [sem(f"values_in{j}") for j in range(6)]
        s_krused, s_vrused = sem("keys_used"), sem("values_used")
        s_newk = sem("new_keys")
        s_zero, s_qpad = sem("pads_zero"), sem("pads_filled")
        s_sS, s_smax, s_sexp, s_srd = sem("s_scores"), sem("s_max"), sem("s_exp"), sem("s_recip")
        s_sT, s_sTev, s_sO, s_sOev = sem("s_turned"), sem("s_turned_kept"), sem("s_out"), sem("s_pair")
        s_sP, s_sPev = sem("s_pair_turned"), sem("s_kept")
        s_km = [sem("mem_cache_in0"), sem("mem_cache_in1")]
        s_cS, s_cmax, s_cexp, s_cnrm = sem("c_scores"), sem("c_max"), sem("c_exp"), sem("c_normed")
        s_cT, s_cTev, s_cO, s_cOev = sem("c_turned"), sem("c_turned_kept"), sem("c_out"), sem("c_kept")
        s_cpad = sem("c_pads")
        s_xt, s_xsq, s_xrms, s_ht = sem("x_turned"), sem("x_sq"), sem("x_rms"), sem("h_tok")
        s_grow, s_dup = sem("gain_row_in"), sem("h_dup")
        s_sc, s_scev = sem("k_scores"), sem("k_scores_kept")
        s_dv, s_gx, s_gxe, s_idx = sem("dve_chain"), sem("gate_diff"), sem("gate_exp"), sem("experts_chosen")
        s_ug = [sem(f"u_in{r}") for r in range(RING)]
        s_vg = [sem(f"v_in{r}") for r in range(RING)]
        s_udot, s_gelu, s_coef, s_dg, s_vmm = sem("u_dots"), sem("gelu"), sem("coefs"), sem("diags"), sem("v_added")
        s_res = sem("residual_in_acc")
        s_fsq, s_frms, s_y = sem("y_sq"), sem("y_rms"), sem("y_ready")
        s_ac = sem("act_chain")
        s_attout = sem("attention_outputs")
        s_copy, s_out = sem("cache_copied"), sem("outputs")
        def chunk_wait(eng, c):
            eng.wait_ge(s_w[c % WR_N], 16 * (c // WR_N + 1))

        block = ctx.enter_context(nc.Block())

        N_NORM = {"mem": 0, "mix": 1, "group": 2, "cross": 3, "ffn": 4}

        @block.sync
        def _(sp):
            sp.dma_start(mem_x, d["memT"]).then_inc(s_memx, 16)
            sp.dma_start(CST[:, 0:n_host_const], d["consts"]).then_inc(s_const, 16)
            for c in range(WR_N):
                sp.dma_start(WR[:, c * D:(c + 1) * D], d["wall"][c]).then_inc(s_w[c], 16)
            sp.dma_start(XT[:, :], d["xT"]).then_inc(s_x, 16)
            sp.dma_start(tab[:, 0:n_tab], d["tables"]).then_inc(s_tab, 16)
            for c in range(WR_N, C_IN):
                sp.wait_ge(s_used, c - WR_N + 1)
                sp.dma_start(WR[:, (c % WR_N) * D:(c % WR_N + 1) * D], d["wall"][c]).then_inc(s_w[c % WR_N], 16)
            with sp.Fori(0, 8) as i:
                for r in range(WR_N):
                    sp.wait_ge(s_used, i * WR_N + (C_IN + r - WR_N + 1))
                    sp.dma_start(WR[:, r * D:(r + 1) * D], d["wall"][bass.ds(i * WR_N + (C_IN + r), 1)].rearrange("o p w -> (o p) w")).then_inc(s_w[r], 16)
                    for name in ("ka", "va"):
                        src = d[name + "_flat"][bass.ds(i * WR_N + r, 1)].rearrange("o p w -> (o p) w")
                        dst = d[name + "_out"][bass.ds(i * WR_N + r, 1)].rearrange("o p w -> (o p) w")
                        sp.dma_start(dst, src).then_inc(s_copy, 16)
            for c in (C_OUT - 2, C_OUT - 1):
                sp.wait_ge(s_used, c - WR_N + 1)
                sp.dma_start(WR[:, (c % WR_N) * D:(c % WR_N + 1) * D], d["wall"][c]).then_inc(s_w[c % WR_N], 16)
            sp.wait_ge(s_ev, T_IN)
            sp.dma_start(d["kaT_new"], QK[:, T_KA * NT:T_QB * NT]).then_inc(s_attout, 16)
            sp.dma_start(d["kbT_new"], QK[:, T_KB * NT:T_VA * NT]).then_inc(s_attout, 16)
            sp.wait_ge(s_vtev, 9)
            sp.dma_start(d["v_new"], VO[:, 0:2 * VW]).then_inc(s_attout, 16)
            sp.dma_start(d["v_new_s"], VO[0:NS_TOK, 2 * VW:3 * VW]).then_inc(s_attout, 16)
            sp.wait_ge(s_kb, 16)
            sp.dma_start(d["kb_out"], HT[:, 4080:5104]).then_inc(s_attout, 16)
            sp.wait_ge(s_vb, 16)
            sp.dma_start(d["vb_out"], VB[:, :]).then_inc(s_attout, 16)
            sp.wait_ge(s_max, 2 * HEADS)
            with sp.Fori(0, (C_PQ - C_OUT) // WR_N) as i:
                for r in range(WR_N):
                    slot = (C_OUT + r) % WR_N
                    sp.wait_ge(s_used, i * WR_N + (C_OUT + r - WR_N + 1))
                    sp.dma_start(WR[:, slot * D:(slot + 1) * D], d["wall"][bass.ds(i * WR_N + (C_OUT + r), 1)].rearrange("o p w -> (o p) w")).then_inc(s_w[slot], 16)
            for c in range(C_PQ, C_PQ + WR_N):
                sp.wait_ge(s_used, W_CO + 4 * (c - C_PQ + 1))
                sp.dma_start(WR[:, (c % WR_N) * D:(c % WR_N + 1) * D], d["wall"][c]).then_inc(s_w[c % WR_N], 16)
            with sp.Fori(0, (C_END - C_PQ) // WR_N - 1) as i:
                for r in range(WR_N):
                    slot = (C_PQ + r) % WR_N
                    sp.wait_ge(s_used, i * WR_N + (W_PQ + r + 1))
                    sp.dma_start(WR[:, slot * D:(slot + 1) * D], d["wall"][bass.ds(i * WR_N + (C_PQ + WR_N + r), 1)].rearrange("o p w -> (o p) w")).then_inc(s_w[slot], 16)
            sp.wait_ge(s_cOev, 10)
            sp.wait_ge(s_h, 16 * 5)
            sp.dma_start(g_row, d["ffn_row"].partition_broadcast(P)).then_inc(s_grow, 16)
            sp.wait_ge(s_ht, 3)
            sp.dma_start(h_tok[2][64:128, :], h_tok[2][0:64, :]).then_inc(s_dup, 16)
            sp.dma_start(g_row, d["fin_row"].partition_broadcast(P)).then_inc(s_grow, 16)
            for t in range(3):
                sp.wait_ge(s_y, t + 1)
                n = P if t < 2 else NS_TOK
                sp.dma_start(d["y"][t * P:t * P + n, :], h_tok[t][0:n, :]).then_inc(s_out, 16)
            sp.wait_ge(s_copy, 2 * 32 * 16)
            sp.wait_ge(s_attout, 6 * 16)
            sp.wait_ge(s_memout, 2 * 16)
            sp.wait_ge(s_out, 3 * 16)

        @block.gpsimd
        def _(pool):
            nc.gpsimd.memset(eps, EPS).then_inc(s_eps, 1)
            pool.dma_start(VB[:, :], d["vb"]).then_inc(s_vb, 16)
            pool.wait_ge(s_memout, 32)
            for k in range(6):
                pool.dma_start(vr[k], d["va"][0, FIRST + k * P:FIRST + (k + 1) * P, :]).then_inc(s_vr[k], 16)
            for j in range(8):
                pool.dma_start(kr[j][:, NEWK:SW], d["kaT"][0, j, :, FIRST:PAST]).then_inc(s_kr[j], 16)
            pool.wait_ge(s_used, W_OUT)
            pool.dma_start(kbT, d["kbT"].rearrange("p (n u) -> p n u", n=REQ)).then_inc(s_kb, 16)
            pool.dma_start(head_mask, d["head_mask"]).then_inc(s_mask, 16)
            for b in (qpad_a[0], qpad_a[1], qpad_b[0], qpad_b[1]):
                nc.gpsimd.memset(b, 0.0).then_inc(s_zero, 1)
            for n in range(1, REQ):
                for j in range(8):
                    pool.wait_ge(s_krused, 8 * (n - 1) + j + 1)
                    pool.dma_start(kr[j][:, NEWK:SW], d["kaT"][n, j, :, FIRST:PAST]).then_inc(s_kr[j], 16)
                for k in range(6):
                    pool.wait_ge(s_vrused, 6 * (n - 1) + k + 1)
                    pool.dma_start(vr[k], d["va"][n, FIRST + k * P:FIRST + (k + 1) * P, :]).then_inc(s_vr[k], 16)
            pool.wait_ge(s_vrused, 6 * REQ)
            for g in range(2):
                if g == 1:
                    pool.wait_ge(s_sPev, 4 * REQ)
                    pool.wait_ge(s_attout, 6 * 16)
                pool.dma_start(km[g].rearrange("p (n w) -> p n w", n=4), d["kmT"][4 * g:4 * g + 4].rearrange("n p w -> p n w")).then_inc(s_km[g], 16)
                pool.dma_start(vm[g].rearrange("p (n w) -> p n w", n=4), d["vm"][4 * g:4 * g + 4].rearrange("n p w -> p n w")).then_inc(s_km[g], 16)
                if g == 0:
                    pool.dma_start(km_p, d["mk_out"]).then_inc(s_km[g], 16)
                    pool.dma_start(vm_p, d["mv_out"]).then_inc(s_km[g], 16)
            def rows(ring, sems, table, idx, n):
                nc.gpsimd.indirect_dma_start(ring[n % RING], None, table, bass.IndirectOffsetOnAxis(idx, 0)).then_inc(sems[n % RING], 16)

            def column(n):
                return eidx[:, n // SLOTS, n % SLOTS:n % SLOTS + 1] if n < 2 * SLOTS else pair_idx[:, n - 2 * SLOTS:n - 2 * SLOTS + 1]

            def u_rows(n):
                pool.wait_ge(s_idx, min(n // SLOTS, 2) + 1)
                if n >= RING:
                    pool.wait_ge(s_udot, n - RING + 1)
                rows(u_ring, s_ug, d["expert_u"], column(n), n)

            def v_rows(n):
                if n >= RING:
                    pool.wait_ge(s_vmm, n + 1)
                rows(v_ring, s_vg, d["expert_v"], column(n), n)

            pool.wait_ge(s_cOev, 10)
            for n in range(SLOTS):
                u_rows(n)
            pool.wait_ge(s_used, W_END)
            nu, nv, n_all = SLOTS, 0, 2 * SLOTS + SLOTS // 2
            lead = 28
            while nv < n_all:
                v_rows(nv)
                nv += 1
                if nv > lead and nu < n_all:
                    u_rows(nu)
                    nu += 1
                if nv == SLOTS:
                    while nu < 2 * SLOTS:
                        u_rows(nu)
                        nu += 1

        @block.scalar
        def _(act):
            nac = [0]

            def link(ins):
                nac[0] += 1
                ins.then_inc(s_ac, 1)
                act.wait_ge(s_ac, nac[0])

            def norm(which, x, width, groups=1):
                u = N_NORM[which]
                extra = {"mem": 0, "mix": 1, "group": 2, "cross": 4, "ffn": 5}[which]
                for k in range(KT):
                    if k >= 8 or u > 0:
                        act.wait_ge(s_ss, 16 * u + k - 7)
                    nc.scalar.activation(sq[:, (k % 8) * NT:(k % 8) * NT + width], x[:, k * width:(k + 1) * width], ACT.Square).then_inc(s_sq, 1)
                for g in range(groups):
                    act.wait_ge(s_ss, 16 * u + (g + 1) * KT // groups)
                    if extra + g > 0:
                        act.wait_ge(s_rs, extra + g)
                    nc.scalar.activation(rms[:, 0:width], bank[2 + g][:, 0:width], ACT.Sqrt, bias=eps, scale=float(groups) / D).then_inc(s_rms, 1)

            act.wait_ge(s_eps, 1)
            act.wait_ge(s_memx, 16)
            norm("mem", mem_x, MEM)
            act.wait_ge(s_x, 16)
            norm("mix", XT, NT)
            for n in range(4):
                act.wait_ge(s_used, n + 1)
                nc.scalar.activation(mem_kT[:, n * MEM:(n + 1) * MEM], bank[n % 2][:, 0:MEM], ACT.Copy).then_inc(s_memev, 1)
            for n in range(2):
                act.wait_ge(s_used, W_IN)
                nc.scalar.activation(mem_v[:, n * 512:(n + 1) * 512], bank[4 + n], ACT.Copy).then_inc(s_memev, 1)
            act.wait_ge(s_memev, 6)
            act.dma_start(d["mk_out"], mem_kT).then_inc(s_memout, 16)
            act.dma_start(d["mv_out"], mem_v).then_inc(s_memout, 16)
            for n in range(9):
                t, q = n // 3, n % 3
                w, m = (512, P) if q < 2 else (128, P)
                if t == 2:
                    m = NS_TOK
                act.wait_ge(s_vt, n + 1)
                nc.scalar.activation(VT[0:m, t, q * 512:q * 512 + w], bank[3 + n % 2][0:m, 0:w], ACT.Copy).then_inc(s_vtev, 1)
            def exp_p(h):
                nb = h % 2
                act.wait_ge(s_max, h + 1)
                mx = stat[:, nb * 8:nb * 8 + 2]
                den = stat[:, nb * 8 + 2:nb * 8 + 4]
                for q, (a, b) in enumerate(((0, 256), (256, 384))):
                    ins = nc.scalar.activation(probs_p[:, nb, a:b], probs_p[:, nb, a:b], ACT.Exp, bias=mx[:, q:q + 1], scale=1.0, accum_out=den[:, q:q + 1])
                    if h < HEADS and q == 1:
                        ins.then_inc(s_exp, 1)
                if h >= HEADS:
                    nc.scalar.activation(stat[:, nb * 8 + 4:nb * 8 + 6], mx, ACT.Exp, bias=sink_prompt[:, h - HEADS:h - HEADS + 1], scale=1.0).then_inc(s_exp, 1)

            def turned_p(h):
                act.wait_ge(s_T, h + 1)
                if h >= 2:
                    act.wait_ge(s_O, h - 1)
                nc.scalar.activation(probsT_p[:, h % 2, :], bank[5][:, 0:384], ACT.Copy).then_inc(s_Tev, 1)

            for it in range(2 * HEADS + 1):
                if it < 2 * HEADS:
                    exp_p(it)
                if it >= 1:
                    turned_p(it - 1)
            for n in range(REQ):
                b = 16 + 8 * (n % 2)
                act.wait_ge(s_smax, 2 * n + 1)
                nc.scalar.activation(s_a, s_a, ACT.Exp, bias=stat[:, b:b + 1], scale=1.0, accum_out=stat[:, b + 2:b + 3]).then_inc(s_sexp, 1)
                act.wait_ge(s_smax, 2 * n + 2)
                nc.scalar.activation(s_b, s_b, ACT.Exp, bias=stat[:, b + 1:b + 2], scale=1.0, accum_out=stat[:, b + 3:b + 4])
                nc.scalar.activation(stat[:, b + 4:b + 5], stat[:, b + 1:b + 2], ACT.Exp, bias=sink_sample, scale=1.0).then_inc(s_sexp, 1)
                act.wait_ge(s_sT, 3 * n + 1)
                nc.scalar.activation(pT_a[0:NEWK, 0:P], bank[2][0:NEWK, 0:P], ACT.Copy)
                nc.scalar.activation(pT_a[:, P:384], bank[2][:, P:384], ACT.Copy).then_inc(s_sTev, 1)
                act.wait_ge(s_sT, 3 * n + 2)
                nc.scalar.activation(pT_a[:, 384:896], bank[3][:, 0:512], ACT.Copy).then_inc(s_sTev, 1)
                act.wait_ge(s_sT, 3 * n + 3)
                nc.scalar.activation(pT_b[:, 0:P], bank[7][:, 256:384], ACT.Copy)
                nc.scalar.activation(pT_b[0:NEWK, P:2 * P], bank[7][0:NEWK, 384:512], ACT.Copy).then_inc(s_sTev, 1)
            act.wait_ge(s_attout, 6 * 16)
            act.wait_ge(s_sPev, 4 * REQ)
            norm("group", OT, NT, 2)
            act.wait_ge(s_ev, T_IN + KT)
            norm("cross", XT, NT)
            def exp_c(u):
                act.wait_ge(s_cmax, u + 1)
                if u >= 2:
                    act.wait_ge(s_cT, u - 1)
                nb = u % 2
                nc.scalar.activation(probs_c[:, nb, :], bank[3 + nb][:, 0:256], ACT.Exp, bias=stat[:, 64 + nb:65 + nb], scale=MEM_SCALE, accum_out=stat[:, 66 + nb:67 + nb]).then_inc(s_cexp, 1)

            def turned_c(u):
                act.wait_ge(s_cT, u + 1)
                if u >= 2:
                    act.wait_ge(s_cO, u - 1)
                nc.scalar.activation(probsT_c[:, u % 2, :], bank[5][:, 0:256], ACT.Copy).then_inc(s_cTev, 1)

            for it in range(11):
                if it < 10:
                    exp_c(it)
                if it >= 1:
                    turned_c(it - 1)
            act.wait_ge(s_ev, T_IN + KT + 4 + KT)
            norm("ffn", XT, NT)
            for t in range(3):
                m = P if t < 2 else NS_TOK
                act.wait_ge(s_xt, t + 1)
                if t == 0:
                    act.wait_ge(s_h, 80)
                link(nc.scalar.activation(h_tok[t][0:m, :], big[0:m, :], ACT.Square, accum_out=stat[0:m, 30 + t:31 + t]))
                nc.scalar.activation(stat[0:m, 33 + t:34 + t], stat[0:m, 30 + t:31 + t], ACT.Sqrt, bias=eps[0:m, :], scale=1.0 / D).then_inc(s_xrms, 1)

            def gate_exp(t):
                act.wait_ge(s_gx, t + 1)
                nc.scalar.activation(gexp[t], gexp[t], ACT.Exp).then_inc(s_gxe, 1)

            def gelu(t):
                n = SLOTS if t < 2 else SLOTS // 2
                act.wait_ge(s_udot, min((t + 1) * SLOTS, 2 * SLOTS + SLOTS // 2))
                nc.scalar.activation(dots[:, t, 0:n], dots[:, t, 0:n], ACT.Gelu).then_inc(s_gelu, 1)

            def diagonals(t):
                n = SLOTS if t < 2 else SLOTS // 2
                src, w = (ident, P) if t < 2 else (pair_sel, 64)
                act.wait_ge(s_coef, t + 1)
                with act.Fori(0, n // RING) as i:
                    for r in range(RING):
                        act.wait_ge(s_vmm, i * RING + (t * SLOTS + r + 1))
                        nc.scalar.activation(diag[r][:, 0:w], src, ACT.Copy, scale=dots[:, t, bass.ds(i * RING + r, 1)]).then_inc(s_dg, 1)

            def finish(t):
                m = P if t < 2 else NS_TOK
                act.wait_ge(s_vmm, min((t + 1) * SLOTS, 2 * SLOTS + SLOTS // 2) + RING)
                link(nc.scalar.activation(h_tok[t][0:m, :], big[0:m, :], ACT.Square, accum_out=stat[0:m, 40 + t:41 + t]))
                nc.scalar.activation(stat[0:m, 43 + t:44 + t], stat[0:m, 40 + t:41 + t], ACT.Sqrt, bias=eps[0:m, :], scale=1.0 / D).then_inc(s_frms, 1)

            for t in range(3):
                gate_exp(t)
                if t:
                    finish(t - 1)
                gelu(t)
                diagonals(t)
            finish(2)

        @block.vector
        def _(dve):
            ndv = [0]

            def link(ins):
                ndv[0] += 1
                ins.then_inc(s_dv, 1)
                dve.wait_ge(s_dv, ndv[0])

            def norm(which, x, gain, out, width, groups=1):
                base = {"mem": 0, "mix": 1, "group": 2, "cross": 4, "ffn": 5}[which]
                u = N_NORM[which]
                per = KT // groups
                for g in range(groups):
                    dve.wait_ge(s_rms, base + g + 1)
                    nc.vector.reciprocal(rs[:, 0:width], rms[:, 0:width]).then_inc(s_rs, 1)
                    dve.wait_ge(s_rs, base + g + 1)
                    for k in range(g * per, (g + 1) * per):
                        nc.vector.scalar_tensor_tensor(out=out[:, k * width:(k + 1) * width], in0=x[:, k * width:(k + 1) * width],
                                                       scalar=gain[:, k:k + 1], in1=rs[:, 0:width], op0=ALU.mult, op1=ALU.mult).then_inc(s_h, 1)
                    dve.wait_ge(s_h, 16 * u + (g + 1) * per)

            dve.wait_ge(s_const, 16)
            norm("mem", mem_x, G_MEM, mem_x, MEM)
            norm("mix", XT, G_MIX, HT, NT)
            dve.wait_ge(s_used, W_IN)
            with dve.Fori(0, 8) as i:
                for r in range(4):
                    dve.wait_ge(s_used, i * 4 + (W_IN + r + 1))
                    nc.vector.tensor_scalar(QK[:, bass.ds(i * (4 * NT) + r * NT, NT)], bank[r % 2][:, 0:NT], 1.0, None, ALU.mult).then_inc(s_ev, 1)
            for f in (T_IN - 2, T_IN - 1):
                dve.wait_ge(s_used, W_IN + f + 1)
                nc.vector.tensor_scalar(QK[:, f * NT:(f + 1) * NT], bank[f % 2][:, 0:NT], 1.0, None, ALU.mult).then_inc(s_ev, 1)
            dve.wait_ge(s_ev, T_IN)
            for n in range(16):
                dve.wait_ge(s_bias, n + 1)
                nc.vector.tensor_copy(bias_p[:, :, n * 16:(n + 1) * 16], bank[6 + n % 2].rearrange("p (c h) -> p h c", h=32)).then_inc(s_biasev, 1)
            dve.wait_ge(s_bias, 17)
            nc.vector.tensor_copy(bias_sa[:, 0:512], bank[6]).then_inc(s_biasev, 1)
            dve.wait_ge(s_bias, 18)
            nc.vector.tensor_copy(bias_sa[:, 512:USED + WIN], bank[7][:, 0:USED + WIN - 512]).then_inc(s_biasev, 1)
            dve.wait_ge(s_bias, 19)
            nc.vector.tensor_copy(bias_sb, bank[6][:, 0:P + WIN]).then_inc(s_biasev, 1)
            for j in range(8):
                nc.vector.tensor_copy(kr[j][:, 0:NEWK], QK[:, (T_KA + j) * NT + NP_TOK:(T_KA + j + 1) * NT]).then_inc(s_newk, 1)
            dve.wait_ge(s_biasev, 19)
            def max_p(h):
                nb = h % 2
                if h >= 2:
                    dve.wait_ge(s_T, h - 1)
                dve.wait_ge(s_S, h + 1)
                pb = probs_p[:, nb, :]
                nc.vector.scalar_tensor_tensor(out=pb[:, 0:256], in0=bank[nb][:, 0:256], scalar=SCALE, in1=bias_p[:, h, :], op0=ALU.mult, op1=ALU.add)
                link(nc.vector.scalar_tensor_tensor(out=pb[:, 256:384], in0=bank[nb][:, 256:384], scalar=SCALE, in1=bias_p[:, h, 128:256], op0=ALU.mult, op1=ALU.add))
                mx = stat[:, nb * 8:nb * 8 + 2]
                t = stat[:, 50:52]
                nc.vector.tensor_reduce(t[:, 0:1], pb[:, 0:256], AX_X, ALU.max)
                link(nc.vector.tensor_reduce(t[:, 1:2], pb[:, 256:384], AX_X, ALU.max))
                if h >= HEADS:
                    nc.vector.tensor_scalar(mx, t, sink_prompt[:, h - HEADS:h - HEADS + 1], -1.0, ALU.max, ALU.mult).then_inc(s_max, 1)
                else:
                    nc.vector.tensor_scalar(mx, t, -1.0, None, ALU.mult).then_inc(s_max, 1)

            def norm_p(h):
                nb = h % 2
                dve.wait_ge(s_exp, h + 1)
                den = stat[:, nb * 8 + 2:nb * 8 + 4]
                rd = stat[:, nb * 8 + 6:nb * 8 + 8]
                if h >= HEADS:
                    link(nc.vector.tensor_tensor(den, den, stat[:, nb * 8 + 4:nb * 8 + 6], ALU.add))
                link(nc.vector.reciprocal(rd, den))
                pb = probs_p[:, nb, :]
                nc.vector.tensor_scalar(pb[:, 0:256], pb[:, 0:256], rd[:, 0:1], None, ALU.mult)
                nc.vector.tensor_scalar(pb[:, 256:384], pb[:, 256:384], rd[:, 1:2], None, ALU.mult).then_inc(s_nrm, 1)

            def out_p(h):
                dve.wait_ge(s_O, h + 1)
                s, f = 64 * (h % HEADS // 8), (h // HEADS) * 8 + h % 8
                nc.vector.tensor_copy(OT[s:s + 64, f * NT:f * NT + NP_TOK], bank[6 + h % 2][0:64, 0:256]).then_inc(s_Oev, 1)

            for it in range(2 * HEADS + 2):
                if it < 2 * HEADS:
                    max_p(it)
                if 1 <= it <= 2 * HEADS:
                    norm_p(it - 1)
                if it >= 2:
                    out_p(it - 2)
            def pads(n):
                if n == 0:
                    dve.wait_ge(s_zero, 4)
                if n >= 2:
                    dve.wait_ge(s_sS, n - 1)
                t0 = NP_TOK + QPR * n
                src_a = QK[:, T_QA * NT:T_KA * NT].rearrange("p (j t) -> p j t", t=NT)
                src_b = QK[:, T_QB * NT:T_KB * NT].rearrange("p (j t) -> p j t", t=NT)
                for s in range(2):
                    rows = slice(64 * s, 64 * s + 64)
                    pa = qpad_a[n % 2][rows, :].rearrange("p (j c) -> p j c", c=136)[:, :, 64 * s:64 * s + QPR]
                    nc.vector.tensor_copy(pa, src_a[rows, :, t0:t0 + QPR]).then_inc(s_qpad, 1)
                    pb = qpad_b[n % 2][rows, 64 * s:64 * s + 64].rearrange("p (j q) -> p j q", q=QPR)
                    nc.vector.tensor_copy(pb, src_b[rows, :, t0:t0 + QPR]).then_inc(s_qpad, 1)

            def softmax_s(n):
                w0, b = (REQ - 1 - n) * QPR, 16 + 8 * (n % 2)
                dve.wait_ge(s_krused, 8 * n + 8)
                if n:
                    dve.wait_ge(s_sT, 3 * n - 1)
                nc.vector.scalar_tensor_tensor(out=s_a[:, 0:NEWK], in0=bank[0][:, 0:NEWK], scalar=SCALE, in1=bias_sa[:, USED + w0:USED + w0 + NEWK], op0=ALU.mult, op1=ALU.add)
                nc.vector.scalar_tensor_tensor(out=s_a[:, NEWK:320], in0=bank[0][:, NEWK:320], scalar=SCALE, in1=bias_sa[:, 0:FIRST], op0=ALU.mult, op1=ALU.add)
                link(nc.vector.scalar_tensor_tensor(out=s_a[:, 320:SW], in0=bank[1], scalar=SCALE, in1=bias_sa[:, FIRST:USED], op0=ALU.mult, op1=ALU.add))
                link(nc.vector.tensor_reduce(stat[:, 52:53], s_a, AX_X, ALU.max))
                nc.vector.tensor_scalar(stat[:, b:b + 1], stat[:, 52:53], -1.0, None, ALU.mult).then_inc(s_smax, 1)
                dve.wait_ge(s_sS, n + 1)
                if n:
                    dve.wait_ge(s_sT, 3 * n)
                nc.vector.scalar_tensor_tensor(out=s_b[:, 0:P], in0=bank[6][:, 0:P], scalar=SCALE, in1=bias_sb[:, 0:P], op0=ALU.mult, op1=ALU.add)
                link(nc.vector.scalar_tensor_tensor(out=s_b[:, P:P + NEWK], in0=bank[6][:, P:P + NEWK], scalar=SCALE, in1=bias_sb[:, P + w0:P + w0 + NEWK], op0=ALU.mult, op1=ALU.add))
                link(nc.vector.tensor_reduce(stat[:, 53:54], s_b, AX_X, ALU.max))
                nc.vector.tensor_scalar(stat[:, b + 1:b + 2], stat[:, 53:54], sink_sample, -1.0, ALU.max, ALU.mult).then_inc(s_smax, 1)

            def pair_s(n):
                b = 16 + 8 * (n % 2)
                dve.wait_ge(s_sexp, 2 * n + 2)
                link(nc.vector.tensor_tensor(stat[:, b + 3:b + 4], stat[:, b + 3:b + 4], stat[:, b + 4:b + 5], ALU.add))
                link(nc.vector.reciprocal(stat[:, b + 5:b + 7], stat[:, b + 2:b + 4]))
                dve.wait_ge(s_vrused, 6 * n + 6)
                for s in range(2):
                    rows = slice(64 * s, 64 * s + 64)
                    ins = nc.vector.scalar_tensor_tensor(out=o_masked[rows, :], in0=bank[4 + s][rows, :], scalar=stat[rows, b + 5:b + 6], in1=head_mask[rows, :], op0=ALU.mult, op1=ALU.mult)
                link(ins)
                if n:
                    dve.wait_ge(s_sP, n)
                nc.vector.tensor_reduce(o_pair[:, 0:64], o_masked.rearrange("p (h e) -> p e h", h=8), AX_X, ALU.add)
                dve.wait_ge(s_sO, n + 1)
                for s in range(2):
                    rows = slice(64 * s, 64 * s + 64)
                    ins = nc.vector.tensor_scalar(o_pair[rows, 64:128], bank[7][rows, 64 * s:64 * s + 64], stat[rows, b + 6:b + 7], None, ALU.mult)
                ins.then_inc(s_sOev, 1)

            def keep_s(n):
                dve.wait_ge(s_sP, n + 1)
                t0 = NP_TOK + QPR * n
                for m in range(2):
                    for s in range(2):
                        dst = OT[64 * s:64 * s + 64, m * 8 * NT:(m + 1) * 8 * NT].rearrange("p (j t) -> p j t", t=NT)[:, :, t0:t0 + QPR]
                        src = bank[7][64 * m:64 * m + 64, 128 + 64 * s:192 + 64 * s].rearrange("p (j q) -> p j q", q=QPR)
                        nc.vector.tensor_copy(dst, src).then_inc(s_sPev, 1)

            pads(0)
            pads(1)
            dve.wait_ge(s_mask, 16)
            dve.wait_ge(s_Oev, 2 * HEADS)
            softmax_s(0)
            for n in range(REQ):
                if n + 2 < REQ:
                    pads(n + 2)
                if n:
                    keep_s(n - 1)
                if n + 1 < REQ:
                    softmax_s(n + 1)
                pair_s(n)
            keep_s(REQ - 1)
            dve.wait_ge(s_sPev, 4 * REQ)
            norm("group", OT, G_AB, OT, NT, 2)

            def add_to_stream(at):
                with dve.Fori(0, 4) as i:
                    for r in range(4):
                        dve.wait_ge(s_used, i * 4 + (W_IN + at + r + 1))
                        x = XT[:, bass.ds(i * (4 * NT) + r * NT, NT)]
                        nc.vector.tensor_tensor(x, x, bank[r % 2][:, 0:NT], ALU.add).then_inc(s_ev, 1)
                dve.wait_ge(s_ev, at + KT)

            add_to_stream(T_IN)
            norm("cross", XT, G_CROSS, HT, NT)
            for f in range(4):
                dve.wait_ge(s_used, W_CQ + f + 1)
                nc.vector.tensor_copy(qc[:, f, :], bank[f % 2][:, 0:NT]).then_inc(s_ev, 1)
            link(nc.vector.memset(qpad_c, 0.0))
            dve.wait_ge(s_ev, T_IN + KT + 4)

            def pads_c(g):
                if g:
                    dve.wait_ge(s_cS, 9)
                for h in range(4):
                    dst = qpad_c.rearrange("p (n h c) -> p n h c", n=4, h=4)[:, :, h, 0:QPR]
                    src = qc[:, h, NP_TOK + 32 * g:NP_TOK + 32 * g + 32].rearrange("p (n q) -> p n q", q=QPR)
                    nc.vector.tensor_copy(dst, src).then_inc(s_cpad, 1)

            def max_c(u):
                nb = u % 2
                dve.wait_ge(s_cS, u + 1)
                if u:
                    dve.wait_ge(s_cmax, u)
                link(nc.vector.tensor_reduce(stat[:, 56:57], bank[3 + nb][:, 0:256], AX_X, ALU.max))
                nc.vector.tensor_scalar(stat[:, 64 + nb:65 + nb], stat[:, 56:57], -MEM_SCALE, None, ALU.mult).then_inc(s_cmax, 1)

            def norm_c(u):
                nb = u % 2
                dve.wait_ge(s_cexp, u + 1)
                link(nc.vector.reciprocal(stat[:, 68 + nb:69 + nb], stat[:, 66 + nb:67 + nb]))
                nc.vector.tensor_scalar(probs_c[:, nb, :], probs_c[:, nb, :], stat[:, 68 + nb:69 + nb], None, ALU.mult).then_inc(s_cnrm, 1)

            def out_c(u):
                dve.wait_ge(s_cO, u + 1)
                if u < 8:
                    h, q = u % 4, u // 4
                    nc.vector.tensor_copy(oc[:, h, q * P:(q + 1) * P], bank[6 + u % 2][:, 0:128]).then_inc(s_cOev, 1)
                else:
                    g = u - 8
                    for h in range(4):
                        src = bank[6 + u % 2][:, 0:128].rearrange("p (n h q) -> p n h q", n=4, h=4)[:, :, h, :]
                        dst = oc[:, h, NP_TOK + 32 * g:NP_TOK + 32 * g + 32].rearrange("p (n q) -> p n q", q=QPR)
                        ins = nc.vector.tensor_copy(dst, src)
                    ins.then_inc(s_cOev, 1)

            pads_c(0)
            for it in range(12):
                if it < 10:
                    max_c(it)
                if 1 <= it <= 10:
                    norm_c(it - 1)
                if it >= 2:
                    out_c(it - 2)
                if it == 8:
                    pads_c(1)
            add_to_stream(T_IN + KT + 4)
            norm("ffn", XT, G_FFN, HT, NT)
            for f in range(KT):
                dve.wait_ge(s_used, W_PQ + f + 1)
                nc.vector.tensor_copy(qp[:, f, 0:NT], bank[f % 2][:, 0:NT])
                nc.vector.tensor_copy(qp[:, f, NT:384], bank[f % 2][:, NP_TOK:NT]).then_inc(s_ev, 1)
            dve.wait_ge(s_grow, 16)
            for t in range(3):
                m = P if t < 2 else NS_TOK
                dve.wait_ge(s_xrms, t + 1)
                link(nc.vector.reciprocal(stat[0:m, 36 + t:37 + t], stat[0:m, 33 + t:34 + t]))
                nc.vector.scalar_tensor_tensor(out=h_tok[t][0:m, :], in0=big[0:m, :], scalar=stat[0:m, 36 + t:37 + t], in1=g_row[0:m, :], op0=ALU.mult, op1=ALU.mult).then_inc(s_ht, 1)

            def top_k(src, values, indices, n):
                for half in range(2):
                    o = slice(8 * half, 8 * half + 8)
                    for x in range(n):
                        ins = nc.vector.max(values(x)[:, o], src(x))
                    link(ins)
                    for x in range(n):
                        ins = nc.vector.max_index(indices(x)[:, o], values(x)[:, o], src(x))
                    link(ins)
                    if half == 0:
                        for x in range(n):
                            ins = nc.vector.match_replace(src(x), values(x)[:, o], src(x), -3e38)
                        link(ins)

            def choose(t):
                dve.wait_ge(s_sc, t + 1)
                for q in range(4):
                    ins = nc.vector.tensor_copy(sc[:, q * 512:(q + 1) * 512], bank[q])
                ins.then_inc(s_scev, 1)
                dve.wait_ge(s_scev, t + 1)
                top_k(lambda x: sc[:, x * P:(x + 1) * P], lambda x: top_v[:, x // 2, x % 2, :], lambda x: top_i[:, x // 2, x % 2, :], 2 * PH)
                nc.vector.tensor_copy(top_f, top_i)
                cand = sc.rearrange("p (h i j) -> p h i j", h=PH, i=PK)
                link(nc.vector.tensor_tensor(cand, top_v[:, :, 0, :].unsqueeze(3).broadcast_to([P, PH, PK, PK]), top_v[:, :, 1, :].unsqueeze(2).broadcast_to([P, PH, PK, PK]), ALU.add))
                top_k(lambda h: sc[:, h * 256:(h + 1) * 256], lambda h: best[:, h, :], lambda h: pos[:, h, :], PH)
                nc.vector.tensor_scalar(pos_i[:, 0:SLOTS], pos.rearrange("p h k -> p (h k)"), 4, None, ALU.logical_shift_right)
                link(nc.vector.tensor_scalar(pos_i[:, SLOTS:2 * SLOTS], pos.rearrange("p h k -> p (h k)"), 15, None, ALU.bitwise_and))
                link(nc.vector.tensor_copy(pos_f, pos_i))
                nc.vector.tensor_tensor(gexp[t], best, best[:, :, 0:1].broadcast_to([P, PH, PK]), ALU.subtract).then_inc(s_gx, 1)
                oh = sc.rearrange("p (s i) -> p s i", i=PK)
                oh4 = sc.rearrange("p (h k i) -> p h k i", h=PH, k=PK)
                for z in range(2):
                    link(nc.vector.tensor_tensor(oh, pos_f[:, z * SLOTS:(z + 1) * SLOTS].unsqueeze(2).broadcast_to([P, SLOTS, PK]), iota16.unsqueeze(1).broadcast_to([P, SLOTS, PK]), ALU.is_equal))
                    link(nc.vector.tensor_tensor(oh4, oh4, top_f[:, :, z, :].unsqueeze(2).broadcast_to([P, PH, PK, PK]), ALU.mult))
                    link(nc.vector.tensor_reduce(exp_f[:, z * SLOTS:(z + 1) * SLOTS], oh, AX_X, ALU.add))
                link(nc.vector.scalar_tensor_tensor(out=eidx_f, in0=exp_f[:, 0:SLOTS], scalar=float(NKEY), in1=exp_f[:, SLOTS:2 * SLOTS], op0=ALU.mult, op1=ALU.add))
                if t < 2:
                    nc.vector.tensor_copy(eidx[:, t, :], eidx_f).then_inc(s_idx, 1)
                else:
                    link(nc.vector.tensor_copy(eidx[:, t, :], eidx_f))
                    for s in range(2):
                        rows = slice(64 * s, 64 * s + 64)
                        ins = nc.vector.tensor_copy(pair_idx[rows, :], eidx[rows, 2, 64 * s:64 * s + 64])
                    ins.then_inc(s_idx, 1)

            def weigh(t):
                dve.wait_ge(s_gxe, t + 1)
                link(nc.vector.tensor_reduce(stat[:, 60:68], gexp[t], AX_X, ALU.add))
                link(nc.vector.reciprocal(stat[:, 68:76], stat[:, 60:68]))
                link(nc.vector.tensor_tensor(gate[:, t, :].rearrange("p (h k) -> p h k", h=PH), gexp[t], stat[:, 68:76].unsqueeze(2).broadcast_to([P, PH, PK]), ALU.mult))
                if t == 2:
                    for s in range(2):
                        rows = slice(64 * s, 64 * s + 64)
                        link(nc.vector.tensor_copy(pair_gate[rows, :], gate[rows, 2, 64 * s:64 * s + 64]))

            def u_dots(t):
                n = SLOTS if t < 2 else SLOTS // 2
                if t == 2:
                    dve.wait_ge(s_dup, 16)
                with dve.Fori(0, n // RING) as i:
                    for r in range(RING):
                        dve.wait_ge(s_ug[r], i * 16 + 16 * (t * SLOTS // RING + 1))
                        nc.vector.scalar_tensor_tensor(out=u_ring[r], in0=u_ring[r], scalar=1.0, in1=h_tok[t], op0=ALU.mult, op1=ALU.mult,
                                                       accum_out=dots[:, t, bass.ds(i * RING + r, 1)]).then_inc(s_udot, 1)

            def coefs(t):
                n = SLOTS if t < 2 else SLOTS // 2
                dve.wait_ge(s_gelu, t + 1)
                g = gate[:, t, :] if t < 2 else pair_gate
                nc.vector.tensor_tensor(dots[:, t, 0:n], dots[:, t, 0:n], g, ALU.mult).then_inc(s_coef, 1)

            def finish(t):
                m = P if t < 2 else NS_TOK
                dve.wait_ge(s_frms, t + 1)
                link(nc.vector.reciprocal(stat[0:m, 46 + t:47 + t], stat[0:m, 43 + t:44 + t]))
                nc.vector.scalar_tensor_tensor(out=h_tok[t][0:m, :], in0=big[0:m, :], scalar=stat[0:m, 46 + t:47 + t], in1=g_row[0:m, :], op0=ALU.mult, op1=ALU.mult).then_inc(s_y, 1)

            dve.wait_ge(s_ht, 3)
            choose(0)
            weigh(0)
            u_dots(0)
            coefs(0)
            choose(1)
            choose(2)
            u_dots(1)
            weigh(1)
            dve.wait_ge(s_grow, 32)
            finish(0)
            coefs(1)
            u_dots(2)
            weigh(2)
            finish(1)
            coefs(2)
            finish(2)

        @block.tensor
        def _(pe):
            def mm(out, lhsT, rhs, start=True, stop=True):
                return nc.tensor.matmul(out, lhsT, rhs, start=start, stop=stop, skip_group_check=True)

            def norm(which, width, groups=1):
                u = N_NORM[which]
                before = {"mem": 0, "mix": 1, "group": 2, "cross": 4, "ffn": 5}[which]
                per = KT // groups
                if before:
                    pe.wait_ge(s_rms, before)
                for k in range(KT):
                    pe.wait_ge(s_sq, 16 * u + k + 1)
                    mm(bank[2 + k // per][:, 0:width], ones, sq[:, (k % 8) * NT:(k % 8) * NT + width], start=(k % per == 0), stop=(k % per == per - 1)).then_inc(s_ss, 1)

            pe.wait_ge(s_const, 16)
            norm("mem", MEM)
            norm("mix", NT)
            pe.wait_ge(s_h, 16)
            for c in range(4):
                chunk_wait(pe, c)
                if c >= 2:
                    pe.wait_ge(s_memev, c - 1)
                w = WR[:, c * D:(c + 1) * D]
                for k in range(KT):
                    ins = mm(bank[c % 2][:, 0:MEM], w[:, k * P:(k + 1) * P], mem_x[:, k * MEM:(k + 1) * MEM], start=(k == 0), stop=(k == KT - 1))
                ins.then_inc(s_used, 1)
            for c in range(4, 8):
                chunk_wait(pe, c)
                w = WR[:, (c - 4) * D:(c - 3) * D]
                for t in range(2):
                    for q in range(4):
                        k = 4 * (c - 4) + q
                        ins = mm(bank[4 + t], mem_x[:, k * MEM + t * P:k * MEM + (t + 1) * P], w[:, q * 512:(q + 1) * 512], start=(k == 0), stop=(k == KT - 1))
                ins.then_inc(s_used, 1)

            def project(slot, x, b):
                for k in range(KT):
                    ins = mm(bank[b][:, 0:NT], WR[:, slot * D + k * P:slot * D + (k + 1) * P], x[:, k * NT:(k + 1) * NT], start=(k == 0), stop=(k == KT - 1))
                return ins

            def tile(slot, x, b, arrived, free):
                pe.wait_ge(s_w[slot], arrived)
                if free is not None:
                    pe.wait_ge(s_ev, free)
                project(slot, x, b).then_inc(s_used, 1)

            pe.wait_ge(s_memev, 4)
            pe.wait_ge(s_h, 32)
            for f in range(4):
                tile(f, HT, f % 2, 16 * 3, f - 1 if f >= 2 else None)
            with pe.Fori(1, 8) as i:
                for r in range(4):
                    tile(r, HT, r % 2, i * 16 + 48, i * 4 + (r - 1))
            for f in (32, 33):
                tile(f % 4, HT, f % 2, 16 * ((f + 8) // 4 + 1), f - 1)

            pe.wait_ge(s_ev, T_IN)
            pe.wait_ge(s_memev, 6)
            for n in range(9):
                t, q = n // 3, n % 3
                m = P if t < 2 else NS_TOK
                if n >= 2:
                    pe.wait_ge(s_vtev, n - 1)
                nf = 4 if q < 2 else 1
                for f in range(nf):
                    src = QK[:, (T_VA + 4 * q + f) * NT + t * P:(T_VA + 4 * q + f) * NT + t * P + m]
                    ins = nc.tensor.transpose(bank[3 + n % 2][0:m, f * P:(f + 1) * P], src, ident)
                ins.then_inc(s_vt, 1)
            pe.wait_ge(s_tab, 16)
            for n in range(16):
                if n >= 2:
                    pe.wait_ge(s_biasev, n - 1)
                for q in range(4):
                    c0 = 16 * n + 4 * q
                    ins = mm(bank[6 + n % 2][:, q * 128:(q + 1) * 128], oh_p[:, 252 - c0:380 - c0], rb_p)
                ins.then_inc(s_bias, 1)
            for n, (g, a, b) in enumerate(((0, 0, 512), (0, 512, USED + WIN), (1, 0, P + WIN))):
                pe.wait_ge(s_biasev, 15 + n)
                oh = oh_sb if g else oh_sa
                for t in range(2):
                    ins = mm(bank[6 + n % 2][:, 0:b - a], rb_s[:, g, t, :], oh[:, t, a:b], start=(t == 0), stop=(t == 1))
                ins.then_inc(s_bias, 1)
            pe.wait_ge(s_biasev, 19)
            pe.wait_ge(s_vtev, 9)

            def scores_p(h):
                s, j, m = 64 * (h % HEADS // 8), h % 8, h // HEADS
                if h >= 2:
                    pe.wait_ge(s_max, h - 1)
                qt = QK[s:s + 64, (T_QB if m else T_QA) * NT + j * NT:][:, 0:NT]
                kt = QK[s:s + 64, (T_KB if m else T_KA + j) * NT:][:, 0:NT]
                mm(bank[h % 2][:, 0:256], qt[:, 128:256], kt[:, 0:256])
                mm(bank[h % 2][:, 256:384], qt[:, 0:128], kt[:, 0:128]).then_inc(s_S, 1)

            def turn_p(h):
                pe.wait_ge(s_nrm, h + 1)
                if h:
                    pe.wait_ge(s_Tev, h)
                for b in range(3):
                    ins = nc.tensor.transpose(bank[5][:, b * P:(b + 1) * P], probs_p[:, h % 2, b * P:(b + 1) * P], ident)
                ins.then_inc(s_T, 1)

            def values_p(h):
                pe.wait_ge(s_Tev, h + 1)
                if h >= 2:
                    pe.wait_ge(s_Oev, h - 1)
                c = (h * DH) if h < HEADS else 1024 + 64 * ((h - HEADS) // 8)
                o = bank[6 + h % 2]
                pT = probsT_p[:, h % 2, :]
                mm(o[0:64, 128:256], VT[:, 0, c:c + DH], pT[:, 0:128], start=True, stop=False)
                mm(o[0:64, 128:256], VT[:, 1, c:c + DH], pT[:, 128:256], start=False, stop=True)
                mm(o[0:64, 0:128], VT[:, 0, c:c + DH], pT[:, 256:384]).then_inc(s_O, 1)

            for it in range(2 * HEADS + 2):
                if it < 2 * HEADS:
                    scores_p(it)
                if it >= 2:
                    values_p(it - 2)
                if 1 <= it <= 2 * HEADS:
                    turn_p(it - 1)
            pe.wait_ge(s_newk, 8)
            pe.wait_ge(s_kb, 16)
            pe.wait_ge(s_vb, 16)
            pe.wait_ge(s_Oev, 2 * HEADS)

            def scores_s(n):
                if n:
                    pe.wait_ge(s_smax, 2 * n)
                pe.wait_ge(s_qpad, 4 * n + 4)
                for j in range(8):
                    pe.wait_ge(s_kr[j], 16 * (n + 1))
                    w = qpad_a[n % 2][:, j * P:(j + 1) * P]
                    mm(bank[0][:, 0:320], w, kr[j][:, 0:320], start=(j == 0), stop=(j == 7))
                    mm(bank[1], w, kr[j][:, 320:SW], start=(j == 0), stop=(j == 7)).then_inc(s_krused, 1)
                mm(bank[6][:, 0:P], qpad_b[n % 2], kbT[:, n, :])
                mm(bank[6][:, P:P + NEWK], qpad_b[n % 2], QK[:, T_KB * NT + NP_TOK:T_VA * NT]).then_inc(s_sS, 1)

            def turn_s(n):
                pe.wait_ge(s_sexp, 2 * n + 1)
                for b, (a, w) in enumerate(((0, 64), (64, 128), (192, 128), (320, 128), (448, 128), (576, 128), (704, 128))):
                    t, o = (2, b * P) if b < 3 else (3, (b - 3) * P)
                    ins = nc.tensor.transpose(bank[t][0:w, o:o + P], s_a[:, a:a + w], ident)
                    if b in (2, 6):
                        ins.then_inc(s_sT, 1)
                pe.wait_ge(s_sexp, 2 * n + 2)
                if n:
                    pe.wait_ge(s_sPev, 4 * n)
                nc.tensor.transpose(bank[7][:, 256:384], s_b[:, 0:P], ident)
                nc.tensor.transpose(bank[7][0:NEWK, 384:512], s_b[:, P:P + NEWK], ident).then_inc(s_sT, 1)

            def values_s(n):
                pe.wait_ge(s_sTev, 3 * n + 2)
                if n:
                    pe.wait_ge(s_sOev, n)
                for b in range(7):
                    m = NEWK if b == 0 else P
                    if b:
                        pe.wait_ge(s_vr[b - 1], 16 * (n + 1))
                    for q in range(2):
                        v = VT[0:m, 2, q * 512:(q + 1) * 512] if b == 0 else vr[b - 1][:, q * 512:(q + 1) * 512]
                        ins = mm(bank[4 + q], pT_a[0:m, b * P:(b + 1) * P], v, start=(b == 0), stop=(b == 6))
                    if b:
                        ins.then_inc(s_vrused, 1)
                pe.wait_ge(s_sTev, 3 * n + 3)
                mm(bank[7][:, 0:P], pT_b[:, 0:P], vb[:, n, :], start=True, stop=False)
                mm(bank[7][:, 0:P], pT_b[0:NEWK, P:2 * P], VT[0:NEWK, 2, 1024:VW], start=False, stop=True).then_inc(s_sO, 1)

            def pair_s(n):
                pe.wait_ge(s_sOev, n + 1)
                if n:
                    pe.wait_ge(s_sPev, 4 * n)
                nc.tensor.transpose(bank[7][:, 128:256], o_pair, ident).then_inc(s_sP, 1)

            scores_s(0)
            for n in range(REQ):
                if n + 1 < REQ:
                    scores_s(n + 1)
                if n:
                    pair_s(n - 1)
                turn_s(n)
                values_s(n)
            pair_s(REQ - 1)
            norm("group", NT, 2)

            def stream_tiles(x, at, c_at):
                with pe.Fori(0, 4) as i:
                    for r in range(4):
                        tile((c_at + r) % 4, x, r % 2, i * 16 + 16 * ((c_at + r) // 4 + 1), i * 4 + (at + r - 1))

            pe.wait_ge(s_h, 48)
            stream_tiles(OT, T_IN, C_OUT)
            at = T_IN + KT
            norm("cross", NT)
            pe.wait_ge(s_h, 64)
            for f in range(4):
                c = C_CQ + f
                tile(c % 4, HT, f % 2, 16 * (c // 4 + 1), at + f - 1)
            at += 4
            pe.wait_ge(s_ev, at)

            def scores_c(u):
                if u >= 2:
                    pe.wait_ge(s_cexp, u - 1)
                o = bank[3 + u % 2][:, 0:256]
                if u < 8:
                    if u == 0:
                        pe.wait_ge(s_km[0], 64)
                    h, q = u % 4, u // 4
                    mm(o, qc[:, h, q * P:(q + 1) * P], km_p[:, h * MEM:(h + 1) * MEM]).then_inc(s_cS, 1)
                else:
                    g = u - 8
                    if g:
                        pe.wait_ge(s_km[1], 32)
                    pe.wait_ge(s_cpad, 4 * g + 4)
                    for m in range(16):
                        ins = mm(o, qpad_c[:, m * P:(m + 1) * P], km[g][:, m * MEM:(m + 1) * MEM], start=(m == 0), stop=(m == 15))
                    ins.then_inc(s_cS, 1)

            def turn_c(u):
                pe.wait_ge(s_cnrm, u + 1)
                if u:
                    pe.wait_ge(s_cTev, u)
                for b in range(2):
                    ins = nc.tensor.transpose(bank[5][:, b * P:(b + 1) * P], probs_c[:, u % 2, b * P:(b + 1) * P], ident)
                ins.then_inc(s_cT, 1)

            def values_c(u):
                pe.wait_ge(s_cTev, u + 1)
                if u >= 2:
                    pe.wait_ge(s_cOev, u - 1)
                o = bank[6 + u % 2]
                pT = probsT_c[:, u % 2, :]
                if u < 8:
                    h = u % 4
                    for b in range(2):
                        ins = mm(o[:, 0:P], vm_p[:, b * 512 + h * P:b * 512 + (h + 1) * P], pT[:, b * P:(b + 1) * P], start=(b == 0), stop=(b == 1))
                else:
                    for m in range(16):
                        n, h = m // 4, m % 4
                        for b in range(2):
                            ins = mm(o[:, m * 8:m * 8 + 8], vm[u - 8][:, n * 1024 + b * 512 + h * P:][:, 0:P], pT[:, b * P + m * 8:b * P + m * 8 + 8], start=(b == 0), stop=(b == 1))
                ins.then_inc(s_cO, 1)

            for it in range(12):
                if it < 10:
                    scores_c(it)
                if it >= 2:
                    values_c(it - 2)
                if 1 <= it <= 10:
                    turn_c(it - 1)
            pe.wait_ge(s_cOev, 10)
            for f in range(KT):
                c = C_CO + f // 4
                chunk_wait(pe, c)
                if f >= 2:
                    pe.wait_ge(s_ev, at + f - 1)
                for k in range(4):
                    w = WR[:, (c % 4) * D + (f % 4) * 512 + k * P:][:, 0:P]
                    ins = mm(bank[f % 2][:, 0:NT], w, oc[:, k, :], start=(k == 0), stop=(k == 3))
                ins.then_inc(s_used, 1)
            at += KT
            norm("ffn", NT)
            pe.wait_ge(s_h, 80)
            stream_tiles(HT, at, C_PQ)
            at += KT
            for t in range(3):
                m = P if t < 2 else NS_TOK
                if t:
                    pe.wait_ge(s_ht, t)
                for k in range(KT):
                    ins = nc.tensor.transpose(big[0:m, k * P:(k + 1) * P], XT[:, k * NT + t * P:k * NT + t * P + m], ident)
                ins.then_inc(s_xt, 1)
            pe.wait_ge(s_ev, at)
            for t in range(3):
                if t:
                    pe.wait_ge(s_scev, t)
                for x in range(2 * PH):
                    ins = mm(bank[x // 4][:, (x % 4) * P:(x % 4 + 1) * P], qp[:, x, t * P:(t + 1) * P], sub_keys[:, (x % 2) * NKEY:(x % 2 + 1) * NKEY])
                ins.then_inc(s_sc, 1)
            pe.sem_inc(s_vmm, RING)
            for t in range(3):
                m = P if t < 2 else NS_TOK
                n = SLOTS if t < 2 else SLOTS // 2
                pe.wait_ge(*((s_y, t) if t else (s_ht, 3)))
                for k in range(KT):
                    mm(big[0:m, k * P:(k + 1) * P], XT[:, k * NT + t * P:k * NT + t * P + m], ident, start=(k % 4 == 0), stop=False)
                with pe.Fori(0, n // RING) as i:
                    for r in range(RING):
                        pe.wait_ge(s_vg[r], i * 16 + 16 * (t * SLOTS // RING + 1))
                        pe.wait_ge(s_dg, i * RING + (t * SLOTS + r + 1))
                        for q in range(4):
                            ins = mm(big[0:m, q * 512:(q + 1) * 512], diag[r][:, 0:m], v_ring[r][:, q * 512:(q + 1) * 512], start=False, stop=False)
                        ins.then_inc(s_vmm, 1)


def bucket(dist):
    dist = np.maximum(np.asarray(dist), 0)
    ratio = np.log(np.maximum(dist, 1) / 16) / math.log(2048 / 16)
    large = np.minimum(16 + (ratio * 16).astype(np.int32), 31)
    return np.where(dist < 16, dist, large).astype(np.int32)


def one_hot(dist, mixer, masked=None):
    dist = np.asarray(dist)
    out = np.zeros((32,) + dist.shape, np.float32)
    b = bucket(dist)
    assert b.max() < 30
    np.put_along_axis(out, b[None], 1.0, axis=0)
    held_a = (dist <= 128).astype(int) + ((dist % 4 == 0) & (dist <= 512)) + (dist % 16 == 0)
    for row, held in ((30, held_a), (31, (dist <= 128).astype(int))):
        if mixer in (row, None):
            seen = (dist >= 0) & (held > 0)
            if masked is not None:
                seen &= ~masked
            out[row] = np.where(seen, np.log(np.maximum(held, 1)), NEG)
    return out


def kernel(**inputs):
    import concourse.bacc as bacc
    from concourse.bass_utils import run_bass_kernel_spmd

    x = {k: np.asarray(v) for k, v in inputs.items()}
    f32 = np.float32

    def tiles(a):
        return a.T.reshape(-1, P, a.shape[0]).transpose(1, 0, 2).reshape(P, -1)

    pair = np.arange(1024).reshape(2, 8, 64).transpose(1, 0, 2).ravel()
    at = np.arange(512).reshape(32, 2, 8)
    key_order = np.concatenate([at[:, 1].ravel(), at[:, 0].ravel(), np.arange(512, PAST)])

    def chunks(w):
        return w.reshape(-1, P, w.shape[1] // P, P).transpose(2, 1, 0, 3).reshape(w.shape[1] // P, P, -1)

    w_in = x["w_in"][0]
    a = 1024
    w_in = np.concatenate([w_in[:, :a][:, pair], w_in[:, a:2 * a][:, pair], w_in[:, 3 * a:4 * a][:, pair],
                           w_in[:, 4 * a:4 * a + P], w_in[:, 2 * a:3 * a], w_in[:, 4 * a + P:]], axis=1)
    rows = np.concatenate([pair, a + pair])
    w_ckv = x["w_ckv"][0]
    wall = np.concatenate([
        chunks(w_ckv[:, :512]),
        w_ckv[:, 512:].reshape(4, 4, P, 512).transpose(0, 2, 1, 3).reshape(4, P, D),
        chunks(w_in), chunks(x["w_out"][0][rows]), chunks(x["w_cq"][0]),
        chunks(x["w_co"][0]).reshape(4, 4, P, 512).transpose(0, 2, 1, 3).reshape(4, P, D),
        chunks(x["w_pq"][0])])

    def gain(g):
        return g.reshape(KT, P).T

    gains = [gain(x["ln_mix"][0]), gain(x["ln_mem"][0]), gain(x["ln_cross"][0]), gain(x["ln_ffn"][0]),
             gain(np.concatenate([x["ln_a_out"][0], x["ln_b_out"][0]])[rows])]
    sinks = x["b_sinks"][0]
    consts = np.concatenate([
        np.eye(P, dtype=f32), np.ones((P, P), f32), *gains, np.broadcast_to(sinks, (P, HEADS)),
        np.repeat(sinks, QPR)[:, None], np.broadcast_to(np.arange(PK, dtype=f32), (P, PK)),
        (np.arange(P)[:, None] % 64 == np.arange(64)).astype(f32), x["sub_keys_1"][0].T, x["sub_keys_2"][0].T], axis=1)

    rel = x["rel_bias"]
    rb = np.zeros((4, 32, 4, 32), f32)
    for g in range(4):
        rb[g, :30, g] = rel[:30]
        rb[g, 30, g, :16] = 1
        rb[g, 31, g, 16:] = 1
    j = np.arange(380)
    oh_p = np.stack([one_hot(j - 124 - g, None) for g in range(4)])
    rb_s = np.zeros((4, 32, 2, 2, HEADS, QPR), f32)
    oh_sa, oh_sb = np.zeros((4, 32, 2, USED + WIN), f32), np.zeros((4, 32, 2, P + WIN), f32)
    new = np.arange(WIN) - 7 * QPR
    for t in range(2):
        for g in range(4):
            q = 4 * t + g
            rb_s[g, :30, :, t, :, q] = rel[:30].reshape(30, 2, HEADS)
            rb_s[g, 30, 0, t, :, q] = 1
            rb_s[g, 31, 1, t, :, q] = 1
            own = (new < 0) | (new >= QPR)
            oh_sa[g, :, t] = np.concatenate([one_hot(PAST + q - key_order[FIRST:], 30), one_hot(q - new, 30, own)], axis=1)
            oh_sb[g, :, t] = np.concatenate([one_hot(P + q - np.arange(P), 31), one_hot(q - new, 31, own)], axis=1)
    tables = np.concatenate([m.reshape(P, -1) for m in (rb, oh_p, rb_s, oh_sa, oh_sb)], axis=1)
    head_mask = (np.arange(P)[:, None] // QPR % 8 == np.arange(512) // 64).astype(f32)

    ka = x["cache_a_k"][0][:, key_order].reshape(REQ, PAST, 1024)[:, :, pair]
    ka = np.ascontiguousarray(ka.transpose(0, 2, 1)).reshape(REQ, 8, P, PAST)
    va = np.ascontiguousarray(x["cache_a_v"][0].reshape(REQ, PAST, 1024)[:, key_order])
    tokens = np.concatenate([x["x_prompt"][0], x["x_sample"].reshape(NS_TOK, D)])
    arrays = {
        "xT": tiles(tokens), "memT": tiles(x["mem_prompt"][0]), "consts": consts, "tables": tables,
        "head_mask": head_mask, "wall": wall, "ffn_row": x["ln_ffn"][0], "fin_row": x["ln_final"],
        "kaT": ka, "va": va,
        "kbT": x["cache_b_k"][0].reshape(REQ, P, P).transpose(2, 0, 1).reshape(P, -1),
        "vb": x["cache_b_v"][0].reshape(REQ, P, P).transpose(1, 0, 2).reshape(P, -1),
        "kmT": x["cache_mem_k"][0].transpose(0, 3, 2, 1).reshape(REQ, P, 1024),
        "vm": x["cache_mem_v"][0].reshape(REQ, 2, P, 512).transpose(0, 2, 1, 3).reshape(REQ, P, 1024),
        "expert_u": x["expert_u"][0], "expert_v": x["expert_v"][0],
    }
    arrays = {k: np.ascontiguousarray(v) for k, v in arrays.items()}
    outs = {
        "y": (NT, D), "ka_out": (32, 256, 1024), "va_out": (32, 256, 1024), "kaT_new": (P, 8 * NT), "kbT_new": (P, NT),
        "v_new": (P, 2 * VW), "v_new_s": (NS_TOK, VW), "kb_out": (P, REQ * P), "vb_out": (P, REQ * P),
        "mk_out": (P, 1024), "mv_out": (P, 1024),
    }
    nc = bacc.Bacc("TRN2", target_bir_lowering=False, num_devices=1)
    d = {k: nc.dram_tensor(k, v.shape, mybir.dt.from_np(v.dtype), kind="ExternalInput").ap() for k, v in arrays.items()}
    d |= {k: nc.dram_tensor(k, s, F32, kind="ExternalOutput").ap() for k, s in outs.items()}
    d["ka_flat"] = d["kaT"].rearrange("n j p u -> (n j p) u").rearrange("(c r) u -> c r u", c=32)
    d["va_flat"] = d["va"].rearrange("n t w -> (n t) w").rearrange("(c r) u -> c r u", c=32)
    build(nc, d)
    o = run_bass_kernel_spmd(nc, [arrays], core_ids=[0]).results[0]

    unpair = np.argsort(pair)
    y = o["y"]
    k_new = o["kaT_new"].reshape(P, 8, NT).transpose(2, 1, 0).reshape(NT, 1024)[:, unpair].reshape(NT, HEADS, DH)
    kb_new = o["kbT_new"].T.reshape(NT, 2, DH)
    v_new = np.concatenate([o["v_new"].reshape(P, 2, VW).transpose(1, 0, 2).reshape(NP_TOK, VW), o["v_new_s"]])
    va_new, vb_new = v_new[:, :1024].reshape(NT, HEADS, DH), v_new[:, 1024:].reshape(NT, 2, DH)
    back = np.argsort(key_order)
    ka_old = o["ka_out"].reshape(REQ, 1024, PAST).transpose(0, 2, 1)[:, back][:, :, unpair].reshape(REQ, PAST, HEADS, DH)
    va_old = o["va_out"].reshape(REQ, PAST, HEADS, DH)[:, back]
    kb_old = o["kb_out"].reshape(P, REQ, P).transpose(1, 2, 0).reshape(REQ, P, 2, DH)
    vb_old = o["vb_out"].reshape(P, REQ, P).transpose(1, 0, 2).reshape(REQ, P, 2, DH)

    def sampled(old, new, drop):
        return np.concatenate([old[:, drop:], new[NP_TOK:].reshape(REQ, QPR, *new.shape[1:])], axis=1)[None]

    mk = o["mk_out"].reshape(P, MEM_HEADS, MEM).transpose(2, 1, 0)[None, None]
    mv = o["mv_out"].reshape(P, 2, MEM_HEADS, MEM_DH).transpose(1, 0, 2, 3).reshape(MEM, MEM_HEADS, MEM_DH)[None, None]
    return tuple(np.ascontiguousarray(r) for r in (
        y[None, :NP_TOK], y[NP_TOK:].reshape(REQ, QPR, D),
        k_new[None, None, :NP_TOK], va_new[None, None, :NP_TOK], kb_new[None, None, NP_TOK - P:NP_TOK], vb_new[None, None, NP_TOK - P:NP_TOK],
        mk, mv,
        sampled(ka_old, k_new, 0), sampled(va_old, va_new, 0), sampled(kb_old, kb_new, QPR), sampled(vb_old, vb_new, QPR)))
```

```python
import math
from contextlib import ExitStack

import numpy as np
import concourse.bass as bass
from concourse import mybir

F32 = mybir.dt.float32
U32 = mybir.dt.uint32
ALU = mybir.AluOpType
ACT = mybir.ActivationFunctionType
AX_X = mybir.AxisListType.X

P = 128
D = 2048
KT = D // P
NP_TOK, NS_TOK = 256, 64
NT = NP_TOK + NS_TOK
REQ, QPR = 8, 8
HEADS, DH = 16, 64
SCALE = DH ** -0.5
PAST = 1024
MEM, MEM_HEADS, MEM_DH = 256, 4, 128
MEM_SCALE = MEM_DH ** -0.5
EPS = 1e-6
NEG = -1e30
T_QA, T_KA, T_QB, T_KB, T_VA, T_VB, T_IN = 0, 8, 16, 24, 25, 33, 34
VW = 9 * P
USED = 768
FIRST = 256
NEWK = NS_TOK
SW = NEWK + USED
WIN = 15 * QPR
C_MEM, C_IN, C_OUT, C_CQ, C_CO, C_PQ, C_END = 0, 8, 42, 58, 62, 66, 82
WR_N = 4
PH, PK, NKEY = 8, 16, 128
SLOTS = PH * PK
W_IN, W_OUT, W_CQ, W_CO, W_PQ, W_END = 8, 42, 58, 62, 78, 94
RING = 4


def build(nc, d):
    with ExitStack() as ctx:
        def sem(name):
            return ctx.enter_context(nc.semaphore(name))

        def region(name, words):
            return ctx.enter_context(nc.sbuf_tensor(name, [P, words], F32))

        CST = region("CST", 776)
        XT = region("XT", KT * NT)
        WR = region("WR", WR_N * D)
        HT = region("HT", KT * NT)
        QK = region("QK", T_IN * NT)
        VO = region("VO", 3 * VW + KT * NT)
        KV = region("KV", 8 * SW + 6 * 1024)
        VB = region("VB", REQ * P)

        cst_at = [0]

        def const(n):
            cst_at[0] += n
            return CST[:, cst_at[0] - n:cst_at[0]]

        ident, ones = const(P), const(P)
        gains = const(5 * KT)
        G_MIX, G_MEM, G_CROSS, G_FFN, G_AB = (gains[:, i * KT:(i + 1) * KT] for i in range(5))
        sink_prompt, sink_sample = const(HEADS), const(1)
        iota16 = const(PK)
        pair_sel = const(64)
        sub_keys = const(2 * NKEY)
        n_host_const = cst_at[0]
        eps = const(1)
        stat = const(80)

        mem_x = QK[:, 0:KT * MEM]
        mem_kT = KV[:, 8 * SW:8 * SW + 1024]
        mem_v = KV[:, 8 * SW + 1024:8 * SW + 2048]
        VT = VO[:, 0:3 * VW].rearrange("p (t w) -> p t w", t=3)
        OT = VO[:, 3 * VW:3 * VW + KT * NT]
        sq = VO[:, 0:4 * NT]
        acc = [VO[:, 4 * NT:5 * NT], VO[:, 5 * NT:6 * NT]]
        rs = VO[:, 8 * NT:9 * NT]
        rms = VO[:, 9 * NT:10 * NT]

        bias_p = WR[:, 0:32 * 256].rearrange("p (h c) -> p h c", h=32)
        tab = OT
        n_tab = 128 + 380 + 4 * 128 + 2 * (USED + WIN + P + WIN)
        rb_p, oh_p = tab[:, 0:128], tab[:, 128:508]
        rb_s = tab[:, 508:1020].rearrange("p (g t c) -> p g t c", g=2, t=2)
        oh_sa = tab[:, 1020:1020 + 2 * (USED + WIN)].rearrange("p (t u) -> p t u", t=2)
        oh_sb = tab[:, 1020 + 2 * (USED + WIN):n_tab].rearrange("p (t u) -> p t u", t=2)
        VTF = QK[:, T_VA * NT:T_IN * NT]
        probs_p = VTF[:, 0:1536].rearrange("p (b s c) -> p b s c", b=2, s=2)
        probsT_p = VTF[:, 1536:2304].rearrange("p (s c) -> p s c", s=2)
        q_apart = VTF[:, 2304:2816].rearrange("p (s c) -> p s c", s=2)
        bias_sa, bias_sb = HT[:, 0:USED + WIN], HT[:, 888:888 + P + WIN]
        head_mask = HT[:, 1136:1648]
        qpad_a = [HT[:, 1648 + i * 1088:2736 + i * 1088] for i in range(2)]
        qpad_b = [HT[:, 3824 + i * 128:3952 + i * 128] for i in range(2)]
        kbT = HT[:, 4080:5104].rearrange("p (n u) -> p n u", n=REQ)
        vb = VB[:, :].rearrange("p (n w) -> p n w", n=REQ)
        kr = [KV[:, j * SW:(j + 1) * SW] for j in range(8)]
        vr = [KV[:, 8 * SW + k * 1024:8 * SW + (k + 1) * 1024] for k in range(6)]
        s_a = VTF[:, 0:SW]
        pT_a = VTF[:, SW:SW + 896]
        s_b = VTF[:, 1728:1728 + 192]
        pT_b = VTF[:, 1920:1920 + 256]
        o_masked = VTF[:, 2176:2688]
        o_pair = VTF[:, 2688:2816]
        km = [KV[:, 0:4096], QK[:, 0:4096]]
        vm = [KV[:, 4096:8192], QK[:, 4096:8192]]
        km_p = KV[:, 8192:9216]
        vm_p = KV[:, 9216:10240]
        qc = QK[:, 8192:8192 + 4 * NT].rearrange("p (h t) -> p h t", h=4)
        oc = QK[:, 9472:9472 + 4 * NT].rearrange("p (h t) -> p h t", h=4)
        probs_c = VO[:, 0:512].rearrange("p (b c) -> p b c", b=2)
        probsT_c = VO[:, 512:1024].rearrange("p (b c) -> p b c", b=2)
        qpad_c = VO[:, 1024:1024 + 2176]
        qp = QK[:, 0:KT * 384].rearrange("p (f t) -> p f t", f=KT)
        sc = QK[:, 6144:8192]
        tk = QK[:, 8192:10880]
        top_v = tk[:, 0:256].rearrange("p (h z k) -> p h z k", h=PH, z=2)
        top_i = tk[:, 256:512].bitcast(U32).rearrange("p (h z k) -> p h z k", h=PH, z=2)
        top_f = tk[:, 512:768].rearrange("p (h z k) -> p h z k", h=PH, z=2)
        best = tk[:, 768:896].rearrange("p (h k) -> p h k", h=PH)
        pos = tk[:, 896:1024].bitcast(U32).rearrange("p (h k) -> p h k", h=PH)
        pos_i = tk[:, 1024:1280].bitcast(U32)
        pos_f = tk[:, 1280:1536]
        exp_f = tk[:, 1536:1792]
        eidx_f = tk[:, 1792:1920]
        gexp = [g.rearrange("p (h k) -> p h k", h=PH) for g in (tk[:, 1920:2048], VB[:, 768:896], VB[:, 896:1024])]
        eidx = tk[:, 2048:2432].bitcast(U32).rearrange("p (t s) -> p t s", t=3)
        gate = VB[:, 0:384].rearrange("p (t s) -> p t s", t=3)
        dots = VB[:, 384:768].rearrange("p (t s) -> p t s", t=3)
        pair_gate, pair_idx = tk[:, 2432:2496], tk[:, 2496:2560].bitcast(U32)
        h_tok = [VO[:, t * D:(t + 1) * D] for t in range(3)]
        g_row = VO[:, 3 * D:4 * D]
        u_ring = [KV[:, r * D:(r + 1) * D] for r in range(RING)]
        v_ring = [WR[:, r * D:(r + 1) * D] for r in range(RING)]
        diag = [HT[:, r * P:(r + 1) * P] for r in range(RING)]

        bank = [ctx.enter_context(nc.psum_tensor(f"bank{i}", [P, 512], F32))[:, :] for i in range(4)]
        big = ctx.enter_context(nc.psum_tensor("big", [P, 2048], F32))[:, :]
        bank += [big[:, i * 512:(i + 1) * 512] for i in range(4)]

        s_const, s_memx, s_x, s_tab = sem("consts_in"), sem("mem_in"), sem("x_in"), sem("tables_in")
        s_mask, s_kb, s_vb = sem("mask_in"), sem("kb_in"), sem("vb_in")
        s_w = [sem(f"chunk_in{i}") for i in range(WR_N)]
        s_used = sem("chunk_used")
        s_eps = sem("eps_set")
        s_sq, s_sqadd, s_ss = sem("squares"), sem("squares_added"), sem("square_sums")
        s_rms, s_rs, s_h = sem("rms"), sem("inv_rms"), sem("normed")
        s_ev = sem("evacuated")
        s_memout, s_memev = sem("mem_out"), sem("mem_kept")
        s_bias, s_biasev = sem("bias_ready"), sem("bias_kept")
        s_vt, s_vtev = sem("values_turned"), sem("values_kept")
        s_qz, s_qapart, s_padz = sem("q_zero"), sem("q_apart"), sem("rows_zero")
        s_S, s_max, s_exp, s_nrm = sem("p_scores"), sem("p_max"), sem("p_exp"), sem("p_normed")
        s_T, s_Tev, s_O, s_Oev = sem("p_turned"), sem("p_turned_kept"), sem("p_out"), sem("p_out_kept")
        s_kr = [sem(f"keys_in{j}") for j in range(8)]
        s_vr = [sem(f"values_in{j}") for j in range(6)]
        s_krused, s_vrused = sem("keys_used"), sem("values_used")
        s_newk = sem("new_keys")
        s_zero, s_qpad = sem("pads_zero"), sem("pads_filled")
        s_sS, s_smax, s_sexp, s_srd = sem("s_scores"), sem("s_max"), sem("s_exp"), sem("s_recip")
        s_sT, s_sTev, s_sO, s_sOev = sem("s_turned"), sem("s_turned_kept"), sem("s_out"), sem("s_pair")
        s_sP, s_sPev = sem("s_pair_turned"), sem("s_kept")
        s_km = [sem("mem_cache_in0"), sem("mem_cache_in1")]
        s_cS, s_cmax, s_cexp, s_cnrm = sem("c_scores"), sem("c_max"), sem("c_exp"), sem("c_normed")
        s_cT, s_cTev, s_cO, s_cOev = sem("c_turned"), sem("c_turned_kept"), sem("c_out"), sem("c_kept")
        s_cpad = sem("c_pads")
        s_xt, s_xsq, s_xrms, s_ht = sem("x_turned"), sem("x_sq"), sem("x_rms"), sem("h_tok")
        s_grow, s_dup = sem("gain_row_in"), sem("h_dup")
        s_sc, s_scev = sem("k_scores"), sem("k_scores_kept")
        s_dv, s_gx, s_gxe, s_idx = sem("dve_chain"), sem("gate_diff"), sem("gate_exp"), sem("experts_chosen")
        s_ug = [sem(f"u_in{r}") for r in range(RING)]
        s_vg = [sem(f"v_in{r}") for r in range(RING)]
        s_udot, s_gelu, s_coef, s_dg, s_vmm = sem("u_dots"), sem("gelu"), sem("coefs"), sem("diags"), sem("v_added")
        s_res = sem("residual_in_acc")
        s_fsq, s_frms, s_y = sem("y_sq"), sem("y_rms"), sem("y_ready")
        s_ac = sem("act_chain")
        s_attout = sem("attention_outputs")
        s_copy, s_out = sem("cache_copied"), sem("outputs")
        def chunk_wait(eng, c):
            eng.wait_ge(s_w[c % WR_N], 16 * (c // WR_N + 1))

        block = ctx.enter_context(nc.Block())

        N_NORM = {"mem": 0, "mix": 1, "group": 2, "cross": 3, "ffn": 4}
        N_SUM = {"mem": 0, "mix": 1, "group": 2, "cross": 4, "ffn": 5}

        @block.sync
        def _(sp):
            sp.dma_start(mem_x, d["memT"]).then_inc(s_memx, 16)
            sp.dma_start(CST[:, 0:n_host_const], d["consts"]).then_inc(s_const, 16)
            for c in range(WR_N):
                sp.dma_start(WR[:, c * D:(c + 1) * D], d["wall"][c]).then_inc(s_w[c], 16)
            sp.dma_start(XT[:, :], d["xT"]).then_inc(s_x, 16)
            sp.dma_start(tab[:, 0:n_tab], d["tables"]).then_inc(s_tab, 16)
            for c in range(WR_N, C_IN):
                sp.wait_ge(s_used, c - WR_N + 1)
                sp.dma_start(WR[:, (c % WR_N) * D:(c % WR_N + 1) * D], d["wall"][c]).then_inc(s_w[c % WR_N], 16)
            with sp.Fori(0, 8) as i:
                for r in range(WR_N):
                    sp.wait_ge(s_used, i * WR_N + (C_IN + r - WR_N + 1))
                    sp.dma_start(WR[:, r * D:(r + 1) * D], d["wall"][bass.ds(i * WR_N + (C_IN + r), 1)].rearrange("o p w -> (o p) w")).then_inc(s_w[r], 16)
                    for name in ("ka", "va"):
                        src = d[name + "_flat"][bass.ds(i * WR_N + r, 1)].rearrange("o p w -> (o p) w")
                        dst = d[name + "_out"][bass.ds(i * WR_N + r, 1)].rearrange("o p w -> (o p) w")
                        sp.dma_start(dst, src).then_inc(s_copy, 16)
            for c in (C_OUT - 2, C_OUT - 1):
                sp.wait_ge(s_used, c - WR_N + 1)
                sp.dma_start(WR[:, (c % WR_N) * D:(c % WR_N + 1) * D], d["wall"][c]).then_inc(s_w[c % WR_N], 16)
            sp.wait_ge(s_ev, T_IN)
            sp.dma_start(d["kaT_new"], QK[:, T_KA * NT:T_QB * NT]).then_inc(s_attout, 16)
            sp.dma_start(d["kbT_new"], QK[:, T_KB * NT:T_VA * NT]).then_inc(s_attout, 16)
            sp.wait_ge(s_vtev, 9)
            sp.dma_start(d["v_new"], VO[:, 0:2 * VW]).then_inc(s_attout, 16)
            sp.dma_start(d["v_new_s"], VO[0:NS_TOK, 2 * VW:3 * VW]).then_inc(s_attout, 16)
            sp.wait_ge(s_kb, 16)
            sp.dma_start(d["kb_out"], HT[:, 4080:5104]).then_inc(s_attout, 16)
            sp.wait_ge(s_vb, 16)
            sp.dma_start(d["vb_out"], VB[:, :]).then_inc(s_attout, 16)
            sp.wait_ge(s_max, HEADS)
            with sp.Fori(0, (C_PQ - C_OUT) // WR_N) as i:
                for r in range(WR_N):
                    slot = (C_OUT + r) % WR_N
                    sp.wait_ge(s_used, i * WR_N + (C_OUT + r - WR_N + 1))
                    sp.dma_start(WR[:, slot * D:(slot + 1) * D], d["wall"][bass.ds(i * WR_N + (C_OUT + r), 1)].rearrange("o p w -> (o p) w")).then_inc(s_w[slot], 16)
            for c in range(C_PQ, C_PQ + WR_N):
                sp.wait_ge(s_used, W_CO + 4 * (c - C_PQ + 1))
                sp.dma_start(WR[:, (c % WR_N) * D:(c % WR_N + 1) * D], d["wall"][c]).then_inc(s_w[c % WR_N], 16)
            with sp.Fori(0, (C_END - C_PQ) // WR_N - 1) as i:
                for r in range(WR_N):
                    slot = (C_PQ + r) % WR_N
                    sp.wait_ge(s_used, i * WR_N + (W_PQ + r + 1))
                    sp.dma_start(WR[:, slot * D:(slot + 1) * D], d["wall"][bass.ds(i * WR_N + (C_PQ + WR_N + r), 1)].rearrange("o p w -> (o p) w")).then_inc(s_w[slot], 16)
            sp.wait_ge(s_cOev, 10)
            sp.wait_ge(s_h, 16 * 5)
            sp.dma_start(g_row, d["ffn_row"].partition_broadcast(P)).then_inc(s_grow, 16)
            sp.wait_ge(s_ht, 3)
            sp.dma_start(h_tok[2][64:128, :], h_tok[2][0:64, :]).then_inc(s_dup, 16)
            sp.dma_start(g_row, d["fin_row"].partition_broadcast(P)).then_inc(s_grow, 16)
            for t in range(3):
                sp.wait_ge(s_y, t + 1)
                n = P if t < 2 else NS_TOK
                sp.dma_start(d["y"][t * P:t * P + n, :], h_tok[t][0:n, :]).then_inc(s_out, 16)
            sp.wait_ge(s_copy, 2 * 32 * 16)
            sp.wait_ge(s_attout, 6 * 16)
            sp.wait_ge(s_memout, 2 * 16)
            sp.wait_ge(s_out, 3 * 16)

        @block.gpsimd
        def _(pool):
            nc.gpsimd.memset(eps, EPS).then_inc(s_eps, 1)
            pool.dma_start(VB[:, :], d["vb"]).then_inc(s_vb, 16)
            pool.wait_ge(s_memout, 32)
            for k in range(6):
                pool.dma_start(vr[k], d["va"][0, FIRST + k * P:FIRST + (k + 1) * P, :]).then_inc(s_vr[k], 16)
            for j in range(8):
                pool.dma_start(kr[j][:, NEWK:SW], d["kaT"][0, j, :, FIRST:PAST]).then_inc(s_kr[j], 16)
            pool.wait_ge(s_used, W_OUT)
            pool.dma_start(kbT, d["kbT"].rearrange("p (n u) -> p n u", n=REQ)).then_inc(s_kb, 16)
            pool.dma_start(head_mask, d["head_mask"]).then_inc(s_mask, 16)
            for b in (qpad_a[0], qpad_a[1], qpad_b[0], qpad_b[1]):
                nc.gpsimd.memset(b, 0.0).then_inc(s_zero, 1)
            for n in range(1, REQ):
                for j in range(8):
                    pool.wait_ge(s_krused, 8 * (n - 1) + j + 1)
                    pool.dma_start(kr[j][:, NEWK:SW], d["kaT"][n, j, :, FIRST:PAST]).then_inc(s_kr[j], 16)
                for k in range(6):
                    pool.wait_ge(s_vrused, 6 * (n - 1) + k + 1)
                    pool.dma_start(vr[k], d["va"][n, FIRST + k * P:FIRST + (k + 1) * P, :]).then_inc(s_vr[k], 16)
            pool.wait_ge(s_vrused, 6 * REQ)
            for g in range(2):
                if g == 1:
                    pool.wait_ge(s_sPev, 4 * REQ)
                    pool.wait_ge(s_attout, 6 * 16)
                pool.dma_start(km[g].rearrange("p (n w) -> p n w", n=4), d["kmT"][4 * g:4 * g + 4].rearrange("n p w -> p n w")).then_inc(s_km[g], 16)
                pool.dma_start(vm[g].rearrange("p (n w) -> p n w", n=4), d["vm"][4 * g:4 * g + 4].rearrange("n p w -> p n w")).then_inc(s_km[g], 16)
                if g == 0:
                    pool.dma_start(km_p, d["mk_out"]).then_inc(s_km[g], 16)
                    pool.dma_start(vm_p, d["mv_out"]).then_inc(s_km[g], 16)
            def rows(ring, sems, table, idx, n):
                nc.gpsimd.indirect_dma_start(ring[n % RING], None, table, bass.IndirectOffsetOnAxis(idx, 0)).then_inc(sems[n % RING], 16)

            def column(n):
                return eidx[:, n // SLOTS, n % SLOTS:n % SLOTS + 1] if n < 2 * SLOTS else pair_idx[:, n - 2 * SLOTS:n - 2 * SLOTS + 1]

            def u_rows(n):
                pool.wait_ge(s_idx, min(n // SLOTS, 2) + 1)
                if n >= RING:
                    pool.wait_ge(s_udot, n - RING + 1)
                rows(u_ring, s_ug, d["expert_u"], column(n), n)

            def v_rows(n):
                if n >= RING:
                    pool.wait_ge(s_vmm, n + 1)
                rows(v_ring, s_vg, d["expert_v"], column(n), n)

            pool.wait_ge(s_cOev, 10)
            for n in range(SLOTS):
                u_rows(n)
            pool.wait_ge(s_used, W_END)
            nu, nv, n_all = SLOTS, 0, 2 * SLOTS + SLOTS // 2
            lead = 28
            while nv < n_all:
                v_rows(nv)
                nv += 1
                if nv > lead and nu < n_all:
                    u_rows(nu)
                    nu += 1
                if nv == SLOTS:
                    while nu < 2 * SLOTS:
                        u_rows(nu)
                        nu += 1

        @block.scalar
        def _(act):
            nac = [0]

            def link(ins):
                nac[0] += 1
                ins.then_inc(s_ac, 1)
                act.wait_ge(s_ac, nac[0])

            def squares(which, x, width):
                u = N_NORM[which]
                for k in range(KT):
                    if u or k >= 4:
                        act.wait_ge(s_sqadd, 16 * u + k - 3)
                    nc.scalar.activation(sq[:, (k % 4) * NT:(k % 4) * NT + width], x[:, k * width:(k + 1) * width], ACT.Square).then_inc(s_sq, 1)

            def squares_of_stream(which, at):
                u = N_NORM[which]
                for k in range(4):
                    act.wait_ge(s_ev, at + k + 1)
                    act.wait_ge(s_sqadd, 16 * u + k - 3)
                    nc.scalar.activation(sq[:, k * NT:(k + 1) * NT], XT[:, k * NT:(k + 1) * NT], ACT.Square).then_inc(s_sq, 1)
                with act.Fori(1, 4) as i:
                    for r in range(4):
                        act.wait_ge(s_ev, i * 4 + (at + r + 1))
                        act.wait_ge(s_sqadd, i * 4 + (16 * u + r - 3))
                        nc.scalar.activation(sq[:, r * NT:(r + 1) * NT], XT[:, bass.ds(i * (4 * NT) + r * NT, NT)], ACT.Square).then_inc(s_sq, 1)

            def roots(which, width, groups=1):
                before = N_SUM[which]
                for g in range(groups):
                    act.wait_ge(s_ss, before + g + 1)
                    if before + g > 0:
                        act.wait_ge(s_rs, before + g)
                    nc.scalar.activation(rms[:, 0:width], bank[2 + g][:, 0:width], ACT.Sqrt, bias=eps, scale=float(groups) / D).then_inc(s_rms, 1)

            act.wait_ge(s_eps, 1)
            act.wait_ge(s_memx, 16)
            squares("mem", mem_x, MEM)
            roots("mem", MEM)
            act.wait_ge(s_x, 16)
            squares("mix", XT, NT)
            roots("mix", NT)
            for n in range(4):
                act.wait_ge(s_used, n + 1)
                nc.scalar.activation(mem_kT[:, n * MEM:(n + 1) * MEM], bank[n % 2][:, 0:MEM], ACT.Copy).then_inc(s_memev, 1)
            for n in range(2):
                act.wait_ge(s_used, W_IN)
                nc.scalar.activation(mem_v[:, n * 512:(n + 1) * 512], bank[4 + n], ACT.Copy).then_inc(s_memev, 1)
            act.wait_ge(s_memev, 6)
            act.dma_start(d["mk_out"], mem_kT).then_inc(s_memout, 16)
            act.dma_start(d["mv_out"], mem_v).then_inc(s_memout, 16)
            for n in range(9):
                t, q = n // 3, n % 3
                w, m = (512, P) if q < 2 else (128, P)
                if t == 2:
                    m = NS_TOK
                act.wait_ge(s_vt, n + 1)
                nc.scalar.activation(VT[0:m, t, q * 512:q * 512 + w], bank[3 + n % 2][0:m, 0:w], ACT.Copy).then_inc(s_vtev, 1)
            def split_q(p):
                if p == 0:
                    act.wait_ge(s_qz, 1)
                else:
                    act.wait_ge(s_S, p)
                for s in range(2):
                    rows = slice(64 * s, 64 * s + 64)
                    q = QK[rows, ((T_QB if p >= 8 else T_QA) + p % 8) * NT:][:, 0:NP_TOK]
                    ins = nc.scalar.activation(q_apart[rows, s, :], q, ACT.Copy)
                ins.then_inc(s_qapart, 1)

            def exp_p(p):
                pb, b = probs_p[:, p % 2], 16 * (p % 2)
                act.wait_ge(s_max, p + 1)
                for s in range(2):
                    for q, (lo, hi) in enumerate(((0, 256), (256, 384))):
                        c = b + 2 * s + q
                        ins = nc.scalar.activation(pb[:, s, lo:hi], pb[:, s, lo:hi], ACT.Exp, bias=stat[:, c:c + 1], scale=1.0, accum_out=stat[:, c + 4:c + 5])
                if p >= 8:
                    for s in range(2):
                        c, h = b + 2 * s, p % 8 + 8 * s
                        ins = nc.scalar.activation(stat[:, c + 8:c + 10], stat[:, c:c + 2], ACT.Exp, bias=sink_prompt[:, h:h + 1], scale=1.0)
                ins.then_inc(s_exp, 1)

            def turned_p(p):
                for s in range(2):
                    act.wait_ge(s_T, 2 * p + s + 1)
                    if p:
                        act.wait_ge(s_O, 2 * p + s - 1)
                    nc.scalar.activation(probsT_p[:, s, :], bank[s][:, 0:384], ACT.Copy).then_inc(s_Tev, 1)

            split_q(0)
            for it in range(HEADS + 1):
                if it + 1 < HEADS:
                    split_q(it + 1)
                if it < HEADS:
                    exp_p(it)
                if it >= 1:
                    turned_p(it - 1)
            for n in range(REQ):
                b = 16 + 8 * (n % 2)
                act.wait_ge(s_smax, 2 * n + 1)
                nc.scalar.activation(s_a, s_a, ACT.Exp, bias=stat[:, b:b + 1], scale=1.0, accum_out=stat[:, b + 2:b + 3]).then_inc(s_sexp, 1)
                act.wait_ge(s_smax, 2 * n + 2)
                nc.scalar.activation(s_b, s_b, ACT.Exp, bias=stat[:, b + 1:b + 2], scale=1.0, accum_out=stat[:, b + 3:b + 4])
                nc.scalar.activation(stat[:, b + 4:b + 5], stat[:, b + 1:b + 2], ACT.Exp, bias=sink_sample, scale=1.0).then_inc(s_sexp, 1)
                act.wait_ge(s_sT, 3 * n + 1)
                nc.scalar.activation(pT_a[0:NEWK, 0:P], bank[2][0:NEWK, 0:P], ACT.Copy)
                nc.scalar.activation(pT_a[:, P:384], bank[2][:, P:384], ACT.Copy).then_inc(s_sTev, 1)
                act.wait_ge(s_sT, 3 * n + 2)
                nc.scalar.activation(pT_a[:, 384:896], bank[3][:, 0:512], ACT.Copy).then_inc(s_sTev, 1)
                act.wait_ge(s_sT, 3 * n + 3)
                nc.scalar.activation(pT_b[:, 0:P], bank[7][:, 256:384], ACT.Copy)
                nc.scalar.activation(pT_b[0:NEWK, P:2 * P], bank[7][0:NEWK, 384:512], ACT.Copy).then_inc(s_sTev, 1)
            act.wait_ge(s_attout, 6 * 16)
            act.wait_ge(s_sPev, 4 * REQ)
            squares("group", OT, NT)
            roots("group", NT, 2)
            squares_of_stream("cross", T_IN)
            roots("cross", NT)
            def exp_c(u):
                act.wait_ge(s_cmax, u + 1)
                if u >= 2:
                    act.wait_ge(s_cT, u - 1)
                nb = u % 2
                nc.scalar.activation(probs_c[:, nb, :], bank[3 + nb][:, 0:256], ACT.Exp, bias=stat[:, 64 + nb:65 + nb], scale=MEM_SCALE, accum_out=stat[:, 66 + nb:67 + nb]).then_inc(s_cexp, 1)

            def turned_c(u):
                act.wait_ge(s_cT, u + 1)
                if u >= 2:
                    act.wait_ge(s_cO, u - 1)
                nc.scalar.activation(probsT_c[:, u % 2, :], bank[5][:, 0:256], ACT.Copy).then_inc(s_cTev, 1)

            for it in range(11):
                if it < 10:
                    exp_c(it)
                if it >= 1:
                    turned_c(it - 1)
            squares_of_stream("ffn", T_IN + KT + 4)
            roots("ffn", NT)
            for t in range(3):
                m = P if t < 2 else NS_TOK
                act.wait_ge(s_xt, t + 1)
                if t == 0:
                    act.wait_ge(s_h, 80)
                link(nc.scalar.activation(h_tok[t][0:m, :], big[0:m, :], ACT.Square, accum_out=stat[0:m, 30 + t:31 + t]))
                nc.scalar.activation(stat[0:m, 33 + t:34 + t], stat[0:m, 30 + t:31 + t], ACT.Sqrt, bias=eps[0:m, :], scale=1.0 / D).then_inc(s_xrms, 1)

            def gate_exp(t):
                act.wait_ge(s_gx, t + 1)
                nc.scalar.activation(gexp[t], gexp[t], ACT.Exp).then_inc(s_gxe, 1)

            def gelu(t):
                n = SLOTS if t < 2 else SLOTS // 2
                act.wait_ge(s_udot, min((t + 1) * SLOTS, 2 * SLOTS + SLOTS // 2))
                nc.scalar.activation(dots[:, t, 0:n], dots[:, t, 0:n], ACT.Gelu).then_inc(s_gelu, 1)

            def diagonals(t):
                n = SLOTS if t < 2 else SLOTS // 2
                src, w = (ident, P) if t < 2 else (pair_sel, 64)
                act.wait_ge(s_coef, t + 1)
                with act.Fori(0, n // RING) as i:
                    for r in range(RING):
                        act.wait_ge(s_vmm, i * RING + (t * SLOTS + r + 1))
                        nc.scalar.activation(diag[r][:, 0:w], src, ACT.Copy, scale=dots[:, t, bass.ds(i * RING + r, 1)]).then_inc(s_dg, 1)

            def finish(t):
                m = P if t < 2 else NS_TOK
                act.wait_ge(s_vmm, min((t + 1) * SLOTS, 2 * SLOTS + SLOTS // 2) + RING)
                link(nc.scalar.activation(h_tok[t][0:m, :], big[0:m, :], ACT.Square, accum_out=stat[0:m, 40 + t:41 + t]))
                nc.scalar.activation(stat[0:m, 43 + t:44 + t], stat[0:m, 40 + t:41 + t], ACT.Sqrt, bias=eps[0:m, :], scale=1.0 / D).then_inc(s_frms, 1)

            for t in range(3):
                gate_exp(t)
                if t:
                    finish(t - 1)
                gelu(t)
                diagonals(t)
            finish(2)

        @block.vector
        def _(dve):
            ndv = [0]

            def link(ins):
                ndv[0] += 1
                ins.then_inc(s_dv, 1)
                dve.wait_ge(s_dv, ndv[0])

            def add_square(u, k, width, per=KT):
                a, q = acc[k // per], sq[:, (k % 4) * NT:(k % 4) * NT + width]
                dve.wait_ge(s_sq, 16 * u + k + 1)
                if k % per == 0:
                    nc.vector.tensor_copy(a[:, 0:width], q).then_inc(s_sqadd, 1)
                else:
                    dve.wait_ge(s_sqadd, 16 * u + k)
                    nc.vector.tensor_tensor(a[:, 0:width], a[:, 0:width], q, ALU.add).then_inc(s_sqadd, 1)

            def norm(which, x, gain, out, width, groups=1, added=False):
                base = N_SUM[which]
                u = N_NORM[which]
                if not added:
                    for k in range(KT):
                        add_square(u, k, width, KT // groups)
                per = KT // groups
                for g in range(groups):
                    dve.wait_ge(s_rms, base + g + 1)
                    nc.vector.reciprocal(rs[:, 0:width], rms[:, 0:width]).then_inc(s_rs, 1)
                    dve.wait_ge(s_rs, base + g + 1)
                    for k in range(g * per, (g + 1) * per):
                        nc.vector.scalar_tensor_tensor(out=out[:, k * width:(k + 1) * width], in0=x[:, k * width:(k + 1) * width],
                                                       scalar=gain[:, k:k + 1], in1=rs[:, 0:width], op0=ALU.mult, op1=ALU.mult).then_inc(s_h, 1)
                    dve.wait_ge(s_h, 16 * u + (g + 1) * per)

            dve.wait_ge(s_const, 16)
            norm("mem", mem_x, G_MEM, mem_x, MEM)
            norm("mix", XT, G_MIX, HT, NT)
            dve.wait_ge(s_used, W_IN)
            with dve.Fori(0, 8) as i:
                for r in range(4):
                    dve.wait_ge(s_used, i * 4 + (W_IN + r + 1))
                    nc.vector.tensor_scalar(QK[:, bass.ds(i * (4 * NT) + r * NT, NT)], bank[r % 2][:, 0:NT], 1.0, None, ALU.mult).then_inc(s_ev, 1)
            for f in (T_IN - 2, T_IN - 1):
                dve.wait_ge(s_used, W_IN + f + 1)
                nc.vector.tensor_scalar(QK[:, f * NT:(f + 1) * NT], bank[f % 2][:, 0:NT], 1.0, None, ALU.mult).then_inc(s_ev, 1)
            dve.wait_ge(s_ev, T_IN)
            for n in range(16):
                dve.wait_ge(s_bias, n + 1)
                nc.vector.tensor_copy(bias_p[:, :, n * 16:(n + 1) * 16], bank[6 + n % 2].rearrange("p (c h) -> p h c", h=32)).then_inc(s_biasev, 1)
            dve.wait_ge(s_bias, 17)
            nc.vector.tensor_copy(bias_sa[:, 0:512], bank[6]).then_inc(s_biasev, 1)
            dve.wait_ge(s_bias, 18)
            nc.vector.tensor_copy(bias_sa[:, 512:USED + WIN], bank[7][:, 0:USED + WIN - 512]).then_inc(s_biasev, 1)
            dve.wait_ge(s_bias, 19)
            nc.vector.tensor_copy(bias_sb, bank[6][:, 0:P + WIN]).then_inc(s_biasev, 1)
            dve.wait_ge(s_vtev, 9)
            nc.vector.memset(q_apart, 0.0).then_inc(s_qz, 1)
            nc.vector.memset(VT[NS_TOK:P, 2, :], 0.0).then_inc(s_padz, 1)
            for j in range(8):
                nc.vector.tensor_copy(kr[j][:, 0:NEWK], QK[:, (T_KA + j) * NT + NP_TOK:(T_KA + j + 1) * NT]).then_inc(s_newk, 1)
            dve.wait_ge(s_biasev, 19)
            t_max = stat[:, 56:60]
            minus_sink = stat[:, 32:48]

            def mark(ins):
                ndv[0] += 1
                ins.then_inc(s_dv, 1)
                return ndv[0]

            def by_block(a):
                return a.rearrange("p (s q) -> p s q", s=2)

            def step_p(p):
                now, last = p < HEADS, p >= 1
                pb, b = probs_p[:, p % 2], 16 * (p % 2)
                pl, bl = probs_p[:, (p + 1) % 2], 16 * ((p + 1) % 2)
                if now:
                    h = 16 * (p // 8) + p % 8
                    if p >= 2:
                        dve.wait_ge(s_T, 2 * p - 2)
                    dve.wait_ge(s_S, p + 1)
                    sc_p = big[:, (p % 2) * 1024:(p % 2 + 1) * 1024].rearrange("p (s c) -> p s c", s=2)
                    m1 = mark(nc.vector.scalar_tensor_tensor(out=pb[:, :, 0:256], in0=sc_p[:, :, 0:256], scalar=SCALE, in1=bias_p[:, h:h + 9:8, :], op0=ALU.mult, op1=ALU.add))
                    m2 = mark(nc.vector.scalar_tensor_tensor(out=pb[:, :, 256:384], in0=sc_p[:, :, 256:384], scalar=SCALE, in1=bias_p[:, h:h + 9:8, 128:256], op0=ALU.mult, op1=ALU.add))
                if last:
                    dve.wait_ge(s_exp, p)
                    den, rd = stat[:, bl + 4:bl + 8], stat[:, bl + 12:bl + 16]
                    if p - 1 >= 8:
                        ma = mark(nc.vector.tensor_tensor(den, den, stat[:, bl + 8:bl + 12], ALU.add))
                if now:
                    dve.wait_ge(s_dv, m1)
                    m3 = mark(nc.vector.tensor_reduce(by_block(t_max)[:, :, 0], pb[:, :, 0:256], AX_X, ALU.max))
                if last:
                    if p - 1 >= 8:
                        dve.wait_ge(s_dv, ma)
                    mr = mark(nc.vector.reciprocal(rd, den))
                if now:
                    dve.wait_ge(s_dv, m2)
                    m4 = mark(nc.vector.tensor_reduce(by_block(t_max)[:, :, 1], pb[:, :, 256:384], AX_X, ALU.max))
                if last:
                    dve.wait_ge(s_dv, mr)
                    nc.vector.tensor_scalar(pl[:, 0, 0:256], pl[:, 0, 0:256], rd[:, 0:1], None, ALU.mult)
                    nc.vector.tensor_scalar(pl[:, 0, 256:384], pl[:, 0, 256:384], rd[:, 1:2], None, ALU.mult).then_inc(s_nrm, 1)
                if now:
                    dve.wait_ge(s_dv, m4)
                    mx = stat[:, b:b + 4]
                    if p >= 8:
                        sink = minus_sink[:, p % 8:p % 8 + 9:8].unsqueeze(2).broadcast_to([P, 2, 2])
                        nc.vector.scalar_tensor_tensor(out=by_block(mx), in0=by_block(t_max), scalar=-1.0, in1=sink, op0=ALU.mult, op1=ALU.min).then_inc(s_max, 1)
                    else:
                        nc.vector.tensor_scalar(mx, t_max, -1.0, None, ALU.mult).then_inc(s_max, 1)
                if last:
                    nc.vector.tensor_scalar(pl[:, 1, 0:256], pl[:, 1, 0:256], rd[:, 2:3], None, ALU.mult)
                    nc.vector.tensor_scalar(pl[:, 1, 256:384], pl[:, 1, 256:384], rd[:, 3:4], None, ALU.mult).then_inc(s_nrm, 1)

            def out_p(p):
                for s in range(2):
                    dve.wait_ge(s_O, 2 * p + s + 1)
                    nc.vector.tensor_copy(OT[64 * s:64 * s + 64, p * NT:p * NT + NP_TOK], bank[2 + s][0:64, 0:256]).then_inc(s_Oev, 1)

            link(nc.vector.tensor_scalar(minus_sink, sink_prompt, -1.0, None, ALU.mult))
            for it in range(HEADS + 2):
                if it <= HEADS:
                    step_p(it)
                if it >= 2:
                    out_p(it - 2)
            def pads(n):
                if n == 0:
                    dve.wait_ge(s_zero, 4)
                if n >= 2:
                    dve.wait_ge(s_sS, n - 1)
                t0 = NP_TOK + QPR * n
                src_a = QK[:, T_QA * NT:T_KA * NT].rearrange("p (j t) -> p j t", t=NT)
                src_b = QK[:, T_QB * NT:T_KB * NT].rearrange("p (j t) -> p j t", t=NT)
                for s in range(2):
                    rows = slice(64 * s, 64 * s + 64)
                    pa = qpad_a[n % 2][rows, :].rearrange("p (j c) -> p j c", c=136)[:, :, 64 * s:64 * s + QPR]
                    nc.vector.tensor_copy(pa, src_a[rows, :, t0:t0 + QPR]).then_inc(s_qpad, 1)
                    pb = qpad_b[n % 2][rows, 64 * s:64 * s + 64].rearrange("p (j q) -> p j q", q=QPR)
                    nc.vector.tensor_copy(pb, src_b[rows, :, t0:t0 + QPR]).then_inc(s_qpad, 1)

            def softmax_s(n):
                w0, b = (REQ - 1 - n) * QPR, 16 + 8 * (n % 2)
                dve.wait_ge(s_krused, 8 * n + 8)
                if n:
                    dve.wait_ge(s_sT, 3 * n - 1)
                nc.vector.scalar_tensor_tensor(out=s_a[:, 0:NEWK], in0=bank[0][:, 0:NEWK], scalar=SCALE, in1=bias_sa[:, USED + w0:USED + w0 + NEWK], op0=ALU.mult, op1=ALU.add)
                nc.vector.scalar_tensor_tensor(out=s_a[:, NEWK:320], in0=bank[0][:, NEWK:320], scalar=SCALE, in1=bias_sa[:, 0:FIRST], op0=ALU.mult, op1=ALU.add)
                link(nc.vector.scalar_tensor_tensor(out=s_a[:, 320:SW], in0=bank[1], scalar=SCALE, in1=bias_sa[:, FIRST:USED], op0=ALU.mult, op1=ALU.add))
                link(nc.vector.tensor_reduce(stat[:, 52:53], s_a, AX_X, ALU.max))
                nc.vector.tensor_scalar(stat[:, b:b + 1], stat[:, 52:53], -1.0, None, ALU.mult).then_inc(s_smax, 1)
                dve.wait_ge(s_sS, n + 1)
                if n:
                    dve.wait_ge(s_sT, 3 * n)
                nc.vector.scalar_tensor_tensor(out=s_b[:, 0:P], in0=bank[6][:, 0:P], scalar=SCALE, in1=bias_sb[:, 0:P], op0=ALU.mult, op1=ALU.add)
                link(nc.vector.scalar_tensor_tensor(out=s_b[:, P:P + NEWK], in0=bank[6][:, P:P + NEWK], scalar=SCALE, in1=bias_sb[:, P + w0:P + w0 + NEWK], op0=ALU.mult, op1=ALU.add))
                link(nc.vector.tensor_reduce(stat[:, 53:54], s_b, AX_X, ALU.max))
                nc.vector.tensor_scalar(stat[:, b + 1:b + 2], stat[:, 53:54], sink_sample, -1.0, ALU.max, ALU.mult).then_inc(s_smax, 1)

            def pair_s(n):
                b = 16 + 8 * (n % 2)
                dve.wait_ge(s_sexp, 2 * n + 2)
                link(nc.vector.tensor_tensor(stat[:, b + 3:b + 4], stat[:, b + 3:b + 4], stat[:, b + 4:b + 5], ALU.add))
                link(nc.vector.reciprocal(stat[:, b + 5:b + 7], stat[:, b + 2:b + 4]))
                dve.wait_ge(s_vrused, 6 * n + 6)
                for s in range(2):
                    rows = slice(64 * s, 64 * s + 64)
                    ins = nc.vector.scalar_tensor_tensor(out=o_masked[rows, :], in0=bank[4 + s][rows, :], scalar=stat[rows, b + 5:b + 6], in1=head_mask[rows, :], op0=ALU.mult, op1=ALU.mult)
                link(ins)
                if n:
                    dve.wait_ge(s_sP, n)
                nc.vector.tensor_reduce(o_pair[:, 0:64], o_masked.rearrange("p (h e) -> p e h", h=8), AX_X, ALU.add)
                dve.wait_ge(s_sO, n + 1)
                for s in range(2):
                    rows = slice(64 * s, 64 * s + 64)
                    ins = nc.vector.tensor_scalar(o_pair[rows, 64:128], bank[7][rows, 64 * s:64 * s + 64], stat[rows, b + 6:b + 7], None, ALU.mult)
                ins.then_inc(s_sOev, 1)

            def keep_s(n):
                dve.wait_ge(s_sP, n + 1)
                t0 = NP_TOK + QPR * n
                for m in range(2):
                    for s in range(2):
                        dst = OT[64 * s:64 * s + 64, m * 8 * NT:(m + 1) * 8 * NT].rearrange("p (j t) -> p j t", t=NT)[:, :, t0:t0 + QPR]
                        src = bank[7][64 * m:64 * m + 64, 128 + 64 * s:192 + 64 * s].rearrange("p (j q) -> p j q", q=QPR)
                        nc.vector.tensor_copy(dst, src).then_inc(s_sPev, 1)

            pads(0)
            pads(1)
            dve.wait_ge(s_mask, 16)
            dve.wait_ge(s_Oev, 2 * HEADS)
            nc.vector.memset(pT_a[NS_TOK:P, 0:P], 0.0).then_inc(s_padz, 1)
            nc.vector.memset(pT_b[NS_TOK:P, P:2 * P], 0.0).then_inc(s_padz, 1)
            softmax_s(0)
            for n in range(REQ):
                if n + 2 < REQ:
                    pads(n + 2)
                if n:
                    keep_s(n - 1)
                if n + 1 < REQ:
                    softmax_s(n + 1)
                pair_s(n)
            keep_s(REQ - 1)
            dve.wait_ge(s_sPev, 4 * REQ)
            norm("group", OT, G_AB, OT, NT, 2)

            def add_to_stream(at, u):
                for k in range(4):
                    dve.wait_ge(s_used, W_IN + at + k + 1)
                    x = XT[:, k * NT:(k + 1) * NT]
                    nc.vector.tensor_tensor(x, x, bank[k % 2][:, 0:NT], ALU.add).then_inc(s_ev, 1)
                    add_square(u, k, NT)
                with dve.Fori(1, 4) as i:
                    for r in range(4):
                        dve.wait_ge(s_used, i * 4 + (W_IN + at + r + 1))
                        x = XT[:, bass.ds(i * (4 * NT) + r * NT, NT)]
                        nc.vector.tensor_tensor(x, x, bank[r % 2][:, 0:NT], ALU.add).then_inc(s_ev, 1)
                        dve.wait_ge(s_sq, i * 4 + (16 * u + r + 1))
                        dve.wait_ge(s_sqadd, i * 4 + (16 * u + r))
                        nc.vector.tensor_tensor(acc[0], acc[0], sq[:, r * NT:(r + 1) * NT], ALU.add).then_inc(s_sqadd, 1)
                dve.wait_ge(s_ev, at + KT)

            add_to_stream(T_IN, N_NORM["cross"])
            norm("cross", XT, G_CROSS, HT, NT, added=True)
            for f in range(4):
                dve.wait_ge(s_used, W_CQ + f + 1)
                nc.vector.tensor_copy(qc[:, f, :], bank[f % 2][:, 0:NT]).then_inc(s_ev, 1)
            link(nc.vector.memset(qpad_c, 0.0))
            dve.wait_ge(s_ev, T_IN + KT + 4)

            def pads_c(g):
                if g:
                    dve.wait_ge(s_cS, 9)
                for h in range(4):
                    dst = qpad_c.rearrange("p (n h c) -> p n h c", n=4, h=4)[:, :, h, 0:QPR]
                    src = qc[:, h, NP_TOK + 32 * g:NP_TOK + 32 * g + 32].rearrange("p (n q) -> p n q", q=QPR)
                    nc.vector.tensor_copy(dst, src).then_inc(s_cpad, 1)

            def max_c(u):
                nb = u % 2
                dve.wait_ge(s_cS, u + 1)
                if u:
                    dve.wait_ge(s_cmax, u)
                link(nc.vector.tensor_reduce(stat[:, 56:57], bank[3 + nb][:, 0:256], AX_X, ALU.max))
                nc.vector.tensor_scalar(stat[:, 64 + nb:65 + nb], stat[:, 56:57], -MEM_SCALE, None, ALU.mult).then_inc(s_cmax, 1)

            def norm_c(u):
                nb = u % 2
                dve.wait_ge(s_cexp, u + 1)
                link(nc.vector.reciprocal(stat[:, 68 + nb:69 + nb], stat[:, 66 + nb:67 + nb]))
                nc.vector.tensor_scalar(probs_c[:, nb, :], probs_c[:, nb, :], stat[:, 68 + nb:69 + nb], None, ALU.mult).then_inc(s_cnrm, 1)

            def out_c(u):
                dve.wait_ge(s_cO, u + 1)
                if u < 8:
                    h, q = u % 4, u // 4
                    nc.vector.tensor_copy(oc[:, h, q * P:(q + 1) * P], bank[6 + u % 2][:, 0:128]).then_inc(s_cOev, 1)
                else:
                    g = u - 8
                    for h in range(4):
                        src = bank[6 + u % 2][:, 0:128].rearrange("p (n h q) -> p n h q", n=4, h=4)[:, :, h, :]
                        dst = oc[:, h, NP_TOK + 32 * g:NP_TOK + 32 * g + 32].rearrange("p (n q) -> p n q", q=QPR)
                        ins = nc.vector.tensor_copy(dst, src)
                    ins.then_inc(s_cOev, 1)

            pads_c(0)
            for it in range(12):
                if it < 10:
                    max_c(it)
                if 1 <= it <= 10:
                    norm_c(it - 1)
                if it >= 2:
                    out_c(it - 2)
                if it == 8:
                    pads_c(1)
            add_to_stream(T_IN + KT + 4, N_NORM["ffn"])
            norm("ffn", XT, G_FFN, HT, NT, added=True)
            for f in range(KT):
                dve.wait_ge(s_used, W_PQ + f + 1)
                nc.vector.tensor_copy(qp[:, f, 0:NT], bank[f % 2][:, 0:NT])
                nc.vector.tensor_copy(qp[:, f, NT:384], bank[f % 2][:, NP_TOK:NT]).then_inc(s_ev, 1)
            dve.wait_ge(s_grow, 16)
            for t in range(3):
                m = P if t < 2 else NS_TOK
                dve.wait_ge(s_xrms, t + 1)
                link(nc.vector.reciprocal(stat[0:m, 36 + t:37 + t], stat[0:m, 33 + t:34 + t]))
                nc.vector.scalar_tensor_tensor(out=h_tok[t][0:m, :], in0=big[0:m, :], scalar=stat[0:m, 36 + t:37 + t], in1=g_row[0:m, :], op0=ALU.mult, op1=ALU.mult).then_inc(s_ht, 1)

            def top_k(src, values, indices, n):
                for half in range(2):
                    o = slice(8 * half, 8 * half + 8)
                    for x in range(n):
                        ins = nc.vector.max(values(x)[:, o], src(x))
                    link(ins)
                    for x in range(n):
                        ins = nc.vector.max_index(indices(x)[:, o], values(x)[:, o], src(x))
                    link(ins)
                    if half == 0:
                        for x in range(n):
                            ins = nc.vector.match_replace(src(x), values(x)[:, o], src(x), -3e38)
                        link(ins)

            def choose(t):
                dve.wait_ge(s_sc, t + 1)
                for q in range(4):
                    ins = nc.vector.tensor_copy(sc[:, q * 512:(q + 1) * 512], bank[q])
                ins.then_inc(s_scev, 1)
                dve.wait_ge(s_scev, t + 1)
                top_k(lambda x: sc[:, x * P:(x + 1) * P], lambda x: top_v[:, x // 2, x % 2, :], lambda x: top_i[:, x // 2, x % 2, :], 2 * PH)
                nc.vector.tensor_copy(top_f, top_i)
                cand = sc.rearrange("p (h i j) -> p h i j", h=PH, i=PK)
                link(nc.vector.tensor_tensor(cand, top_v[:, :, 0, :].unsqueeze(3).broadcast_to([P, PH, PK, PK]), top_v[:, :, 1, :].unsqueeze(2).broadcast_to([P, PH, PK, PK]), ALU.add))
                top_k(lambda h: sc[:, h * 256:(h + 1) * 256], lambda h: best[:, h, :], lambda h: pos[:, h, :], PH)
                nc.vector.tensor_scalar(pos_i[:, 0:SLOTS], pos.rearrange("p h k -> p (h k)"), 4, None, ALU.logical_shift_right)
                link(nc.vector.tensor_scalar(pos_i[:, SLOTS:2 * SLOTS], pos.rearrange("p h k -> p (h k)"), 15, None, ALU.bitwise_and))
                link(nc.vector.tensor_copy(pos_f, pos_i))
                nc.vector.tensor_tensor(gexp[t], best, best[:, :, 0:1].broadcast_to([P, PH, PK]), ALU.subtract).then_inc(s_gx, 1)
                oh = sc.rearrange("p (s i) -> p s i", i=PK)
                oh4 = sc.rearrange("p (h k i) -> p h k i", h=PH, k=PK)
                for z in range(2):
                    link(nc.vector.tensor_tensor(oh, pos_f[:, z * SLOTS:(z + 1) * SLOTS].unsqueeze(2).broadcast_to([P, SLOTS, PK]), iota16.unsqueeze(1).broadcast_to([P, SLOTS, PK]), ALU.is_equal))
                    link(nc.vector.tensor_tensor(oh4, oh4, top_f[:, :, z, :].unsqueeze(2).broadcast_to([P, PH, PK, PK]), ALU.mult))
                    link(nc.vector.tensor_reduce(exp_f[:, z * SLOTS:(z + 1) * SLOTS], oh, AX_X, ALU.add))
                link(nc.vector.scalar_tensor_tensor(out=eidx_f, in0=exp_f[:, 0:SLOTS], scalar=float(NKEY), in1=exp_f[:, SLOTS:2 * SLOTS], op0=ALU.mult, op1=ALU.add))
                if t < 2:
                    nc.vector.tensor_copy(eidx[:, t, :], eidx_f).then_inc(s_idx, 1)
                else:
                    link(nc.vector.tensor_copy(eidx[:, t, :], eidx_f))
                    for s in range(2):
                        rows = slice(64 * s, 64 * s + 64)
                        ins = nc.vector.tensor_copy(pair_idx[rows, :], eidx[rows, 2, 64 * s:64 * s + 64])
                    ins.then_inc(s_idx, 1)

            def weigh(t):
                dve.wait_ge(s_gxe, t + 1)
                link(nc.vector.tensor_reduce(stat[:, 60:68], gexp[t], AX_X, ALU.add))
                link(nc.vector.reciprocal(stat[:, 68:76], stat[:, 60:68]))
                link(nc.vector.tensor_tensor(gate[:, t, :].rearrange("p (h k) -> p h k", h=PH), gexp[t], stat[:, 68:76].unsqueeze(2).broadcast_to([P, PH, PK]), ALU.mult))
                if t == 2:
                    for s in range(2):
                        rows = slice(64 * s, 64 * s + 64)
                        link(nc.vector.tensor_copy(pair_gate[rows, :], gate[rows, 2, 64 * s:64 * s + 64]))

            def u_dots(t):
                n = SLOTS if t < 2 else SLOTS // 2
                if t == 2:
                    dve.wait_ge(s_dup, 16)
                with dve.Fori(0, n // RING) as i:
                    for r in range(RING):
                        dve.wait_ge(s_ug[r], i * 16 + 16 * (t * SLOTS // RING + 1))
                        nc.vector.scalar_tensor_tensor(out=u_ring[r], in0=u_ring[r], scalar=1.0, in1=h_tok[t], op0=ALU.mult, op1=ALU.mult,
                                                       accum_out=dots[:, t, bass.ds(i * RING + r, 1)]).then_inc(s_udot, 1)

            def coefs(t):
                n = SLOTS if t < 2 else SLOTS // 2
                dve.wait_ge(s_gelu, t + 1)
                g = gate[:, t, :] if t < 2 else pair_gate
                nc.vector.tensor_tensor(dots[:, t, 0:n], dots[:, t, 0:n], g, ALU.mult).then_inc(s_coef, 1)

            def finish(t):
                m = P if t < 2 else NS_TOK
                dve.wait_ge(s_frms, t + 1)
                link(nc.vector.reciprocal(stat[0:m, 46 + t:47 + t], stat[0:m, 43 + t:44 + t]))
                nc.vector.scalar_tensor_tensor(out=h_tok[t][0:m, :], in0=big[0:m, :], scalar=stat[0:m, 46 + t:47 + t], in1=g_row[0:m, :], op0=ALU.mult, op1=ALU.mult).then_inc(s_y, 1)

            dve.wait_ge(s_ht, 3)
            choose(0)
            weigh(0)
            u_dots(0)
            coefs(0)
            choose(1)
            choose(2)
            u_dots(1)
            weigh(1)
            dve.wait_ge(s_grow, 32)
            finish(0)
            coefs(1)
            u_dots(2)
            weigh(2)
            finish(1)
            coefs(2)
            finish(2)

        @block.tensor
        def _(pe):
            def mm(out, lhsT, rhs, start=True, stop=True):
                return nc.tensor.matmul(out, lhsT, rhs, start=start, stop=stop, skip_group_check=True)

            def norm(which, width, groups=1):
                before = N_SUM[which]
                for g in range(groups):
                    if before and g == 0:
                        pe.wait_ge(s_rms, before)
                    pe.wait_ge(s_sqadd, 16 * N_NORM[which] + (g + 1) * KT // groups)
                    mm(bank[2 + g][:, 0:width], ones, acc[g][:, 0:width]).then_inc(s_ss, 1)

            pe.wait_ge(s_const, 16)
            norm("mem", MEM)
            for c in range(4):
                if c == 1:
                    norm("mix", NT)
                chunk_wait(pe, c)
                if c >= 2:
                    pe.wait_ge(s_memev, c - 1)
                w = WR[:, c * D:(c + 1) * D]
                for k in range(KT):
                    if c == 0:
                        pe.wait_ge(s_h, k + 1)
                    ins = mm(bank[c % 2][:, 0:MEM], w[:, k * P:(k + 1) * P], mem_x[:, k * MEM:(k + 1) * MEM], start=(k == 0), stop=(k == KT - 1))
                ins.then_inc(s_used, 1)
            for c in range(4, 8):
                chunk_wait(pe, c)
                w = WR[:, (c - 4) * D:(c - 3) * D]
                for t in range(2):
                    for q in range(4):
                        k = 4 * (c - 4) + q
                        ins = mm(bank[4 + t], mem_x[:, k * MEM + t * P:k * MEM + (t + 1) * P], w[:, q * 512:(q + 1) * 512], start=(k == 0), stop=(k == KT - 1))
                ins.then_inc(s_used, 1)

            def project(slot, x, b, normed=None):
                for k in range(KT):
                    if normed is not None:
                        pe.wait_ge(s_h, normed + k + 1)
                    ins = mm(bank[b][:, 0:NT], WR[:, slot * D + k * P:slot * D + (k + 1) * P], x[:, k * NT:(k + 1) * NT], start=(k == 0), stop=(k == KT - 1))
                return ins

            def tile(slot, x, b, arrived, free, normed=None):
                pe.wait_ge(s_w[slot], arrived)
                if free is not None:
                    pe.wait_ge(s_ev, free)
                project(slot, x, b, normed).then_inc(s_used, 1)

            pe.wait_ge(s_memev, 4)
            for f in range(4):
                tile(f, HT, f % 2, 16 * 3, f - 1 if f >= 2 else None, None if f else 16)
            with pe.Fori(1, 8) as i:
                for r in range(4):
                    tile(r, HT, r % 2, i * 16 + 48, i * 4 + (r - 1))
            for f in (32, 33):
                tile(f % 4, HT, f % 2, 16 * ((f + 8) // 4 + 1), f - 1)

            pe.wait_ge(s_ev, T_IN)
            pe.wait_ge(s_memev, 6)
            for n in range(9):
                t, q = n // 3, n % 3
                m = P if t < 2 else NS_TOK
                if n >= 2:
                    pe.wait_ge(s_vtev, n - 1)
                nf = 4 if q < 2 else 1
                for f in range(nf):
                    src = QK[:, (T_VA + 4 * q + f) * NT + t * P:(T_VA + 4 * q + f) * NT + t * P + m]
                    ins = nc.tensor.transpose(bank[3 + n % 2][0:m, f * P:(f + 1) * P], src, ident)
                ins.then_inc(s_vt, 1)
            pe.wait_ge(s_tab, 16)
            for n in range(16):
                if n >= 2:
                    pe.wait_ge(s_biasev, n - 1)
                for q in range(4):
                    c0 = 16 * n + 4 * q
                    ins = mm(bank[6 + n % 2][:, q * 128:(q + 1) * 128], oh_p[:, 252 - c0:380 - c0], rb_p)
                ins.then_inc(s_bias, 1)
            for n, (g, a, b) in enumerate(((0, 0, 512), (0, 512, USED + WIN), (1, 0, P + WIN))):
                pe.wait_ge(s_biasev, 15 + n)
                oh = oh_sb if g else oh_sa
                for t in range(2):
                    ins = mm(bank[6 + n % 2][:, 0:b - a], rb_s[:, g, t, :], oh[:, t, a:b], start=(t == 0), stop=(t == 1))
                ins.then_inc(s_bias, 1)
            pe.wait_ge(s_biasev, 19)
            pe.wait_ge(s_vtev, 9)

            def scores_p(p):
                pe.wait_ge(s_qapart, p + 1)
                if p >= 2:
                    pe.wait_ge(s_max, p - 1)
                kt = QK[:, (T_KB if p >= 8 else T_KA + p) * NT:][:, 0:NT]
                for s in range(2):
                    o = bank[4 + 2 * (p % 2) + s]
                    mm(o[:, 0:256], q_apart[:, s, 128:256], kt[:, 0:256])
                    ins = mm(o[:, 256:384], q_apart[:, s, 0:128], kt[:, 0:128])
                ins.then_inc(s_S, 1)

            def turn_p(p):
                for s in range(2):
                    pe.wait_ge(s_nrm, 2 * p + s + 1)
                    if p:
                        pe.wait_ge(s_Tev, 2 * p + s - 1)
                    for b in range(3):
                        ins = nc.tensor.transpose(bank[s][:, b * P:(b + 1) * P], probs_p[:, p % 2, s, b * P:(b + 1) * P], ident)
                    ins.then_inc(s_T, 1)

            def values_p(p):
                for s in range(2):
                    pe.wait_ge(s_Tev, 2 * p + s + 1)
                    if p:
                        pe.wait_ge(s_Oev, 2 * p + s - 1)
                    c = (p + 8 * s) * DH if p < 8 else 1024 + 64 * s
                    o = bank[2 + s]
                    pT = probsT_p[:, s, :]
                    mm(o[0:64, 128:256], VT[:, 0, c:c + DH], pT[:, 0:128], start=True, stop=False)
                    mm(o[0:64, 128:256], VT[:, 1, c:c + DH], pT[:, 128:256], start=False, stop=True)
                    mm(o[0:64, 0:128], VT[:, 0, c:c + DH], pT[:, 256:384]).then_inc(s_O, 1)

            for it in range(HEADS + 2):
                if it < HEADS:
                    scores_p(it)
                if it >= 2:
                    values_p(it - 2)
                if 1 <= it <= HEADS:
                    turn_p(it - 1)
            pe.wait_ge(s_newk, 8)
            pe.wait_ge(s_kb, 16)
            pe.wait_ge(s_vb, 16)
            pe.wait_ge(s_Oev, 2 * HEADS)

            def scores_s(n):
                if n:
                    pe.wait_ge(s_smax, 2 * n)
                pe.wait_ge(s_qpad, 4 * n + 4)
                for j in range(8):
                    pe.wait_ge(s_kr[j], 16 * (n + 1))
                    w = qpad_a[n % 2][:, j * P:(j + 1) * P]
                    mm(bank[0][:, 0:320], w, kr[j][:, 0:320], start=(j == 0), stop=(j == 7))
                    mm(bank[1], w, kr[j][:, 320:SW], start=(j == 0), stop=(j == 7)).then_inc(s_krused, 1)
                mm(bank[6][:, 0:P], qpad_b[n % 2], kbT[:, n, :])
                mm(bank[6][:, P:P + NEWK], qpad_b[n % 2], QK[:, T_KB * NT + NP_TOK:T_VA * NT]).then_inc(s_sS, 1)

            def turn_s(n):
                pe.wait_ge(s_sexp, 2 * n + 1)
                for b, (a, w) in enumerate(((0, 64), (64, 128), (192, 128), (320, 128), (448, 128), (576, 128), (704, 128))):
                    t, o = (2, b * P) if b < 3 else (3, (b - 3) * P)
                    ins = nc.tensor.transpose(bank[t][0:w, o:o + P], s_a[:, a:a + w], ident)
                    if b in (2, 6):
                        ins.then_inc(s_sT, 1)
                pe.wait_ge(s_sexp, 2 * n + 2)
                if n:
                    pe.wait_ge(s_sPev, 4 * n)
                nc.tensor.transpose(bank[7][:, 256:384], s_b[:, 0:P], ident)
                nc.tensor.transpose(bank[7][0:NEWK, 384:512], s_b[:, P:P + NEWK], ident).then_inc(s_sT, 1)

            def values_s(n):
                pe.wait_ge(s_sTev, 3 * n + 2)
                if n:
                    pe.wait_ge(s_sOev, n)
                else:
                    pe.wait_ge(s_padz, 3)
                for b in range(7):
                    if b:
                        pe.wait_ge(s_vr[b - 1], 16 * (n + 1))
                    for q in range(2):
                        v = VT[:, 2, q * 512:(q + 1) * 512] if b == 0 else vr[b - 1][:, q * 512:(q + 1) * 512]
                        ins = mm(bank[4 + q], pT_a[:, b * P:(b + 1) * P], v, start=(b == 0), stop=(b == 6))
                    if b:
                        ins.then_inc(s_vrused, 1)
                pe.wait_ge(s_sTev, 3 * n + 3)
                mm(bank[7][:, 0:P], pT_b[:, 0:P], vb[:, n, :], start=True, stop=False)
                mm(bank[7][:, 0:P], pT_b[:, P:2 * P], VT[:, 2, 1024:VW], start=False, stop=True).then_inc(s_sO, 1)

            def pair_s(n):
                pe.wait_ge(s_sOev, n + 1)
                if n:
                    pe.wait_ge(s_sPev, 4 * n)
                nc.tensor.transpose(bank[7][:, 128:256], o_pair, ident).then_inc(s_sP, 1)

            scores_s(0)
            for n in range(REQ):
                if n + 1 < REQ:
                    scores_s(n + 1)
                if n:
                    pair_s(n - 1)
                turn_s(n)
                values_s(n)
            pair_s(REQ - 1)
            norm("group", NT, 2)

            def stream_tiles(x, at, c_at, normed):
                for r in range(4):
                    tile((c_at + r) % 4, x, r % 2, 16 * ((c_at + r) // 4 + 1), at + r - 1, None if r else normed)
                with pe.Fori(1, 4) as i:
                    for r in range(4):
                        tile((c_at + r) % 4, x, r % 2, i * 16 + 16 * ((c_at + r) // 4 + 1), i * 4 + (at + r - 1))

            stream_tiles(OT, T_IN, C_OUT, 32)
            at = T_IN + KT
            norm("cross", NT)
            for f in range(4):
                c = C_CQ + f
                tile(c % 4, HT, f % 2, 16 * (c // 4 + 1), at + f - 1, None if f else 48)
            at += 4
            pe.wait_ge(s_ev, at)

            def scores_c(u):
                if u >= 2:
                    pe.wait_ge(s_cexp, u - 1)
                o = bank[3 + u % 2][:, 0:256]
                if u < 8:
                    if u == 0:
                        pe.wait_ge(s_km[0], 64)
                    h, q = u % 4, u // 4
                    mm(o, qc[:, h, q * P:(q + 1) * P], km_p[:, h * MEM:(h + 1) * MEM]).then_inc(s_cS, 1)
                else:
                    g = u - 8
                    if g:
                        pe.wait_ge(s_km[1], 32)
                    pe.wait_ge(s_cpad, 4 * g + 4)
                    for m in range(16):
                        ins = mm(o, qpad_c[:, m * P:(m + 1) * P], km[g][:, m * MEM:(m + 1) * MEM], start=(m == 0), stop=(m == 15))
                    ins.then_inc(s_cS, 1)

            def turn_c(u):
                pe.wait_ge(s_cnrm, u + 1)
                if u:
                    pe.wait_ge(s_cTev, u)
                for b in range(2):
                    ins = nc.tensor.transpose(bank[5][:, b * P:(b + 1) * P], probs_c[:, u % 2, b * P:(b + 1) * P], ident)
                ins.then_inc(s_cT, 1)

            def values_c(u):
                pe.wait_ge(s_cTev, u + 1)
                if u >= 2:
                    pe.wait_ge(s_cOev, u - 1)
                o = bank[6 + u % 2]
                pT = probsT_c[:, u % 2, :]
                if u < 8:
                    h = u % 4
                    for b in range(2):
                        ins = mm(o[:, 0:P], vm_p[:, b * 512 + h * P:b * 512 + (h + 1) * P], pT[:, b * P:(b + 1) * P], start=(b == 0), stop=(b == 1))
                else:
                    for m in range(16):
                        n, h = m // 4, m % 4
                        for b in range(2):
                            ins = mm(o[:, m * 8:m * 8 + 8], vm[u - 8][:, n * 1024 + b * 512 + h * P:][:, 0:P], pT[:, b * P + m * 8:b * P + m * 8 + 8], start=(b == 0), stop=(b == 1))
                ins.then_inc(s_cO, 1)

            for it in range(12):
                if it < 10:
                    scores_c(it)
                if it >= 2:
                    values_c(it - 2)
                if 1 <= it <= 10:
                    turn_c(it - 1)
            pe.wait_ge(s_cOev, 10)
            for f in range(KT):
                c = C_CO + f // 4
                chunk_wait(pe, c)
                if f >= 2:
                    pe.wait_ge(s_ev, at + f - 1)
                for k in range(4):
                    w = WR[:, (c % 4) * D + (f % 4) * 512 + k * P:][:, 0:P]
                    ins = mm(bank[f % 2][:, 0:NT], w, oc[:, k, :], start=(k == 0), stop=(k == 3))
                ins.then_inc(s_used, 1)
            at += KT
            norm("ffn", NT)
            stream_tiles(HT, at, C_PQ, 64)
            at += KT
            for t in range(3):
                m = P if t < 2 else NS_TOK
                if t:
                    pe.wait_ge(s_ht, t)
                for k in range(KT):
                    ins = nc.tensor.transpose(big[0:m, k * P:(k + 1) * P], XT[:, k * NT + t * P:k * NT + t * P + m], ident)
                ins.then_inc(s_xt, 1)
            pe.wait_ge(s_ev, at)
            for t in range(3):
                if t:
                    pe.wait_ge(s_scev, t)
                for x in range(2 * PH):
                    ins = mm(bank[x // 4][:, (x % 4) * P:(x % 4 + 1) * P], qp[:, x, t * P:(t + 1) * P], sub_keys[:, (x % 2) * NKEY:(x % 2 + 1) * NKEY])
                ins.then_inc(s_sc, 1)
            pe.sem_inc(s_vmm, RING)
            for t in range(3):
                m = P if t < 2 else NS_TOK
                n = SLOTS if t < 2 else SLOTS // 2
                pe.wait_ge(*((s_y, t) if t else (s_ht, 3)))
                for k in range(KT):
                    mm(big[0:m, k * P:(k + 1) * P], XT[:, k * NT + t * P:k * NT + t * P + m], ident, start=(k % 4 == 0), stop=False)
                with pe.Fori(0, n // RING) as i:
                    for r in range(RING):
                        pe.wait_ge(s_vg[r], i * 16 + 16 * (t * SLOTS // RING + 1))
                        pe.wait_ge(s_dg, i * RING + (t * SLOTS + r + 1))
                        for q in range(4):
                            ins = mm(big[0:m, q * 512:(q + 1) * 512], diag[r][:, 0:m], v_ring[r][:, q * 512:(q + 1) * 512], start=False, stop=False)
                        ins.then_inc(s_vmm, 1)


def bucket(dist):
    dist = np.maximum(np.asarray(dist), 0)
    ratio = np.log(np.maximum(dist, 1) / 16) / math.log(2048 / 16)
    large = np.minimum(16 + (ratio * 16).astype(np.int32), 31)
    return np.where(dist < 16, dist, large).astype(np.int32)


def one_hot(dist, mixer, masked=None):
    dist = np.asarray(dist)
    out = np.zeros((32,) + dist.shape, np.float32)
    b = bucket(dist)
    assert b.max() < 30
    np.put_along_axis(out, b[None], 1.0, axis=0)
    held_a = (dist <= 128).astype(int) + ((dist % 4 == 0) & (dist <= 512)) + (dist % 16 == 0)
    for row, held in ((30, held_a), (31, (dist <= 128).astype(int))):
        if mixer in (row, None):
            seen = (dist >= 0) & (held > 0)
            if masked is not None:
                seen &= ~masked
            out[row] = np.where(seen, np.log(np.maximum(held, 1)), NEG)
    return out


def kernel(**inputs):
    import concourse.bacc as bacc
    from concourse.bass_utils import run_bass_kernel_spmd

    x = {k: np.asarray(v) for k, v in inputs.items()}
    f32 = np.float32

    def tiles(a):
        return a.T.reshape(-1, P, a.shape[0]).transpose(1, 0, 2).reshape(P, -1)

    pair = np.arange(1024).reshape(2, 8, 64).transpose(1, 0, 2).ravel()
    at = np.arange(512).reshape(32, 2, 8)
    key_order = np.concatenate([at[:, 1].ravel(), at[:, 0].ravel(), np.arange(512, PAST)])

    def chunks(w):
        return w.reshape(-1, P, w.shape[1] // P, P).transpose(2, 1, 0, 3).reshape(w.shape[1] // P, P, -1)

    w_in = x["w_in"][0]
    a = 1024
    w_in = np.concatenate([w_in[:, :a][:, pair], w_in[:, a:2 * a][:, pair], w_in[:, 3 * a:4 * a][:, pair],
                           w_in[:, 4 * a:4 * a + P], w_in[:, 2 * a:3 * a], w_in[:, 4 * a + P:]], axis=1)
    rows = np.concatenate([pair, a + pair])
    w_ckv = x["w_ckv"][0]
    wall = np.concatenate([
        chunks(w_ckv[:, :512]),
        w_ckv[:, 512:].reshape(4, 4, P, 512).transpose(0, 2, 1, 3).reshape(4, P, D),
        chunks(w_in), chunks(x["w_out"][0][rows]), chunks(x["w_cq"][0]),
        chunks(x["w_co"][0]).reshape(4, 4, P, 512).transpose(0, 2, 1, 3).reshape(4, P, D),
        chunks(x["w_pq"][0])])

    def gain(g):
        return g.reshape(KT, P).T

    gains = [gain(x["ln_mix"][0]), gain(x["ln_mem"][0]), gain(x["ln_cross"][0]), gain(x["ln_ffn"][0]),
             gain(np.concatenate([x["ln_a_out"][0], x["ln_b_out"][0]])[rows])]
    sinks = x["b_sinks"][0]
    consts = np.concatenate([
        np.eye(P, dtype=f32), np.ones((P, P), f32), *gains, np.broadcast_to(sinks, (P, HEADS)),
        np.repeat(sinks, QPR)[:, None], np.broadcast_to(np.arange(PK, dtype=f32), (P, PK)),
        (np.arange(P)[:, None] % 64 == np.arange(64)).astype(f32), x["sub_keys_1"][0].T, x["sub_keys_2"][0].T], axis=1)

    rel = x["rel_bias"]
    rb = np.zeros((4, 32, 4, 32), f32)
    for g in range(4):
        rb[g, :30, g] = rel[:30]
        rb[g, 30, g, :16] = 1
        rb[g, 31, g, 16:] = 1
    j = np.arange(380)
    oh_p = np.stack([one_hot(j - 124 - g, None) for g in range(4)])
    rb_s = np.zeros((4, 32, 2, 2, HEADS, QPR), f32)
    oh_sa, oh_sb = np.zeros((4, 32, 2, USED + WIN), f32), np.zeros((4, 32, 2, P + WIN), f32)
    new = np.arange(WIN) - 7 * QPR
    for t in range(2):
        for g in range(4):
            q = 4 * t + g
            rb_s[g, :30, :, t, :, q] = rel[:30].reshape(30, 2, HEADS)
            rb_s[g, 30, 0, t, :, q] = 1
            rb_s[g, 31, 1, t, :, q] = 1
            own = (new < 0) | (new >= QPR)
            oh_sa[g, :, t] = np.concatenate([one_hot(PAST + q - key_order[FIRST:], 30), one_hot(q - new, 30, own)], axis=1)
            oh_sb[g, :, t] = np.concatenate([one_hot(P + q - np.arange(P), 31), one_hot(q - new, 31, own)], axis=1)
    tables = np.concatenate([m.reshape(P, -1) for m in (rb, oh_p, rb_s, oh_sa, oh_sb)], axis=1)
    head_mask = (np.arange(P)[:, None] // QPR % 8 == np.arange(512) // 64).astype(f32)

    ka = x["cache_a_k"][0][:, key_order].reshape(REQ, PAST, 1024)[:, :, pair]
    ka = np.ascontiguousarray(ka.transpose(0, 2, 1)).reshape(REQ, 8, P, PAST)
    va = np.ascontiguousarray(x["cache_a_v"][0].reshape(REQ, PAST, 1024)[:, key_order])
    tokens = np.concatenate([x["x_prompt"][0], x["x_sample"].reshape(NS_TOK, D)])
    arrays = {
        "xT": tiles(tokens), "memT": tiles(x["mem_prompt"][0]), "consts": consts, "tables": tables,
        "head_mask": head_mask, "wall": wall, "ffn_row": x["ln_ffn"][0], "fin_row": x["ln_final"],
        "kaT": ka, "va": va,
        "kbT": x["cache_b_k"][0].reshape(REQ, P, P).transpose(2, 0, 1).reshape(P, -1),
        "vb": x["cache_b_v"][0].reshape(REQ, P, P).transpose(1, 0, 2).reshape(P, -1),
        "kmT": x["cache_mem_k"][0].transpose(0, 3, 2, 1).reshape(REQ, P, 1024),
        "vm": x["cache_mem_v"][0].reshape(REQ, 2, P, 512).transpose(0, 2, 1, 3).reshape(REQ, P, 1024),
        "expert_u": x["expert_u"][0], "expert_v": x["expert_v"][0],
    }
    arrays = {k: np.ascontiguousarray(v) for k, v in arrays.items()}
    outs = {
        "y": (NT, D), "ka_out": (32, 256, 1024), "va_out": (32, 256, 1024), "kaT_new": (P, 8 * NT), "kbT_new": (P, NT),
        "v_new": (P, 2 * VW), "v_new_s": (NS_TOK, VW), "kb_out": (P, REQ * P), "vb_out": (P, REQ * P),
        "mk_out": (P, 1024), "mv_out": (P, 1024),
    }
    nc = bacc.Bacc("TRN2", target_bir_lowering=False, num_devices=1)
    d = {k: nc.dram_tensor(k, v.shape, mybir.dt.from_np(v.dtype), kind="ExternalInput").ap() for k, v in arrays.items()}
    d |= {k: nc.dram_tensor(k, s, F32, kind="ExternalOutput").ap() for k, s in outs.items()}
    d["ka_flat"] = d["kaT"].rearrange("n j p u -> (n j p) u").rearrange("(c r) u -> c r u", c=32)
    d["va_flat"] = d["va"].rearrange("n t w -> (n t) w").rearrange("(c r) u -> c r u", c=32)
    build(nc, d)
    o = run_bass_kernel_spmd(nc, [arrays], core_ids=[0]).results[0]

    unpair = np.argsort(pair)
    y = o["y"]
    k_new = o["kaT_new"].reshape(P, 8, NT).transpose(2, 1, 0).reshape(NT, 1024)[:, unpair].reshape(NT, HEADS, DH)
    kb_new = o["kbT_new"].T.reshape(NT, 2, DH)
    v_new = np.concatenate([o["v_new"].reshape(P, 2, VW).transpose(1, 0, 2).reshape(NP_TOK, VW), o["v_new_s"]])
    va_new, vb_new = v_new[:, :1024].reshape(NT, HEADS, DH), v_new[:, 1024:].reshape(NT, 2, DH)
    back = np.argsort(key_order)
    ka_old = o["ka_out"].reshape(REQ, 1024, PAST).transpose(0, 2, 1)[:, back][:, :, unpair].reshape(REQ, PAST, HEADS, DH)
    va_old = o["va_out"].reshape(REQ, PAST, HEADS, DH)[:, back]
    kb_old = o["kb_out"].reshape(P, REQ, P).transpose(1, 2, 0).reshape(REQ, P, 2, DH)
    vb_old = o["vb_out"].reshape(P, REQ, P).transpose(1, 0, 2).reshape(REQ, P, 2, DH)

    def sampled(old, new, drop):
        return np.concatenate([old[:, drop:], new[NP_TOK:].reshape(REQ, QPR, *new.shape[1:])], axis=1)[None]

    mk = o["mk_out"].reshape(P, MEM_HEADS, MEM).transpose(2, 1, 0)[None, None]
    mv = o["mv_out"].reshape(P, 2, MEM_HEADS, MEM_DH).transpose(1, 0, 2, 3).reshape(MEM, MEM_HEADS, MEM_DH)[None, None]
    return tuple(np.ascontiguousarray(r) for r in (
        y[None, :NP_TOK], y[NP_TOK:].reshape(REQ, QPR, D),
        k_new[None, None, :NP_TOK], va_new[None, None, :NP_TOK], kb_new[None, None, NP_TOK - P:NP_TOK], vb_new[None, None, NP_TOK - P:NP_TOK],
        mk, mv,
        sampled(ka_old, k_new, 0), sampled(va_old, va_new, 0), sampled(kb_old, kb_new, QPR), sampled(vb_old, vb_new, QPR)))
```

```python
import math
from contextlib import ExitStack

import numpy as np
import concourse.bass as bass
from concourse import mybir

F32 = mybir.dt.float32
U32 = mybir.dt.uint32
ALU = mybir.AluOpType
ACT = mybir.ActivationFunctionType
AX_X = mybir.AxisListType.X

P = 128
D = 2048
KT = D // P
NP_TOK, NS_TOK = 256, 64
NT = NP_TOK + NS_TOK
REQ, QPR = 8, 8
HEADS, DH = 16, 64
SCALE = DH ** -0.5
PAST = 1024
MEM, MEM_HEADS, MEM_DH = 256, 4, 128
MEM_SCALE = MEM_DH ** -0.5
EPS = 1e-6
NEG = -1e30
T_QA, T_KA, T_QB, T_KB, T_VA, T_VB, T_IN = 0, 8, 16, 24, 25, 33, 34
VW = 9 * P
USED = 768
FIRST = 256
NEWK = NS_TOK
SW = NEWK + USED
WIN = 15 * QPR
C_MEM, C_IN, C_OUT, C_CQ, C_CO, C_PQ, C_END = 0, 8, 42, 58, 62, 66, 82
WR_N = 4
PH, PK, NKEY = 8, 16, 128
SLOTS = PH * PK
W_IN, W_OUT, W_CQ, W_CO, W_PQ, W_END = 8, 42, 58, 62, 78, 94
RING = 4
ROWS = (SLOTS, SLOTS, SLOTS // 2)
GROUPS = [(0, 0, 1), (0, 1, 1), (0, 2, 2), (0, 4, 2), (0, 6, 2)] + [(t, h, 2) for t in (1, 2) for h in range(0, PH, 2)]
FIRST_OF = [0, 5, 9, 13]
SHARED_FROM = (SLOTS, SLOTS // 2, 0)


def on_vector(t, s):
    return s >= SHARED_FROM[t] and s % RING == RING - 1


def rows_added(t, s, vector):
    return sum(on_vector(u, v) == vector for u in range(t + 1) for v in range(ROWS[u] if u < t else s))


def build(nc, d):
    with ExitStack() as ctx:
        def sem(name):
            return ctx.enter_context(nc.semaphore(name))

        def region(name, words):
            return ctx.enter_context(nc.sbuf_tensor(name, [P, words], F32))

        CST = region("CST", 776)
        XT = region("XT", KT * NT)
        WR = region("WR", WR_N * D)
        HT = region("HT", KT * NT)
        QK = region("QK", T_IN * NT)
        VO = region("VO", 3 * VW + KT * NT)
        KV = region("KV", 8 * SW + 6 * 1024)
        VB = region("VB", REQ * P)

        cst_at = [0]

        def const(n):
            cst_at[0] += n
            return CST[:, cst_at[0] - n:cst_at[0]]

        ident, ones = const(P), const(P)
        gains = const(5 * KT)
        G_MIX, G_MEM, G_CROSS, G_FFN, G_AB = (gains[:, i * KT:(i + 1) * KT] for i in range(5))
        sink_prompt, sink_sample = const(HEADS), const(1)
        iota16 = const(PK)
        pair_sel = const(64)
        sub_keys = const(2 * NKEY)
        n_host_const = cst_at[0]
        eps = const(1)
        stat = const(80)

        mem_x = QK[:, 0:KT * MEM]
        mem_kT = KV[:, 8 * SW:8 * SW + 1024]
        mem_v = KV[:, 8 * SW + 1024:8 * SW + 2048]
        VT = VO[:, 0:3 * VW].rearrange("p (t w) -> p t w", t=3)
        OT = VO[:, 3 * VW:3 * VW + KT * NT]
        sq = VO[:, 0:4 * NT]
        acc = [VO[:, 4 * NT:5 * NT], VO[:, 5 * NT:6 * NT]]
        rs = VO[:, 8 * NT:9 * NT]
        rms = VO[:, 9 * NT:10 * NT]

        bias_p = WR[:, 0:32 * 256].rearrange("p (h c) -> p h c", h=32)
        tab = OT
        n_tab = 128 + 380 + 4 * 128 + 2 * (USED + WIN + P + WIN)
        rb_p, oh_p = tab[:, 0:128], tab[:, 128:508]
        rb_s = tab[:, 508:1020].rearrange("p (g t c) -> p g t c", g=2, t=2)
        oh_sa = tab[:, 1020:1020 + 2 * (USED + WIN)].rearrange("p (t u) -> p t u", t=2)
        oh_sb = tab[:, 1020 + 2 * (USED + WIN):n_tab].rearrange("p (t u) -> p t u", t=2)
        VTF = QK[:, T_VA * NT:T_IN * NT]
        probs_p = VTF[:, 0:1536].rearrange("p (b s c) -> p b s c", b=2, s=2)
        probsT_p = VTF[:, 1536:2304].rearrange("p (s c) -> p s c", s=2)
        q_apart = VTF[:, 2304:2816].rearrange("p (s c) -> p s c", s=2)
        bias_sa, bias_sb = HT[:, 0:USED + WIN], HT[:, 888:888 + P + WIN]
        head_mask = HT[:, 1136:1648]
        qpad_a = [HT[:, 1648 + i * 1088:2736 + i * 1088] for i in range(2)]
        qpad_b = [HT[:, 3824 + i * 128:3952 + i * 128] for i in range(2)]
        kbT = HT[:, 4080:5104].rearrange("p (n u) -> p n u", n=REQ)
        vb = VB[:, :].rearrange("p (n w) -> p n w", n=REQ)
        kr = [KV[:, j * SW:(j + 1) * SW] for j in range(8)]
        vr = [KV[:, 8 * SW + k * 1024:8 * SW + (k + 1) * 1024] for k in range(6)]
        s_a = VTF[:, 0:SW]
        pT_a = VTF[:, SW:SW + 896]
        s_b = VTF[:, 1728:1728 + 192]
        pT_b = VTF[:, 1920:1920 + 256]
        o_masked = VTF[:, 2176:2688]
        o_pair = VTF[:, 2688:2816]
        km = [KV[:, 0:4096], QK[:, 0:4096]]
        vm = [KV[:, 4096:8192], QK[:, 4096:8192]]
        km_p = KV[:, 8192:9216]
        vm_p = KV[:, 9216:10240]
        qc = QK[:, 8192:8192 + 4 * NT].rearrange("p (h t) -> p h t", h=4)
        oc = QK[:, 9472:9472 + 4 * NT].rearrange("p (h t) -> p h t", h=4)
        probs_c = VO[:, 0:512].rearrange("p (b c) -> p b c", b=2)
        probsT_c = VO[:, 512:1024].rearrange("p (b c) -> p b c", b=2)
        qpad_c = VO[:, 1024:1024 + 2176]
        probsT_r = VO[:, 3 * VW:3 * VW + 512].rearrange("p (b c) -> p b c", b=2)
        qp = QK[:, 0:KT * 384].rearrange("p (f t) -> p f t", f=KT)
        sc = QK[:, 6144:8192]
        tk = QK[:, 8192:10880]
        top_v = tk[:, 0:256].rearrange("p (h z k) -> p h z k", h=PH, z=2)
        top_i = tk[:, 256:512].bitcast(U32).rearrange("p (h z k) -> p h z k", h=PH, z=2)
        top_f = tk[:, 512:768].rearrange("p (h z k) -> p h z k", h=PH, z=2)
        best = tk[:, 768:896].rearrange("p (h k) -> p h k", h=PH)
        pos = tk[:, 896:1024].bitcast(U32).rearrange("p (h k) -> p h k", h=PH)
        pos_i = tk[:, 1024:1280].bitcast(U32)
        pos_f = tk[:, 1280:1536]
        exp_f = tk[:, 1536:1792]
        eidx_f = tk[:, 1792:1920]
        gexp = [g.rearrange("p (h k) -> p h k", h=PH) for g in (tk[:, 1920:2048], VB[:, 768:896], VB[:, 896:1024])]
        eidx = tk[:, 2048:2432].bitcast(U32).rearrange("p (t s) -> p t s", t=3)
        gate = VB[:, 0:384].rearrange("p (t s) -> p t s", t=3)
        dots = VB[:, 384:768].rearrange("p (t s) -> p t s", t=3)
        pair_gate, pair_idx = tk[:, 2432:2496], tk[:, 2496:2560].bitcast(U32)
        h_tok = [VO[:, t * D:(t + 1) * D] for t in range(3)]
        g_row = VO[:, 3 * D:4 * D]
        u_ring = [KV[:, r * D:(r + 1) * D] for r in range(RING)]
        v_ring = [WR[:, r * D:(r + 1) * D] for r in range(RING)]
        diag = [HT[:, r * P:(r + 1) * P] for r in range(RING)]

        low = ctx.enter_context(nc.psum_tensor("low", [P, 2048], F32))[:, :]
        big = ctx.enter_context(nc.psum_tensor("big", [P, 2048], F32))[:, :]
        bank = [half[:, i * 512:(i + 1) * 512] for half in (low, big) for i in range(4)]
        y_acc = [big, low, big]

        s_const, s_x, s_tab = sem("consts_in"), sem("x_in"), sem("tables_in")
        s_memx = [sem(f"mem_in{i}") for i in range(4)]
        s_mask, s_kb, s_vb = sem("mask_in"), sem("kb_in"), sem("vb_in")
        s_w = [sem(f"chunk_in{i}") for i in range(WR_N)]
        s_used = sem("chunk_used")
        s_eps = sem("eps_set")
        s_sq, s_sqadd, s_ss = sem("squares"), sem("squares_added"), sem("square_sums")
        s_rms, s_rs, s_h = sem("rms"), sem("inv_rms"), sem("normed")
        s_ev = sem("evacuated")
        s_memout, s_memev = sem("mem_out"), sem("mem_kept")
        s_bias, s_biasev = sem("bias_ready"), sem("bias_kept")
        s_vt, s_vtev = sem("values_turned"), sem("values_kept")
        s_qz, s_qapart, s_padz = sem("q_zero"), sem("q_apart"), sem("rows_zero")
        s_S, s_max, s_exp, s_nrm = sem("p_scores"), sem("p_max"), sem("p_exp"), sem("p_normed")
        s_T, s_Tev, s_O, s_Oev = sem("p_turned"), sem("p_turned_kept"), sem("p_out"), sem("p_out_kept")
        s_kr = [sem(f"keys_in{j}") for j in range(8)]
        s_vr = [sem(f"values_in{j}") for j in range(6)]
        s_krused, s_vrused = sem("keys_used"), sem("values_used")
        s_newk = sem("new_keys")
        s_zero, s_qpad = sem("pads_zero"), sem("pads_filled")
        s_sS, s_smax, s_sexp = sem("s_scores"), sem("s_max"), sem("s_exp")
        s_sT, s_sTev, s_sO, s_sOev = sem("s_turned"), sem("s_turned_kept"), sem("s_out"), sem("s_pair")
        s_sP, s_sPev = sem("s_pair_turned"), sem("s_kept")
        s_km = [sem("mem_cache_in0"), sem("mem_cache_in1")]
        s_cS, s_cmax, s_cexp, s_cnrm = sem("c_scores"), sem("c_max"), sem("c_exp"), sem("c_normed")
        s_cT, s_cTev, s_cO, s_cOev = sem("c_turned"), sem("c_turned_kept"), sem("c_out"), sem("c_kept")
        s_cpad, s_cOr = sem("c_pads"), sem("c_out_requests")
        s_xt, s_xrms, s_ht = sem("x_turned"), sem("x_rms"), sem("h_tok")
        s_grow, s_dup = sem("gain_row_in"), sem("h_dup")
        s_sc, s_scev = sem("k_scores"), sem("k_scores_kept")
        s_dv, s_gx, s_gxe, s_idx = sem("dve_chain"), sem("gate_diff"), sem("gate_exp"), sem("experts_chosen")
        s_ug = [sem(f"u_in{r}") for r in range(RING)]
        s_vg = [sem(f"v_in{r}") for r in range(RING)]
        s_udot, s_gelu, s_coef, s_dg, s_vmm = sem("u_dots"), sem("gelu"), sem("coefs"), sem("diags"), sem("v_added")
        s_vsum, s_vall = sem("v_summed"), sem("tile_complete")
        s_frms, s_y = sem("y_rms"), sem("y_ready")
        s_ac = sem("act_chain")
        s_attout = sem("attention_outputs")
        s_copy, s_out = sem("cache_copied"), sem("outputs")
        def chunk_wait(eng, c):
            eng.wait_ge(s_w[c % WR_N], 16 * (c // WR_N + 1))

        block = ctx.enter_context(nc.Block())

        N_NORM = {"mem": 0, "mix": 1, "group": 2, "cross": 3, "ffn": 4}
        N_SUM = {"mem": 0, "mix": 1, "group": 2, "cross": 4, "ffn": 5}

        @block.sync
        def _(sp):
            for i in range(4):
                part = slice(i * 4 * MEM, (i + 1) * 4 * MEM)
                sp.dma_start(mem_x[:, part], d["memT"][:, part]).then_inc(s_memx[i], 16)
            sp.dma_start(CST[:, 0:n_host_const], d["consts"]).then_inc(s_const, 16)
            for c in range(WR_N):
                sp.dma_start(WR[:, c * D:(c + 1) * D], d["wall"][c]).then_inc(s_w[c], 16)
            sp.dma_start(XT[:, :], d["xT"]).then_inc(s_x, 16)
            sp.dma_start(tab[:, 0:n_tab], d["tables"]).then_inc(s_tab, 16)
            for c in range(WR_N, C_IN):
                sp.wait_ge(s_used, c - WR_N + 1)
                sp.dma_start(WR[:, (c % WR_N) * D:(c % WR_N + 1) * D], d["wall"][c]).then_inc(s_w[c % WR_N], 16)
            with sp.Fori(0, 8) as i:
                for r in range(WR_N):
                    sp.wait_ge(s_used, i * WR_N + (C_IN + r - WR_N + 1))
                    sp.dma_start(WR[:, r * D:(r + 1) * D], d["wall"][bass.ds(i * WR_N + (C_IN + r), 1)].rearrange("o p w -> (o p) w")).then_inc(s_w[r], 16)
                    for name in ("ka", "va"):
                        src = d[name + "_flat"][bass.ds(i * WR_N + r, 1)].rearrange("o p w -> (o p) w")
                        dst = d[name + "_out"][bass.ds(i * WR_N + r, 1)].rearrange("o p w -> (o p) w")
                        sp.dma_start(dst, src).then_inc(s_copy, 16)
            for c in (C_OUT - 2, C_OUT - 1):
                sp.wait_ge(s_used, c - WR_N + 1)
                sp.dma_start(WR[:, (c % WR_N) * D:(c % WR_N + 1) * D], d["wall"][c]).then_inc(s_w[c % WR_N], 16)
            sp.wait_ge(s_ev, T_IN)
            sp.dma_start(d["kaT_new"], QK[:, T_KA * NT:T_QB * NT]).then_inc(s_attout, 16)
            sp.dma_start(d["kbT_new"], QK[:, T_KB * NT:T_VA * NT]).then_inc(s_attout, 16)
            sp.wait_ge(s_vtev, 9)
            sp.dma_start(d["v_new"], VO[:, 0:2 * VW]).then_inc(s_attout, 16)
            sp.dma_start(d["v_new_s"], VO[0:NS_TOK, 2 * VW:3 * VW]).then_inc(s_attout, 16)
            sp.wait_ge(s_kb, 16)
            sp.dma_start(d["kb_out"], HT[:, 4080:5104]).then_inc(s_attout, 16)
            sp.wait_ge(s_vb, 16)
            sp.dma_start(d["vb_out"], VB[:, :]).then_inc(s_attout, 16)
            sp.wait_ge(s_max, HEADS)
            with sp.Fori(0, (C_PQ - C_OUT) // WR_N) as i:
                for r in range(WR_N):
                    slot = (C_OUT + r) % WR_N
                    sp.wait_ge(s_used, i * WR_N + (C_OUT + r - WR_N + 1))
                    sp.dma_start(WR[:, slot * D:(slot + 1) * D], d["wall"][bass.ds(i * WR_N + (C_OUT + r), 1)].rearrange("o p w -> (o p) w")).then_inc(s_w[slot], 16)
            sp.wait_ge(s_used, W_CQ)
            sp.dma_start(g_row, d["ffn_row"].partition_broadcast(P)).then_inc(s_grow, 16)
            for c in range(C_PQ, C_PQ + WR_N):
                sp.wait_ge(s_used, W_CO + 4 * (c - C_PQ + 1))
                sp.dma_start(WR[:, (c % WR_N) * D:(c % WR_N + 1) * D], d["wall"][c]).then_inc(s_w[c % WR_N], 16)
            with sp.Fori(0, (C_END - C_PQ) // WR_N - 1) as i:
                for r in range(WR_N):
                    slot = (C_PQ + r) % WR_N
                    sp.wait_ge(s_used, i * WR_N + (W_PQ + r + 1))
                    sp.dma_start(WR[:, slot * D:(slot + 1) * D], d["wall"][bass.ds(i * WR_N + (C_PQ + WR_N + r), 1)].rearrange("o p w -> (o p) w")).then_inc(s_w[slot], 16)
            sp.wait_ge(s_ht, 3)
            sp.dma_start(h_tok[2][64:128, :], h_tok[2][0:64, :]).then_inc(s_dup, 16)
            sp.dma_start(g_row, d["fin_row"].partition_broadcast(P)).then_inc(s_grow, 16)
            for t in range(3):
                sp.wait_ge(s_y, t + 1)
                n = P if t < 2 else NS_TOK
                sp.dma_start(d["y"][t * P:t * P + n, :], h_tok[t][0:n, :]).then_inc(s_out, 16)
            sp.wait_ge(s_copy, 2 * 32 * 16)
            sp.wait_ge(s_attout, 6 * 16)
            sp.wait_ge(s_memout, 2 * 16)
            sp.wait_ge(s_out, 3 * 16)

        @block.gpsimd
        def _(pool):
            nc.gpsimd.memset(eps, EPS).then_inc(s_eps, 1)
            pool.dma_start(VB[:, :], d["vb"]).then_inc(s_vb, 16)
            pool.wait_ge(s_memout, 32)
            for k in range(6):
                pool.dma_start(vr[k], d["va"][0, FIRST + k * P:FIRST + (k + 1) * P, :]).then_inc(s_vr[k], 16)
            for j in range(8):
                pool.dma_start(kr[j][:, NEWK:SW], d["kaT"][0, j, :, FIRST:PAST]).then_inc(s_kr[j], 16)
            pool.wait_ge(s_used, W_OUT)
            pool.dma_start(kbT, d["kbT"].rearrange("p (n u) -> p n u", n=REQ)).then_inc(s_kb, 16)
            pool.dma_start(head_mask, d["head_mask"]).then_inc(s_mask, 16)
            for b in (qpad_a[0], qpad_a[1], qpad_b[0], qpad_b[1]):
                nc.gpsimd.memset(b, 0.0).then_inc(s_zero, 1)
            for n in range(1, REQ + 1):
                if n < REQ:
                    for j in range(8):
                        pool.wait_ge(s_krused, 8 * (n - 1) + j + 1)
                        pool.dma_start(kr[j][:, NEWK:SW], d["kaT"][n, j, :, FIRST:PAST]).then_inc(s_kr[j], 16)
                if n >= 2:
                    for k in range(6):
                        pool.wait_ge(s_vrused, 6 * (n - 2) + k + 1)
                        pool.dma_start(vr[k], d["va"][n - 1, FIRST + k * P:FIRST + (k + 1) * P, :]).then_inc(s_vr[k], 16)
            pool.wait_ge(s_vrused, 6 * REQ)
            for g in range(2):
                if g == 1:
                    pool.wait_ge(s_sPev, 4 * REQ)
                    pool.wait_ge(s_attout, 6 * 16)
                pool.dma_start(km[g].rearrange("p (n w) -> p n w", n=4), d["kmT"][4 * g:4 * g + 4].rearrange("n p w -> p n w")).then_inc(s_km[g], 16)
                pool.dma_start(vm[g].rearrange("p (n w) -> p n w", n=4), d["vm"][4 * g:4 * g + 4].rearrange("n p w -> p n w")).then_inc(s_km[g], 16)
                if g == 0:
                    pool.dma_start(km_p, d["mk_out"]).then_inc(s_km[g], 16)
                    pool.dma_start(vm_p, d["mv_out"]).then_inc(s_km[g], 16)
            def rows(ring, sems, table, idx, n):
                nc.gpsimd.indirect_dma_start(ring[n % RING], None, table, bass.IndirectOffsetOnAxis(idx, 0)).then_inc(sems[n % RING], 16)

            def column(n):
                return eidx[:, n // SLOTS, n % SLOTS:n % SLOTS + 1] if n < 2 * SLOTS else pair_idx[:, n - 2 * SLOTS:n - 2 * SLOTS + 1]

            def u_rows(n):
                t, head = min(n // SLOTS, 2), n % SLOTS // PK
                c = next(c for c, (u, h, k) in enumerate(GROUPS) if u == t and h <= head < h + k)
                pool.wait_ge(s_idx, c + 1 if t < 2 else len(GROUPS))
                if n >= RING:
                    pool.wait_ge(s_udot, n - RING + 1)
                rows(u_ring, s_ug, d["expert_u"], column(n), n)

            def v_rows(n):
                if n >= RING:
                    t, s = (n - RING) // SLOTS, (n - RING) % SLOTS
                    if on_vector(t, s):
                        pool.wait_ge(s_vsum, rows_added(t, s, True) + 1)
                    else:
                        pool.wait_ge(s_vmm, RING + rows_added(t, s, False) + 1)
                rows(v_ring, s_vg, d["expert_v"], column(n), n)

            pool.wait_ge(s_cOev, 10)
            for n in range(SLOTS):
                u_rows(n)
            pool.wait_ge(s_used, W_END)
            nu, nv, n_all = SLOTS, 0, 2 * SLOTS + SLOTS // 2
            while nv < n_all:
                v_rows(nv)
                nv += 1
                if nu < n_all:
                    u_rows(nu)
                    nu += 1
                if nv == SLOTS:
                    while nu < 2 * SLOTS:
                        u_rows(nu)
                        nu += 1

        @block.scalar
        def _(act):
            nac = [0]

            def link(ins):
                nac[0] += 1
                ins.then_inc(s_ac, 1)
                act.wait_ge(s_ac, nac[0])

            def squares(which, x, width):
                u = N_NORM[which]
                for k in range(KT):
                    if which == "mem" and k % 4 == 0:
                        act.wait_ge(s_memx[k // 4], 16)
                    if u or k >= 4:
                        act.wait_ge(s_sqadd, 16 * u + k - 3)
                    nc.scalar.activation(sq[:, (k % 4) * NT:(k % 4) * NT + width], x[:, k * width:(k + 1) * width], ACT.Square).then_inc(s_sq, 1)

            def squares_of_stream(which, at):
                u = N_NORM[which]
                for k in range(4):
                    act.wait_ge(s_ev, at + k + 1)
                    act.wait_ge(s_sqadd, 16 * u + k - 3)
                    nc.scalar.activation(sq[:, k * NT:(k + 1) * NT], XT[:, k * NT:(k + 1) * NT], ACT.Square).then_inc(s_sq, 1)
                with act.Fori(1, 4) as i:
                    for r in range(4):
                        act.wait_ge(s_ev, i * 4 + (at + r + 1))
                        act.wait_ge(s_sqadd, i * 4 + (16 * u + r - 3))
                        nc.scalar.activation(sq[:, r * NT:(r + 1) * NT], XT[:, bass.ds(i * (4 * NT) + r * NT, NT)], ACT.Square).then_inc(s_sq, 1)

            def roots(which, width, groups=1):
                before = N_SUM[which]
                for g in range(groups):
                    act.wait_ge(s_ss, before + g + 1)
                    if before + g > 0:
                        act.wait_ge(s_rs, before + g)
                    nc.scalar.activation(rms[:, 0:width], bank[2 + g][:, 0:width], ACT.Sqrt, bias=eps, scale=float(groups) / D).then_inc(s_rms, 1)

            act.wait_ge(s_eps, 1)
            squares("mem", mem_x, MEM)
            roots("mem", MEM)
            act.wait_ge(s_x, 16)
            squares("mix", XT, NT)
            roots("mix", NT)
            for n in range(4):
                act.wait_ge(s_used, n + 1)
                nc.scalar.activation(mem_kT[:, n * MEM:(n + 1) * MEM], bank[n % 2][:, 0:MEM], ACT.Copy).then_inc(s_memev, 1)
            for n in range(2):
                act.wait_ge(s_used, W_IN)
                nc.scalar.activation(mem_v[:, n * 512:(n + 1) * 512], bank[4 + n], ACT.Copy).then_inc(s_memev, 1)
            act.wait_ge(s_memev, 6)
            act.dma_start(d["mk_out"], mem_kT).then_inc(s_memout, 16)
            act.dma_start(d["mv_out"], mem_v).then_inc(s_memout, 16)
            for n in range(9):
                t, q = n // 3, n % 3
                w, m = (512, P) if q < 2 else (128, P)
                if t == 2:
                    m = NS_TOK
                act.wait_ge(s_vt, n + 1)
                nc.scalar.activation(VT[0:m, t, q * 512:q * 512 + w], bank[3 + n % 2][0:m, 0:w], ACT.Copy).then_inc(s_vtev, 1)
            def split_q(p):
                if p == 0:
                    act.wait_ge(s_qz, 1)
                else:
                    act.wait_ge(s_S, p)
                for s in range(2):
                    rows = slice(64 * s, 64 * s + 64)
                    q = QK[rows, ((T_QB if p >= 8 else T_QA) + p % 8) * NT:][:, 0:NP_TOK]
                    ins = nc.scalar.activation(q_apart[rows, s, :], q, ACT.Copy)
                ins.then_inc(s_qapart, 1)

            def exp_p(p):
                pb, b = probs_p[:, p % 2], 16 * (p % 2)
                act.wait_ge(s_max, p + 1)
                for s in range(2):
                    for q, (lo, hi) in enumerate(((0, 256), (256, 384))):
                        c = b + 2 * s + q
                        ins = nc.scalar.activation(pb[:, s, lo:hi], pb[:, s, lo:hi], ACT.Exp, bias=stat[:, c:c + 1], scale=1.0, accum_out=stat[:, c + 4:c + 5])
                if p >= 8:
                    for s in range(2):
                        c, h = b + 2 * s, p % 8 + 8 * s
                        ins = nc.scalar.activation(stat[:, c + 8:c + 10], stat[:, c:c + 2], ACT.Exp, bias=sink_prompt[:, h:h + 1], scale=1.0)
                ins.then_inc(s_exp, 1)

            def turned_p(p):
                for s in range(2):
                    act.wait_ge(s_T, 2 * p + s + 1)
                    if p:
                        act.wait_ge(s_O, 2 * p + s - 1)
                    nc.scalar.activation(probsT_p[:, s, :], bank[s][:, 0:384], ACT.Copy).then_inc(s_Tev, 1)

            split_q(0)
            split_q(1)
            for it in range(HEADS + 1):
                if it + 2 < HEADS:
                    split_q(it + 2)
                if it < HEADS:
                    exp_p(it)
                if it >= 1:
                    turned_p(it - 1)
            for n in range(REQ):
                b = 16 + 8 * (n % 2)
                act.wait_ge(s_smax, 2 * n + 1)
                nc.scalar.activation(s_a, s_a, ACT.Exp, bias=stat[:, b:b + 1], scale=1.0, accum_out=stat[:, b + 2:b + 3]).then_inc(s_sexp, 1)
                act.wait_ge(s_smax, 2 * n + 2)
                nc.scalar.activation(s_b, s_b, ACT.Exp, bias=stat[:, b + 1:b + 2], scale=1.0, accum_out=stat[:, b + 3:b + 4])
                nc.scalar.activation(stat[:, b + 4:b + 5], stat[:, b + 1:b + 2], ACT.Exp, bias=sink_sample, scale=1.0).then_inc(s_sexp, 1)
                act.wait_ge(s_sT, 3 * n + 1)
                nc.scalar.activation(pT_a[0:NEWK, 0:P], bank[2][0:NEWK, 0:P], ACT.Copy)
                nc.scalar.activation(pT_a[:, P:384], bank[2][:, P:384], ACT.Copy).then_inc(s_sTev, 1)
                act.wait_ge(s_sT, 3 * n + 2)
                nc.scalar.activation(pT_a[:, 384:896], bank[3][:, 0:512], ACT.Copy).then_inc(s_sTev, 1)
                act.wait_ge(s_sT, 3 * n + 3)
                nc.scalar.activation(pT_b[:, 0:P], bank[7][:, 256:384], ACT.Copy)
                nc.scalar.activation(pT_b[0:NEWK, P:2 * P], bank[7][0:NEWK, 384:512], ACT.Copy).then_inc(s_sTev, 1)
            act.wait_ge(s_attout, 6 * 16)
            act.wait_ge(s_sPev, 4 * REQ)
            squares("group", OT, NT)
            roots("group", NT, 2)
            squares_of_stream("cross", T_IN)
            roots("cross", NT)
            def exp_c(u):
                act.wait_ge(s_cmax, u + 1)
                if u >= 2:
                    act.wait_ge(s_cT, u - 1)
                nb = u % 2
                nc.scalar.activation(probs_c[:, nb, :], bank[3 + nb][:, 0:256], ACT.Exp, bias=stat[:, 64 + nb:65 + nb], scale=MEM_SCALE, accum_out=stat[:, 66 + nb:67 + nb]).then_inc(s_cexp, 1)

            def turned_c(u):
                act.wait_ge(s_cT, u + 1)
                if u >= 4:
                    act.wait_ge(s_cO, u - 3)
                dst = probsT_r if u < 2 else probsT_c
                nc.scalar.activation(dst[:, u % 2, :], bank[5][:, 0:256], ACT.Copy).then_inc(s_cTev, 1)

            for it in range(11):
                if it < 10:
                    exp_c(it)
                if it >= 1:
                    turned_c(it - 1)
            squares_of_stream("ffn", T_IN + KT + 4)
            roots("ffn", NT)
            def gate_exp(t):
                act.wait_ge(s_gx, FIRST_OF[t + 1])
                nc.scalar.activation(gexp[t], gexp[t], ACT.Exp).then_inc(s_gxe, 1)

            def h_rms(t):
                m = P if t < 2 else NS_TOK
                act.wait_ge(s_xt, t + 1)
                if t:
                    act.wait_ge(s_h, 80)
                link(nc.scalar.activation(h_tok[t][0:m, :], big[0:m, :], ACT.Square, accum_out=stat[0:m, 30 + t:31 + t]))
                nc.scalar.activation(stat[0:m, 33 + t:34 + t], stat[0:m, 30 + t:31 + t], ACT.Sqrt, bias=eps[0:m, :], scale=1.0 / D).then_inc(s_xrms, 1)

            h_rms(0)
            for f in range(KT):
                act.wait_ge(s_used, W_PQ + f + 1)
                nc.scalar.activation(qp[:, f, 0:NT], bank[f % 2][:, 0:NT], ACT.Copy)
                nc.scalar.activation(qp[:, f, NT:384], bank[f % 2][:, NP_TOK:NT], ACT.Copy).then_inc(s_ev, 1)
                if f < 2:
                    h_rms(f + 1)

            def gelu(t):
                n = SLOTS if t < 2 else SLOTS // 2
                act.wait_ge(s_udot, min((t + 1) * SLOTS, 2 * SLOTS + SLOTS // 2))
                nc.scalar.activation(dots[:, t, 0:n], dots[:, t, 0:n], ACT.Gelu).then_inc(s_gelu, 1)

            def diagonals(t):
                src, w = (ident, P) if t < 2 else (pair_sel, 64)
                act.wait_ge(s_coef, t + 1)
                for lo, hi, per in ((0, SHARED_FROM[t], RING), (SHARED_FROM[t], ROWS[t], RING - 1)):
                    if lo == hi:
                        continue
                    at = rows_added(t, lo, False)
                    with act.Fori(0, (hi - lo) // RING) as i:
                        for r in range(per):
                            act.wait_ge(s_vmm, i * per + (RING + at + r + 1 - per))
                            nc.scalar.activation(diag[r][:, 0:w], src, ACT.Copy, scale=dots[:, t, bass.ds(i * RING + (lo + r), 1)]).then_inc(s_dg, 1)

            def finish(t):
                m = P if t < 2 else NS_TOK
                if t:
                    act.wait_ge(s_vall, t)
                else:
                    act.wait_ge(s_vmm, RING + SLOTS)
                link(nc.scalar.activation(h_tok[t][0:m, :], y_acc[t][0:m, :], ACT.Square, accum_out=stat[0:m, 40 + t:41 + t]))
                nc.scalar.activation(stat[0:m, 43 + t:44 + t], stat[0:m, 40 + t:41 + t], ACT.Sqrt, bias=eps[0:m, :], scale=1.0 / D).then_inc(s_frms, 1)

            gate_exp(0)
            gelu(0)
            diagonals(0)
            gate_exp(1)
            gelu(1)
            gate_exp(2)
            finish(0)
            diagonals(1)
            gelu(2)
            finish(1)
            diagonals(2)
            finish(2)

        @block.vector
        def _(dve):
            ndv = [0]

            def link(ins):
                ndv[0] += 1
                ins.then_inc(s_dv, 1)
                dve.wait_ge(s_dv, ndv[0])

            def add_square(u, k, width, per=KT):
                a, q = acc[k // per], sq[:, (k % 4) * NT:(k % 4) * NT + width]
                dve.wait_ge(s_sq, 16 * u + k + 1)
                if k % per == 0:
                    nc.vector.tensor_copy(a[:, 0:width], q).then_inc(s_sqadd, 1)
                else:
                    dve.wait_ge(s_sqadd, 16 * u + k)
                    nc.vector.tensor_tensor(a[:, 0:width], a[:, 0:width], q, ALU.add).then_inc(s_sqadd, 1)

            def norm(which, x, gain, out, width, groups=1, added=False):
                base = N_SUM[which]
                u = N_NORM[which]
                if not added:
                    for k in range(KT):
                        add_square(u, k, width, KT // groups)
                per = KT // groups
                for g in range(groups):
                    dve.wait_ge(s_rms, base + g + 1)
                    nc.vector.reciprocal(rs[:, 0:width], rms[:, 0:width]).then_inc(s_rs, 1)
                    dve.wait_ge(s_rs, base + g + 1)
                    for k in range(g * per, (g + 1) * per):
                        nc.vector.scalar_tensor_tensor(out=out[:, k * width:(k + 1) * width], in0=x[:, k * width:(k + 1) * width],
                                                       scalar=gain[:, k:k + 1], in1=rs[:, 0:width], op0=ALU.mult, op1=ALU.mult).then_inc(s_h, 1)
                    dve.wait_ge(s_h, 16 * u + (g + 1) * per)

            dve.wait_ge(s_const, 16)
            norm("mem", mem_x, G_MEM, mem_x, MEM)
            norm("mix", XT, G_MIX, HT, NT)
            dve.wait_ge(s_used, W_IN)
            with dve.Fori(0, 8) as i:
                for r in range(4):
                    dve.wait_ge(s_used, i * 4 + (W_IN + r + 1))
                    nc.vector.tensor_scalar(QK[:, bass.ds(i * (4 * NT) + r * NT, NT)], bank[r % 2][:, 0:NT], 1.0, None, ALU.mult).then_inc(s_ev, 1)
            for f in (T_IN - 2, T_IN - 1):
                dve.wait_ge(s_used, W_IN + f + 1)
                nc.vector.tensor_scalar(QK[:, f * NT:(f + 1) * NT], bank[f % 2][:, 0:NT], 1.0, None, ALU.mult).then_inc(s_ev, 1)
            dve.wait_ge(s_ev, T_IN)
            for n in range(16):
                dve.wait_ge(s_bias, n + 1)
                nc.vector.tensor_copy(bias_p[:, :, n * 16:(n + 1) * 16], bank[6 + n % 2].rearrange("p (c h) -> p h c", h=32)).then_inc(s_biasev, 1)
            dve.wait_ge(s_bias, 17)
            nc.vector.tensor_copy(bias_sa[:, 0:512], bank[6]).then_inc(s_biasev, 1)
            dve.wait_ge(s_bias, 18)
            nc.vector.tensor_copy(bias_sa[:, 512:USED + WIN], bank[7][:, 0:USED + WIN - 512]).then_inc(s_biasev, 1)
            dve.wait_ge(s_bias, 19)
            nc.vector.tensor_copy(bias_sb, bank[6][:, 0:P + WIN]).then_inc(s_biasev, 1)
            dve.wait_ge(s_vtev, 9)
            nc.vector.memset(q_apart, 0.0).then_inc(s_qz, 1)
            nc.vector.memset(VT[NS_TOK:P, 2, :], 0.0).then_inc(s_padz, 1)
            for j in range(8):
                nc.vector.tensor_copy(kr[j][:, 0:NEWK], QK[:, (T_KA + j) * NT + NP_TOK:(T_KA + j + 1) * NT]).then_inc(s_newk, 1)
            dve.wait_ge(s_biasev, 19)
            t_max = stat[:, 56:60]
            minus_sink = stat[:, 32:48]

            def mark(ins):
                ndv[0] += 1
                ins.then_inc(s_dv, 1)
                return ndv[0]

            def by_block(a):
                return a.rearrange("p (s q) -> p s q", s=2)

            def step_p(p):
                now, last = p < HEADS, p >= 1
                pb, b = probs_p[:, p % 2], 16 * (p % 2)
                pl, bl = probs_p[:, (p + 1) % 2], 16 * ((p + 1) % 2)
                if now:
                    h = 16 * (p // 8) + p % 8
                    if p >= 2:
                        dve.wait_ge(s_T, 2 * p - 2)
                    dve.wait_ge(s_S, p + 1)
                    sc_p = big[:, (p % 2) * 1024:(p % 2 + 1) * 1024].rearrange("p (s c) -> p s c", s=2)
                    m1 = mark(nc.vector.scalar_tensor_tensor(out=pb[:, :, 0:256], in0=sc_p[:, :, 0:256], scalar=SCALE, in1=bias_p[:, h:h + 9:8, :], op0=ALU.mult, op1=ALU.add))
                    m2 = mark(nc.vector.scalar_tensor_tensor(out=pb[:, :, 256:384], in0=sc_p[:, :, 256:384], scalar=SCALE, in1=bias_p[:, h:h + 9:8, 128:256], op0=ALU.mult, op1=ALU.add))
                if last:
                    dve.wait_ge(s_exp, p)
                    den, rd = stat[:, bl + 4:bl + 8], stat[:, bl + 12:bl + 16]
                    if p - 1 >= 8:
                        ma = mark(nc.vector.tensor_tensor(den, den, stat[:, bl + 8:bl + 12], ALU.add))
                if now:
                    dve.wait_ge(s_dv, m1)
                    m3 = mark(nc.vector.tensor_reduce(by_block(t_max)[:, :, 0], pb[:, :, 0:256], AX_X, ALU.max))
                if last:
                    if p - 1 >= 8:
                        dve.wait_ge(s_dv, ma)
                    mr = mark(nc.vector.reciprocal(rd, den))
                if now:
                    dve.wait_ge(s_dv, m2)
                    m4 = mark(nc.vector.tensor_reduce(by_block(t_max)[:, :, 1], pb[:, :, 256:384], AX_X, ALU.max))
                if last:
                    dve.wait_ge(s_dv, mr)
                    nc.vector.tensor_scalar(pl[:, 0, 0:256], pl[:, 0, 0:256], rd[:, 0:1], None, ALU.mult)
                    nc.vector.tensor_scalar(pl[:, 0, 256:384], pl[:, 0, 256:384], rd[:, 1:2], None, ALU.mult).then_inc(s_nrm, 1)
                if now:
                    dve.wait_ge(s_dv, m4)
                    mx = stat[:, b:b + 4]
                    if p >= 8:
                        sink = minus_sink[:, p % 8:p % 8 + 9:8].unsqueeze(2).broadcast_to([P, 2, 2])
                        nc.vector.scalar_tensor_tensor(out=by_block(mx), in0=by_block(t_max), scalar=-1.0, in1=sink, op0=ALU.mult, op1=ALU.min).then_inc(s_max, 1)
                    else:
                        nc.vector.tensor_scalar(mx, t_max, -1.0, None, ALU.mult).then_inc(s_max, 1)
                if last:
                    nc.vector.tensor_scalar(pl[:, 1, 0:256], pl[:, 1, 0:256], rd[:, 2:3], None, ALU.mult)
                    nc.vector.tensor_scalar(pl[:, 1, 256:384], pl[:, 1, 256:384], rd[:, 3:4], None, ALU.mult).then_inc(s_nrm, 1)

            def out_p(p):
                for s in range(2):
                    dve.wait_ge(s_O, 2 * p + s + 1)
                    nc.vector.tensor_copy(OT[64 * s:64 * s + 64, p * NT:p * NT + NP_TOK], bank[2 + s][0:64, 0:256]).then_inc(s_Oev, 1)

            link(nc.vector.tensor_scalar(minus_sink, sink_prompt, -1.0, None, ALU.mult))
            for it in range(HEADS + 2):
                if it <= HEADS:
                    step_p(it)
                if it >= 2:
                    out_p(it - 2)
            def pads(n):
                if n == 0:
                    dve.wait_ge(s_zero, 4)
                if n >= 2:
                    dve.wait_ge(s_sS, n - 1)
                t0 = NP_TOK + QPR * n
                src_a = QK[:, T_QA * NT:T_KA * NT].rearrange("p (j t) -> p j t", t=NT)
                src_b = QK[:, T_QB * NT:T_KB * NT].rearrange("p (j t) -> p j t", t=NT)
                for s in range(2):
                    rows = slice(64 * s, 64 * s + 64)
                    pa = qpad_a[n % 2][rows, :].rearrange("p (j c) -> p j c", c=136)[:, :, 64 * s:64 * s + QPR]
                    nc.vector.tensor_copy(pa, src_a[rows, :, t0:t0 + QPR]).then_inc(s_qpad, 1)
                    pb = qpad_b[n % 2][rows, 64 * s:64 * s + 64].rearrange("p (j q) -> p j q", q=QPR)
                    nc.vector.tensor_copy(pb, src_b[rows, :, t0:t0 + QPR]).then_inc(s_qpad, 1)

            def softmax_s(n):
                w0, b = (REQ - 1 - n) * QPR, 16 + 8 * (n % 2)
                dve.wait_ge(s_krused, 8 * n + 8)
                if n:
                    dve.wait_ge(s_sT, 3 * n - 1)
                nc.vector.scalar_tensor_tensor(out=s_a[:, 0:NEWK], in0=bank[0][:, 0:NEWK], scalar=SCALE, in1=bias_sa[:, USED + w0:USED + w0 + NEWK], op0=ALU.mult, op1=ALU.add)
                nc.vector.scalar_tensor_tensor(out=s_a[:, NEWK:320], in0=bank[0][:, NEWK:320], scalar=SCALE, in1=bias_sa[:, 0:FIRST], op0=ALU.mult, op1=ALU.add)
                link(nc.vector.scalar_tensor_tensor(out=s_a[:, 320:SW], in0=bank[1], scalar=SCALE, in1=bias_sa[:, FIRST:USED], op0=ALU.mult, op1=ALU.add))
                link(nc.vector.tensor_reduce(stat[:, 52:53], s_a, AX_X, ALU.max))
                nc.vector.tensor_scalar(stat[:, b:b + 1], stat[:, 52:53], -1.0, None, ALU.mult).then_inc(s_smax, 1)
                dve.wait_ge(s_sS, n + 1)
                if n:
                    dve.wait_ge(s_sT, 3 * n)
                nc.vector.scalar_tensor_tensor(out=s_b[:, 0:P], in0=bank[6][:, 0:P], scalar=SCALE, in1=bias_sb[:, 0:P], op0=ALU.mult, op1=ALU.add)
                link(nc.vector.scalar_tensor_tensor(out=s_b[:, P:P + NEWK], in0=bank[6][:, P:P + NEWK], scalar=SCALE, in1=bias_sb[:, P + w0:P + w0 + NEWK], op0=ALU.mult, op1=ALU.add))
                link(nc.vector.tensor_reduce(stat[:, 53:54], s_b, AX_X, ALU.max))
                nc.vector.tensor_scalar(stat[:, b + 1:b + 2], stat[:, 53:54], sink_sample, -1.0, ALU.max, ALU.mult).then_inc(s_smax, 1)

            def pair_s(n):
                b = 16 + 8 * (n % 2)
                dve.wait_ge(s_sexp, 2 * n + 2)
                link(nc.vector.tensor_tensor(stat[:, b + 3:b + 4], stat[:, b + 3:b + 4], stat[:, b + 4:b + 5], ALU.add))
                link(nc.vector.reciprocal(stat[:, b + 5:b + 7], stat[:, b + 2:b + 4]))
                dve.wait_ge(s_vrused, 6 * n + 6)
                for s in range(2):
                    rows = slice(64 * s, 64 * s + 64)
                    ins = nc.vector.scalar_tensor_tensor(out=o_masked[rows, :], in0=bank[4 + s][rows, :], scalar=stat[rows, b + 5:b + 6], in1=head_mask[rows, :], op0=ALU.mult, op1=ALU.mult)
                link(ins)
                if n:
                    dve.wait_ge(s_sP, n)
                nc.vector.tensor_reduce(o_pair[:, 0:64], o_masked.rearrange("p (h e) -> p e h", h=8), AX_X, ALU.add)
                dve.wait_ge(s_sO, n + 1)
                for s in range(2):
                    rows = slice(64 * s, 64 * s + 64)
                    ins = nc.vector.tensor_scalar(o_pair[rows, 64:128], bank[7][rows, 64 * s:64 * s + 64], stat[rows, b + 6:b + 7], None, ALU.mult)
                ins.then_inc(s_sOev, 1)

            def keep_s(n):
                dve.wait_ge(s_sP, n + 1)
                t0 = NP_TOK + QPR * n
                for m in range(2):
                    for s in range(2):
                        dst = OT[64 * s:64 * s + 64, m * 8 * NT:(m + 1) * 8 * NT].rearrange("p (j t) -> p j t", t=NT)[:, :, t0:t0 + QPR]
                        src = bank[7][64 * m:64 * m + 64, 128 + 64 * s:192 + 64 * s].rearrange("p (j q) -> p j q", q=QPR)
                        nc.vector.tensor_copy(dst, src).then_inc(s_sPev, 1)

            pads(0)
            pads(1)
            dve.wait_ge(s_mask, 16)
            dve.wait_ge(s_Oev, 2 * HEADS)
            nc.vector.memset(pT_a[NS_TOK:P, 0:P], 0.0).then_inc(s_padz, 1)
            nc.vector.memset(pT_b[NS_TOK:P, P:2 * P], 0.0).then_inc(s_padz, 1)
            softmax_s(0)
            for n in range(REQ):
                if n + 2 < REQ:
                    pads(n + 2)
                if n:
                    keep_s(n - 1)
                if n + 1 < REQ:
                    softmax_s(n + 1)
                pair_s(n)
            keep_s(REQ - 1)
            dve.wait_ge(s_sPev, 4 * REQ)
            norm("group", OT, G_AB, OT, NT, 2)

            def add_to_stream(at, u):
                for k in range(4):
                    dve.wait_ge(s_used, W_IN + at + k + 1)
                    x = XT[:, k * NT:(k + 1) * NT]
                    nc.vector.tensor_tensor(x, x, bank[k % 2][:, 0:NT], ALU.add).then_inc(s_ev, 1)
                    add_square(u, k, NT)
                with dve.Fori(1, 4) as i:
                    for r in range(4):
                        dve.wait_ge(s_used, i * 4 + (W_IN + at + r + 1))
                        x = XT[:, bass.ds(i * (4 * NT) + r * NT, NT)]
                        nc.vector.tensor_tensor(x, x, bank[r % 2][:, 0:NT], ALU.add).then_inc(s_ev, 1)
                        dve.wait_ge(s_sq, i * 4 + (16 * u + r + 1))
                        dve.wait_ge(s_sqadd, i * 4 + (16 * u + r))
                        nc.vector.tensor_tensor(acc[0], acc[0], sq[:, r * NT:(r + 1) * NT], ALU.add).then_inc(s_sqadd, 1)
                dve.wait_ge(s_ev, at + KT)

            add_to_stream(T_IN, N_NORM["cross"])
            norm("cross", XT, G_CROSS, HT, NT, added=True)
            for f in range(4):
                dve.wait_ge(s_used, W_CQ + f + 1)
                nc.vector.tensor_copy(qc[:, f, :], bank[f % 2][:, 0:NT]).then_inc(s_ev, 1)
            link(nc.vector.memset(qpad_c, 0.0))
            dve.wait_ge(s_ev, T_IN + KT + 4)

            def pads_c(g):
                if g:
                    dve.wait_ge(s_cS, 1)
                for h in range(4):
                    dst = qpad_c.rearrange("p (n h c) -> p n h c", n=4, h=4)[:, :, h, 0:QPR]
                    src = qc[:, h, NP_TOK + 32 * g:NP_TOK + 32 * g + 32].rearrange("p (n q) -> p n q", q=QPR)
                    nc.vector.tensor_copy(dst, src).then_inc(s_cpad, 1)

            def max_c(u):
                nb = u % 2
                dve.wait_ge(s_cS, u + 1)
                if u:
                    dve.wait_ge(s_cmax, u)
                link(nc.vector.tensor_reduce(stat[:, 56:57], bank[3 + nb][:, 0:256], AX_X, ALU.max))
                nc.vector.tensor_scalar(stat[:, 64 + nb:65 + nb], stat[:, 56:57], -MEM_SCALE, None, ALU.mult).then_inc(s_cmax, 1)

            def norm_c(u):
                nb = u % 2
                dve.wait_ge(s_cexp, u + 1)
                link(nc.vector.reciprocal(stat[:, 68 + nb:69 + nb], stat[:, 66 + nb:67 + nb]))
                nc.vector.tensor_scalar(probs_c[:, nb, :], probs_c[:, nb, :], stat[:, 68 + nb:69 + nb], None, ALU.mult).then_inc(s_cnrm, 1)

            def out_c(u):
                if u >= 2:
                    h, q = (u - 2) % 4, (u - 2) // 4
                    dve.wait_ge(s_cO, u - 1)
                    nc.vector.tensor_copy(oc[:, h, q * P:(q + 1) * P], bank[6 + u % 2][:, 0:128]).then_inc(s_cOev, 1)
                else:
                    dve.wait_ge(s_cOr, u + 1)
                    for h in range(4):
                        src = bank[u][:, 0:128].rearrange("p (n h q) -> p n h q", n=4, h=4)[:, :, h, :]
                        dst = oc[:, h, NP_TOK + 32 * u:NP_TOK + 32 * u + 32].rearrange("p (n q) -> p n q", q=QPR)
                        ins = nc.vector.tensor_copy(dst, src)
                    ins.then_inc(s_cOev, 1)

            pads_c(0)
            pads_c(1)
            for it in range(12):
                if 1 <= it <= 10:
                    norm_c(it - 1)
                if it < 10:
                    max_c(it)
                if it >= 4:
                    out_c(it - 2)
            out_c(0)
            out_c(1)
            add_to_stream(T_IN + KT + 4, N_NORM["ffn"])
            norm("ffn", XT, G_FFN, HT, NT, added=True)
            def token_major():
                dve.wait_ge(s_grow, 16)
                for t in range(3):
                    m = P if t < 2 else NS_TOK
                    dve.wait_ge(s_xrms, t + 1)
                    link(nc.vector.reciprocal(stat[0:m, 36 + t:37 + t], stat[0:m, 33 + t:34 + t]))
                    nc.vector.scalar_tensor_tensor(out=h_tok[t][0:m, :], in0=big[0:m, :], scalar=stat[0:m, 36 + t:37 + t], in1=g_row[0:m, :], op0=ALU.mult, op1=ALU.mult).then_inc(s_ht, 1)

            def top_k(src, values, indices, n):
                for half in range(2):
                    o = slice(8 * half, 8 * half + 8)
                    for x in range(n):
                        ins = nc.vector.max(values(x)[:, o], src(x))
                    link(ins)
                    for x in range(n):
                        ins = nc.vector.max_index(indices(x)[:, o], values(x)[:, o], src(x))
                    link(ins)
                    if half == 0:
                        for x in range(n):
                            ins = nc.vector.match_replace(src(x), values(x)[:, o], src(x), -3e38)
                        link(ins)

            pos_flat = pos.rearrange("p h k -> p (h k)")

            def keep_scores(c):
                t, h, n = GROUPS[c]
                dve.wait_ge(s_sc, c + 1)
                nc.vector.tensor_copy(sc[:, h * 256:(h + n) * 256], bank[h // 2 if t else 2 + c % 2][:, 0:256 * n]).then_inc(s_scev, 1)

            def sub_keys_of(c):
                t, h, n = GROUPS[c]
                dve.wait_ge(s_scev, c + 1)
                top_k(lambda x: sc[:, (2 * h + x) * P:(2 * h + x + 1) * P], lambda x: top_v[:, h + x // 2, x % 2, :], lambda x: top_i[:, h + x // 2, x % 2, :], 2 * n)

            def sums_of(c):
                t, h, n = GROUPS[c]
                hs, mine = slice(h, h + n), slice(h * 256, (h + n) * 256)
                nc.vector.tensor_copy(top_f[:, hs], top_i[:, hs])
                cand = sc[:, mine].rearrange("p (h i j) -> p h i j", h=n, i=PK)
                link(nc.vector.tensor_tensor(cand, top_v[:, hs, 0, :].unsqueeze(3).broadcast_to([P, n, PK, PK]), top_v[:, hs, 1, :].unsqueeze(2).broadcast_to([P, n, PK, PK]), ALU.add))
                top_k(lambda x: sc[:, (h + x) * 256:(h + x + 1) * 256], lambda x: best[:, h + x, :], lambda x: pos[:, h + x, :], n)
                nc.vector.tensor_tensor(gexp[t][:, hs], best[:, hs], best[:, hs, 0:1].broadcast_to([P, n, PK]), ALU.subtract).then_inc(s_gx, 1)
                e = slice(h * PK, (h + n) * PK)
                at = [slice(z * SLOTS + h * PK, z * SLOTS + (h + n) * PK) for z in range(2)]
                nc.vector.tensor_scalar(pos_i[:, at[0]], pos_flat[:, e], 4, None, ALU.logical_shift_right)
                link(nc.vector.tensor_scalar(pos_i[:, at[1]], pos_flat[:, e], 15, None, ALU.bitwise_and))
                for z in range(2):
                    ins = nc.vector.tensor_copy(pos_f[:, at[z]], pos_i[:, at[z]])
                link(ins)

            def experts_of(c):
                t, h, n = GROUPS[c]
                hs, mine = slice(h, h + n), slice(h * 256, (h + n) * 256)
                e = slice(h * PK, (h + n) * PK)
                at = [slice(z * SLOTS + h * PK, z * SLOTS + (h + n) * PK) for z in range(2)]
                oh = sc[:, mine].rearrange("p (s i) -> p s i", i=PK)
                oh4 = sc[:, mine].rearrange("p (h k i) -> p h k i", h=n, k=PK)
                for z in range(2):
                    link(nc.vector.tensor_tensor(oh, pos_f[:, at[z]].unsqueeze(2).broadcast_to([P, n * PK, PK]), iota16.unsqueeze(1).broadcast_to([P, n * PK, PK]), ALU.is_equal))
                    link(nc.vector.tensor_tensor(oh4, oh4, top_f[:, hs, z, :].unsqueeze(2).broadcast_to([P, n, PK, PK]), ALU.mult))
                    link(nc.vector.tensor_reduce(exp_f[:, at[z]], oh, AX_X, ALU.add))
                link(nc.vector.scalar_tensor_tensor(out=eidx_f[:, e], in0=exp_f[:, at[0]], scalar=float(NKEY), in1=exp_f[:, at[1]], op0=ALU.mult, op1=ALU.add))
                if c < len(GROUPS) - 1:
                    nc.vector.tensor_copy(eidx[:, t, e], eidx_f[:, e]).then_inc(s_idx, 1)
                else:
                    link(nc.vector.tensor_copy(eidx[:, t, e], eidx_f[:, e]))
                    for s in range(2):
                        rows = slice(64 * s, 64 * s + 64)
                        ins = nc.vector.tensor_copy(pair_idx[rows, :], eidx[rows, 2, 64 * s:64 * s + 64])
                    ins.then_inc(s_idx, 1)

            def weigh(t):
                dve.wait_ge(s_gxe, t + 1)
                link(nc.vector.tensor_reduce(stat[:, 60:68], gexp[t], AX_X, ALU.add))
                link(nc.vector.reciprocal(stat[:, 68:76], stat[:, 60:68]))
                link(nc.vector.tensor_tensor(gate[:, t, :].rearrange("p (h k) -> p h k", h=PH), gexp[t], stat[:, 68:76].unsqueeze(2).broadcast_to([P, PH, PK]), ALU.mult))
                if t == 2:
                    for s in range(2):
                        rows = slice(64 * s, 64 * s + 64)
                        link(nc.vector.tensor_copy(pair_gate[rows, :], gate[rows, 2, 64 * s:64 * s + 64]))

            def u_dots(t, lo, hi):
                if t == 2:
                    dve.wait_ge(s_dup, 16)
                with dve.Fori(0, (hi - lo) // RING) as i:
                    for r in range(RING):
                        dve.wait_ge(s_ug[r], i * 16 + 16 * ((t * SLOTS + lo) // RING + 1))
                        nc.vector.scalar_tensor_tensor(out=u_ring[r], in0=u_ring[r], scalar=1.0, in1=h_tok[t], op0=ALU.mult, op1=ALU.mult,
                                                       accum_out=dots[:, t, bass.ds(i * RING + (lo + r), 1)]).then_inc(s_udot, 1)

            def coefs(t):
                n = SLOTS if t < 2 else SLOTS // 2
                dve.wait_ge(s_gelu, t + 1)
                g = gate[:, t, :] if t < 2 else pair_gate
                nc.vector.tensor_tensor(dots[:, t, 0:n], dots[:, t, 0:n], g, ALU.mult).then_inc(s_coef, 1)

            def v_share(t):
                for s in range(SHARED_FROM[t] + RING - 1, ROWS[t], RING):
                    n = rows_added(t, s, True)
                    dve.wait_ge(s_vg[RING - 1], 16 * ((t * SLOTS + s) // RING + 1))
                    if s < SHARED_FROM[t] + RING:
                        if t == 1:
                            dve.wait_ge(s_coef, 2)
                        nc.vector.tensor_scalar(h_tok[t], v_ring[RING - 1], dots[:, t, s:s + 1], None, ALU.mult).then_inc(s_vsum, 1)
                    else:
                        dve.wait_ge(s_vsum, n)
                        nc.vector.scalar_tensor_tensor(out=h_tok[t], in0=v_ring[RING - 1], scalar=dots[:, t, s:s + 1], in1=h_tok[t], op0=ALU.mult, op1=ALU.add).then_inc(s_vsum, 1)

            def finish(t):
                m = P if t < 2 else NS_TOK
                dve.wait_ge(s_frms, t + 1)
                link(nc.vector.reciprocal(stat[0:m, 46 + t:47 + t], stat[0:m, 43 + t:44 + t]))
                nc.vector.scalar_tensor_tensor(out=h_tok[t][0:m, :], in0=y_acc[t][0:m, :], scalar=stat[0:m, 46 + t:47 + t], in1=g_row[0:m, :], op0=ALU.mult, op1=ALU.mult).then_inc(s_y, 1)

            token_major()
            keep_scores(0)
            sub_keys_of(0)
            sums_of(0)
            experts_of(0)
            dve.wait_ge(s_ht, 3)
            def choose_part(c, part):
                if part == 0 and c < FIRST_OF[1]:
                    keep_scores(c)
                if part == 0 and c == FIRST_OF[1]:
                    for k in range(FIRST_OF[1], FIRST_OF[2]):
                        keep_scores(k)
                (sub_keys_of, sums_of, experts_of)[part](c)
                if part == 2 and GROUPS[c][0] == 1:
                    keep_scores(c + FIRST_OF[2] - FIRST_OF[1])

            for n in range(SLOTS // 8):
                u_dots(0, 8 * n, 8 * n + 8)
                if n == 0:
                    for part in range(3):
                        choose_part(1, part)
                elif n == 1:
                    choose_part(2, 0)
                    choose_part(2, 1)
                elif n < 12:
                    choose_part(2 + n // 3, n % 3)
            weigh(0)
            coefs(0)
            for n in range(SLOTS // 8):
                u_dots(1, 8 * n, 8 * n + 8)
                for m in ((12 + n,) if n < 9 else (3 + 2 * n, 4 + 2 * n)):
                    if 2 + m // 3 < len(GROUPS):
                        choose_part(2 + m // 3, m % 3)
            weigh(1)
            dve.wait_ge(s_grow, 32)
            coefs(1)
            finish(0)
            u_dots(2, 0, SLOTS // 2)
            weigh(2)
            v_share(1)
            coefs(2)
            finish(1)
            dve.wait_ge(s_coef, 3)
            v_share(2)
            finish(2)

        @block.tensor
        def _(pe):
            def mm(out, lhsT, rhs, start=True, stop=True):
                return nc.tensor.matmul(out, lhsT, rhs, start=start, stop=stop, skip_group_check=True)

            def norm(which, width, groups=1):
                before = N_SUM[which]
                for g in range(groups):
                    if before and g == 0:
                        pe.wait_ge(s_rms, before)
                    pe.wait_ge(s_sqadd, 16 * N_NORM[which] + (g + 1) * KT // groups)
                    mm(bank[2 + g][:, 0:width], ones, acc[g][:, 0:width]).then_inc(s_ss, 1)

            pe.wait_ge(s_const, 16)
            norm("mem", MEM)
            for c in range(4):
                if c == 2:
                    norm("mix", NT)
                chunk_wait(pe, c)
                if c >= 2:
                    pe.wait_ge(s_memev, c - 1)
                w = WR[:, c * D:(c + 1) * D]
                for k in range(KT):
                    if c == 0:
                        pe.wait_ge(s_h, k + 1)
                    ins = mm(bank[c % 2][:, 0:MEM], w[:, k * P:(k + 1) * P], mem_x[:, k * MEM:(k + 1) * MEM], start=(k == 0), stop=(k == KT - 1))
                ins.then_inc(s_used, 1)
            for c in range(4, 8):
                chunk_wait(pe, c)
                w = WR[:, (c - 4) * D:(c - 3) * D]
                for t in range(2):
                    for q in range(4):
                        k = 4 * (c - 4) + q
                        ins = mm(bank[4 + t], mem_x[:, k * MEM + t * P:k * MEM + (t + 1) * P], w[:, q * 512:(q + 1) * 512], start=(k == 0), stop=(k == KT - 1))
                ins.then_inc(s_used, 1)

            def project(slot, x, b, normed=None):
                for k in range(KT):
                    if normed is not None:
                        pe.wait_ge(s_h, normed + k + 1)
                    ins = mm(bank[b][:, 0:NT], WR[:, slot * D + k * P:slot * D + (k + 1) * P], x[:, k * NT:(k + 1) * NT], start=(k == 0), stop=(k == KT - 1))
                return ins

            def tile(slot, x, b, arrived, free, normed=None):
                pe.wait_ge(s_w[slot], arrived)
                if free is not None:
                    pe.wait_ge(s_ev, free)
                project(slot, x, b, normed).then_inc(s_used, 1)

            pe.wait_ge(s_memev, 4)
            for f in range(4):
                tile(f, HT, f % 2, 16 * 3, f - 1 if f >= 2 else None, None if f else 16)
            with pe.Fori(1, 8) as i:
                for r in range(4):
                    tile(r, HT, r % 2, i * 16 + 48, i * 4 + (r - 1))
            for f in (32, 33):
                tile(f % 4, HT, f % 2, 16 * ((f + 8) // 4 + 1), f - 1)

            pe.wait_ge(s_ev, T_IN)
            pe.wait_ge(s_memev, 6)
            for n in range(9):
                t, q = n // 3, n % 3
                m = P if t < 2 else NS_TOK
                if n >= 2:
                    pe.wait_ge(s_vtev, n - 1)
                nf = 4 if q < 2 else 1
                for f in range(nf):
                    src = QK[:, (T_VA + 4 * q + f) * NT + t * P:(T_VA + 4 * q + f) * NT + t * P + m]
                    ins = nc.tensor.transpose(bank[3 + n % 2][0:m, f * P:(f + 1) * P], src, ident)
                ins.then_inc(s_vt, 1)
            pe.wait_ge(s_tab, 16)
            for n in range(16):
                if n >= 2:
                    pe.wait_ge(s_biasev, n - 1)
                for q in range(4):
                    c0 = 16 * n + 4 * q
                    ins = mm(bank[6 + n % 2][:, q * 128:(q + 1) * 128], oh_p[:, 252 - c0:380 - c0], rb_p)
                ins.then_inc(s_bias, 1)
            for n, (g, a, b) in enumerate(((0, 0, 512), (0, 512, USED + WIN), (1, 0, P + WIN))):
                pe.wait_ge(s_biasev, 15 + n)
                oh = oh_sb if g else oh_sa
                for t in range(2):
                    ins = mm(bank[6 + n % 2][:, 0:b - a], rb_s[:, g, t, :], oh[:, t, a:b], start=(t == 0), stop=(t == 1))
                ins.then_inc(s_bias, 1)
            pe.wait_ge(s_biasev, 19)
            pe.wait_ge(s_vtev, 9)

            def scores_p(p):
                pe.wait_ge(s_qapart, p + 1)
                if p >= 2:
                    pe.wait_ge(s_max, p - 1)
                kt = QK[:, (T_KB if p >= 8 else T_KA + p) * NT:][:, 0:NT]
                for s in range(2):
                    o = bank[4 + 2 * (p % 2) + s]
                    mm(o[:, 0:256], q_apart[:, s, 128:256], kt[:, 0:256])
                    ins = mm(o[:, 256:384], q_apart[:, s, 0:128], kt[:, 0:128])
                ins.then_inc(s_S, 1)

            def turn_p(p):
                for s in range(2):
                    pe.wait_ge(s_nrm, 2 * p + s + 1)
                    if p:
                        pe.wait_ge(s_Tev, 2 * p + s - 1)
                    for b in range(3):
                        ins = nc.tensor.transpose(bank[s][:, b * P:(b + 1) * P], probs_p[:, p % 2, s, b * P:(b + 1) * P], ident)
                    ins.then_inc(s_T, 1)

            def values_p(p):
                for s in range(2):
                    pe.wait_ge(s_Tev, 2 * p + s + 1)
                    if p:
                        pe.wait_ge(s_Oev, 2 * p + s - 1)
                    c = (p + 8 * s) * DH if p < 8 else 1024 + 64 * s
                    o = bank[2 + s]
                    pT = probsT_p[:, s, :]
                    mm(o[0:64, 128:256], VT[:, 0, c:c + DH], pT[:, 0:128], start=True, stop=False)
                    mm(o[0:64, 128:256], VT[:, 1, c:c + DH], pT[:, 128:256], start=False, stop=True)
                    mm(o[0:64, 0:128], VT[:, 0, c:c + DH], pT[:, 256:384]).then_inc(s_O, 1)

            scores_p(0)
            for it in range(HEADS + 2):
                if it + 1 < HEADS:
                    scores_p(it + 1)
                if it >= 2:
                    values_p(it - 2)
                if 1 <= it <= HEADS:
                    turn_p(it - 1)
            pe.wait_ge(s_newk, 8)
            pe.wait_ge(s_kb, 16)
            pe.wait_ge(s_vb, 16)
            pe.wait_ge(s_Oev, 2 * HEADS)

            def scores_s(n):
                if n:
                    pe.wait_ge(s_smax, 2 * n)
                pe.wait_ge(s_qpad, 4 * n + 4)
                for j in range(8):
                    pe.wait_ge(s_kr[j], 16 * (n + 1))
                    w = qpad_a[n % 2][:, j * P:(j + 1) * P]
                    mm(bank[0][:, 0:320], w, kr[j][:, 0:320], start=(j == 0), stop=(j == 7))
                    mm(bank[1], w, kr[j][:, 320:SW], start=(j == 0), stop=(j == 7)).then_inc(s_krused, 1)
                mm(bank[6][:, 0:P], qpad_b[n % 2], kbT[:, n, :])
                mm(bank[6][:, P:P + NEWK], qpad_b[n % 2], QK[:, T_KB * NT + NP_TOK:T_VA * NT]).then_inc(s_sS, 1)

            def turn_s(n):
                pe.wait_ge(s_sexp, 2 * n + 1)
                for b, (a, w) in enumerate(((0, 64), (64, 128), (192, 128), (320, 128), (448, 128), (576, 128), (704, 128))):
                    t, o = (2, b * P) if b < 3 else (3, (b - 3) * P)
                    ins = nc.tensor.transpose(bank[t][0:w, o:o + P], s_a[:, a:a + w], ident)
                    if b in (2, 6):
                        ins.then_inc(s_sT, 1)
                pe.wait_ge(s_sexp, 2 * n + 2)
                if n:
                    pe.wait_ge(s_sPev, 4 * n)
                nc.tensor.transpose(bank[7][:, 256:384], s_b[:, 0:P], ident)
                nc.tensor.transpose(bank[7][0:NEWK, 384:512], s_b[:, P:P + NEWK], ident).then_inc(s_sT, 1)

            def values_s(n):
                pe.wait_ge(s_sTev, 3 * n + 2)
                if n:
                    pe.wait_ge(s_sOev, n)
                else:
                    pe.wait_ge(s_padz, 3)
                for b in range(7):
                    if b:
                        pe.wait_ge(s_vr[b - 1], 16 * (n + 1))
                    for q in range(2):
                        v = VT[:, 2, q * 512:(q + 1) * 512] if b == 0 else vr[b - 1][:, q * 512:(q + 1) * 512]
                        ins = mm(bank[4 + q], pT_a[:, b * P:(b + 1) * P], v, start=(b == 0), stop=(b == 6))
                    if b:
                        ins.then_inc(s_vrused, 1)
                pe.wait_ge(s_sTev, 3 * n + 3)
                mm(bank[7][:, 0:P], pT_b[:, 0:P], vb[:, n, :], start=True, stop=False)
                mm(bank[7][:, 0:P], pT_b[:, P:2 * P], VT[:, 2, 1024:VW], start=False, stop=True).then_inc(s_sO, 1)

            def pair_s(n):
                pe.wait_ge(s_sOev, n + 1)
                if n:
                    pe.wait_ge(s_sPev, 4 * n)
                nc.tensor.transpose(bank[7][:, 128:256], o_pair, ident).then_inc(s_sP, 1)

            scores_s(0)
            for n in range(REQ):
                if n + 1 < REQ:
                    scores_s(n + 1)
                if n:
                    pair_s(n - 1)
                turn_s(n)
                values_s(n)
            pair_s(REQ - 1)
            norm("group", NT, 2)

            def stream_tiles(x, at, c_at, normed):
                for r in range(4):
                    tile((c_at + r) % 4, x, r % 2, 16 * ((c_at + r) // 4 + 1), at + r - 1, None if r else normed)
                with pe.Fori(1, 4) as i:
                    for r in range(4):
                        tile((c_at + r) % 4, x, r % 2, i * 16 + 16 * ((c_at + r) // 4 + 1), i * 4 + (at + r - 1))

            stream_tiles(OT, T_IN, C_OUT, 32)
            at = T_IN + KT
            norm("cross", NT)
            for f in range(4):
                c = C_CQ + f
                tile(c % 4, HT, f % 2, 16 * (c // 4 + 1), at + f - 1, None if f else 48)
            at += 4
            pe.wait_ge(s_ev, at)

            def scores_c(u):
                if u >= 2:
                    pe.wait_ge(s_cexp, u - 1)
                o = bank[3 + u % 2][:, 0:256]
                if u >= 2:
                    h, q = (u - 2) % 4, (u - 2) // 4
                    mm(o, qc[:, h, q * P:(q + 1) * P], km_p[:, h * MEM:(h + 1) * MEM]).then_inc(s_cS, 1)
                else:
                    pe.wait_ge(s_km[u], 32 if u else 64)
                    pe.wait_ge(s_cpad, 4 * u + 4)
                    for m in range(16):
                        ins = mm(o, qpad_c[:, m * P:(m + 1) * P], km[u][:, m * MEM:(m + 1) * MEM], start=(m == 0), stop=(m == 15))
                    ins.then_inc(s_cS, 1)

            def turn_c(u):
                pe.wait_ge(s_cnrm, u + 1)
                if u:
                    pe.wait_ge(s_cTev, u)
                for b in range(2):
                    ins = nc.tensor.transpose(bank[5][:, b * P:(b + 1) * P], probs_c[:, u % 2, b * P:(b + 1) * P], ident)
                ins.then_inc(s_cT, 1)

            def values_c(u):
                pe.wait_ge(s_cTev, u + 1)
                if u >= 4:
                    pe.wait_ge(s_cOev, u - 3)
                h, o, pT = (u - 2) % 4, bank[6 + u % 2], probsT_c[:, u % 2, :]
                for b in range(2):
                    ins = mm(o[:, 0:P], vm_p[:, b * 512 + h * P:b * 512 + (h + 1) * P], pT[:, b * P:(b + 1) * P], start=(b == 0), stop=(b == 1))
                ins.then_inc(s_cO, 1)

            def values_r(u, n):
                pe.wait_ge(s_cTev, u + 1)
                for h in range(4):
                    m = 4 * n + h
                    for b in range(2):
                        ins = mm(bank[u][:, m * 8:m * 8 + 8], vm[u][:, n * 1024 + b * 512 + h * P:][:, 0:P], probsT_r[:, u, b * P + m * 8:b * P + m * 8 + 8], start=(b == 0), stop=(b == 1))
                if n == 3:
                    ins.then_inc(s_cOr, 1)

            for it in range(12):
                if it < 10:
                    scores_c(it)
                if 2 <= it < 10:
                    values_r((it - 2) // 4, (it - 2) % 4)
                if it >= 4:
                    values_c(it - 2)
                if 1 <= it <= 10:
                    turn_c(it - 1)
            pe.wait_ge(s_cOev, 10)
            for f in range(KT):
                c = C_CO + f // 4
                chunk_wait(pe, c)
                if f >= 2:
                    pe.wait_ge(s_ev, at + f - 1)
                for k in range(4):
                    w = WR[:, (c % 4) * D + (f % 4) * 512 + k * P:][:, 0:P]
                    ins = mm(bank[f % 2][:, 0:NT], w, oc[:, k, :], start=(k == 0), stop=(k == 3))
                ins.then_inc(s_used, 1)
            at += KT
            norm("ffn", NT)

            def turn_stream(t):
                m = P if t < 2 else NS_TOK
                if t:
                    pe.wait_ge(s_ht, t)
                for k in range(KT):
                    ins = nc.tensor.transpose(big[0:m, k * P:(k + 1) * P], XT[:, k * NT + t * P:k * NT + t * P + m], ident)
                ins.then_inc(s_xt, 1)

            def key_scores(c):
                t, h, n = GROUPS[c]
                if t == 0:
                    pe.wait_ge(s_ev, at + 2 * (h + n))
                    if c >= 2:
                        pe.wait_ge(s_scev, c - 1)
                else:
                    pe.wait_ge(s_scev, FIRST_OF[1] if t == 1 else FIRST_OF[1] + h // 2 + 1)
                for x in range(2 * n):
                    o = bank[h // 2 if t else 2 + c % 2][:, x * P:(x + 1) * P]
                    ins = mm(o, qp[:, 2 * h + x, t * P:(t + 1) * P], sub_keys[:, (x % 2) * NKEY:(x % 2 + 1) * NKEY])
                ins.then_inc(s_sc, 1)

            turn_stream(0)
            for f in range(KT):
                c = C_PQ + f
                tile(c % WR_N, HT, f % 2, 16 * (c // WR_N + 1), at + f - 1, None if f else 64)
                if f < 2:
                    turn_stream(f + 1)
                for c, (t, h, n) in enumerate(GROUPS):
                    if t == 0 and f == 2 * (h + n):
                        key_scores(c)
            for c in range(FIRST_OF[1] - 1, len(GROUPS)):
                key_scores(c)
            at += KT
            pe.sem_inc(s_vmm, RING)
            for t in range(3):
                m = P if t < 2 else NS_TOK
                if t == 0:
                    pe.wait_ge(s_ht, 3)
                elif t == 1:
                    pe.wait_ge(s_scev, len(GROUPS))
                else:
                    pe.wait_ge(s_y, 1)
                acc_t = y_acc[t][0:m, :]
                for k in range(KT):
                    ins = mm(acc_t[:, k * P:(k + 1) * P], XT[:, k * NT + t * P:k * NT + t * P + m], ident, start=(k % 4 == 0), stop=False)
                for lo, hi, per in ((0, SHARED_FROM[t], RING), (SHARED_FROM[t], ROWS[t], RING - 1)):
                    if lo == hi:
                        continue
                    at = rows_added(t, lo, False)
                    with pe.Fori(0, (hi - lo) // RING) as i:
                        for r in range(per):
                            pe.wait_ge(s_vg[r], i * 16 + 16 * ((t * SLOTS + lo) // RING + 1))
                            pe.wait_ge(s_dg, i * per + (at + r + 1))
                            for q in range(4):
                                ins = mm(acc_t[:, q * 512:(q + 1) * 512], diag[r][:, 0:m], v_ring[r][:, q * 512:(q + 1) * 512], start=False, stop=False)
                            ins.then_inc(s_vmm, 1)
                if t:
                    pe.wait_ge(s_vsum, rows_added(t, ROWS[t], True))
                    for q in range(4):
                        ins = mm(acc_t[:, q * 512:(q + 1) * 512], (ident if t < 2 else pair_sel), h_tok[t][:, q * 512:(q + 1) * 512], start=False, stop=True)
                    ins.then_inc(s_vall, 1)


def bucket(dist):
    dist = np.maximum(np.asarray(dist), 0)
    ratio = np.log(np.maximum(dist, 1) / 16) / math.log(2048 / 16)
    large = np.minimum(16 + (ratio * 16).astype(np.int32), 31)
    return np.where(dist < 16, dist, large).astype(np.int32)


def one_hot(dist, mixer, masked=None):
    dist = np.asarray(dist)
    out = np.zeros((32,) + dist.shape, np.float32)
    b = bucket(dist)
    assert b.max() < 30
    np.put_along_axis(out, b[None], 1.0, axis=0)
    held_a = (dist <= 128).astype(int) + ((dist % 4 == 0) & (dist <= 512)) + (dist % 16 == 0)
    for row, held in ((30, held_a), (31, (dist <= 128).astype(int))):
        if mixer in (row, None):
            seen = (dist >= 0) & (held > 0)
            if masked is not None:
                seen &= ~masked
            out[row] = np.where(seen, np.log(np.maximum(held, 1)), NEG)
    return out


def kernel(**inputs):
    import concourse.bacc as bacc
    from concourse.bass_utils import run_bass_kernel_spmd

    x = {k: np.asarray(v) for k, v in inputs.items()}
    f32 = np.float32

    def tiles(a):
        return a.T.reshape(-1, P, a.shape[0]).transpose(1, 0, 2).reshape(P, -1)

    pair = np.arange(1024).reshape(2, 8, 64).transpose(1, 0, 2).ravel()
    at = np.arange(512).reshape(32, 2, 8)
    key_order = np.concatenate([at[:, 1].ravel(), at[:, 0].ravel(), np.arange(512, PAST)])

    def chunks(w):
        return w.reshape(-1, P, w.shape[1] // P, P).transpose(2, 1, 0, 3).reshape(w.shape[1] // P, P, -1)

    w_in = x["w_in"][0]
    a = 1024
    w_in = np.concatenate([w_in[:, :a][:, pair], w_in[:, a:2 * a][:, pair], w_in[:, 3 * a:4 * a][:, pair],
                           w_in[:, 4 * a:4 * a + P], w_in[:, 2 * a:3 * a], w_in[:, 4 * a + P:]], axis=1)
    rows = np.concatenate([pair, a + pair])
    w_ckv = x["w_ckv"][0]
    wall = np.concatenate([
        chunks(w_ckv[:, :512]),
        w_ckv[:, 512:].reshape(4, 4, P, 512).transpose(0, 2, 1, 3).reshape(4, P, D),
        chunks(w_in), chunks(x["w_out"][0][rows]), chunks(x["w_cq"][0]),
        chunks(x["w_co"][0]).reshape(4, 4, P, 512).transpose(0, 2, 1, 3).reshape(4, P, D),
        chunks(x["w_pq"][0])])

    def gain(g):
        return g.reshape(KT, P).T

    gains = [gain(x["ln_mix"][0]), gain(x["ln_mem"][0]), gain(x["ln_cross"][0]), gain(x["ln_ffn"][0]),
             gain(np.concatenate([x["ln_a_out"][0], x["ln_b_out"][0]])[rows])]
    sinks = x["b_sinks"][0]
    consts = np.concatenate([
        np.eye(P, dtype=f32), np.ones((P, P), f32), *gains, np.broadcast_to(sinks, (P, HEADS)),
        np.repeat(sinks, QPR)[:, None], np.broadcast_to(np.arange(PK, dtype=f32), (P, PK)),
        (np.arange(P)[:, None] % 64 == np.arange(64)).astype(f32), x["sub_keys_1"][0].T, x["sub_keys_2"][0].T], axis=1)

    rel = x["rel_bias"]
    rb = np.zeros((4, 32, 4, 32), f32)
    for g in range(4):
        rb[g, :30, g] = rel[:30]
        rb[g, 30, g, :16] = 1
        rb[g, 31, g, 16:] = 1
    j = np.arange(380)
    oh_p = np.stack([one_hot(j - 124 - g, None) for g in range(4)])
    rb_s = np.zeros((4, 32, 2, 2, HEADS, QPR), f32)
    oh_sa, oh_sb = np.zeros((4, 32, 2, USED + WIN), f32), np.zeros((4, 32, 2, P + WIN), f32)
    new = np.arange(WIN) - 7 * QPR
    for t in range(2):
        for g in range(4):
            q = 4 * t + g
            rb_s[g, :30, :, t, :, q] = rel[:30].reshape(30, 2, HEADS)
            rb_s[g, 30, 0, t, :, q] = 1
            rb_s[g, 31, 1, t, :, q] = 1
            own = (new < 0) | (new >= QPR)
            oh_sa[g, :, t] = np.concatenate([one_hot(PAST + q - key_order[FIRST:], 30), one_hot(q - new, 30, own)], axis=1)
            oh_sb[g, :, t] = np.concatenate([one_hot(P + q - np.arange(P), 31), one_hot(q - new, 31, own)], axis=1)
    tables = np.concatenate([m.reshape(P, -1) for m in (rb, oh_p, rb_s, oh_sa, oh_sb)], axis=1)
    head_mask = (np.arange(P)[:, None] // QPR % 8 == np.arange(512) // 64).astype(f32)

    ka = x["cache_a_k"][0][:, key_order].reshape(REQ, PAST, 1024)[:, :, pair]
    ka = np.ascontiguousarray(ka.transpose(0, 2, 1)).reshape(REQ, 8, P, PAST)
    va = np.ascontiguousarray(x["cache_a_v"][0].reshape(REQ, PAST, 1024)[:, key_order])
    tokens = np.concatenate([x["x_prompt"][0], x["x_sample"].reshape(NS_TOK, D)])
    arrays = {
        "xT": tiles(tokens), "memT": tiles(x["mem_prompt"][0]), "consts": consts, "tables": tables,
        "head_mask": head_mask, "wall": wall, "ffn_row": x["ln_ffn"][0], "fin_row": x["ln_final"],
        "kaT": ka, "va": va,
        "kbT": x["cache_b_k"][0].reshape(REQ, P, P).transpose(2, 0, 1).reshape(P, -1),
        "vb": x["cache_b_v"][0].reshape(REQ, P, P).transpose(1, 0, 2).reshape(P, -1),
        "kmT": x["cache_mem_k"][0].transpose(0, 3, 2, 1).reshape(REQ, P, 1024),
        "vm": x["cache_mem_v"][0].reshape(REQ, 2, P, 512).transpose(0, 2, 1, 3).reshape(REQ, P, 1024),
        "expert_u": x["expert_u"][0], "expert_v": x["expert_v"][0],
    }
    arrays = {k: np.ascontiguousarray(v) for k, v in arrays.items()}
    outs = {
        "y": (NT, D), "ka_out": (32, 256, 1024), "va_out": (32, 256, 1024), "kaT_new": (P, 8 * NT), "kbT_new": (P, NT),
        "v_new": (P, 2 * VW), "v_new_s": (NS_TOK, VW), "kb_out": (P, REQ * P), "vb_out": (P, REQ * P),
        "mk_out": (P, 1024), "mv_out": (P, 1024),
    }
    nc = bacc.Bacc("TRN2", target_bir_lowering=False, num_devices=1)
    d = {k: nc.dram_tensor(k, v.shape, mybir.dt.from_np(v.dtype), kind="ExternalInput").ap() for k, v in arrays.items()}
    d |= {k: nc.dram_tensor(k, s, F32, kind="ExternalOutput").ap() for k, s in outs.items()}
    d["ka_flat"] = d["kaT"].rearrange("n j p u -> (n j p) u").rearrange("(c r) u -> c r u", c=32)
    d["va_flat"] = d["va"].rearrange("n t w -> (n t) w").rearrange("(c r) u -> c r u", c=32)
    build(nc, d)
    o = run_bass_kernel_spmd(nc, [arrays], core_ids=[0]).results[0]

    unpair = np.argsort(pair)
    y = o["y"]
    k_new = o["kaT_new"].reshape(P, 8, NT).transpose(2, 1, 0).reshape(NT, 1024)[:, unpair].reshape(NT, HEADS, DH)
    kb_new = o["kbT_new"].T.reshape(NT, 2, DH)
    v_new = np.concatenate([o["v_new"].reshape(P, 2, VW).transpose(1, 0, 2).reshape(NP_TOK, VW), o["v_new_s"]])
    va_new, vb_new = v_new[:, :1024].reshape(NT, HEADS, DH), v_new[:, 1024:].reshape(NT, 2, DH)
    back = np.argsort(key_order)
    ka_old = o["ka_out"].reshape(REQ, 1024, PAST).transpose(0, 2, 1)[:, back][:, :, unpair].reshape(REQ, PAST, HEADS, DH)
    va_old = o["va_out"].reshape(REQ, PAST, HEADS, DH)[:, back]
    kb_old = o["kb_out"].reshape(P, REQ, P).transpose(1, 2, 0).reshape(REQ, P, 2, DH)
    vb_old = o["vb_out"].reshape(P, REQ, P).transpose(1, 0, 2).reshape(REQ, P, 2, DH)

    def sampled(old, new, drop):
        return np.concatenate([old[:, drop:], new[NP_TOK:].reshape(REQ, QPR, *new.shape[1:])], axis=1)[None]

    mk = o["mk_out"].reshape(P, MEM_HEADS, MEM).transpose(2, 1, 0)[None, None]
    mv = o["mv_out"].reshape(P, 2, MEM_HEADS, MEM_DH).transpose(1, 0, 2, 3).reshape(MEM, MEM_HEADS, MEM_DH)[None, None]
    return tuple(np.ascontiguousarray(r) for r in (
        y[None, :NP_TOK], y[NP_TOK:].reshape(REQ, QPR, D),
        k_new[None, None, :NP_TOK], va_new[None, None, :NP_TOK], kb_new[None, None, NP_TOK - P:NP_TOK], vb_new[None, None, NP_TOK - P:NP_TOK],
        mk, mv,
        sampled(ka_old, k_new, 0), sampled(va_old, va_new, 0), sampled(kb_old, kb_new, QPR), sampled(vb_old, vb_new, QPR)))
```
